# Optimizing a Trainium2 kernel written in Bass

```python
import math
import jax, jax.numpy as jnp
from jax import lax
import numpy as np

D_MODEL = 1024
BATCH = 1
SEQ = 512
DEPTH = 1

MEM_LEN = 256
EPS = 1e-6

ATT_HEAD_DIM = 64
ATT_WIDTH = D_MODEL // 2
ATT_HEADS = ATT_WIDTH // ATT_HEAD_DIM
DILATED_CONFIGS = ((128, 1), (512, 4), (2048, 16))
ATT_BLOCK = 128
ROPE_THETA = 500000.0
ROPE_DIM = ATT_HEAD_DIM // 4

M_WIDTH = D_MODEL - ATT_WIDTH
M_HEADS = 4
M_HEAD_DIM = M_WIDTH // M_HEADS
CONV_WIDTH = 4
M_CHUNK = 128

IN_WIDTH = 3 * ATT_WIDTH + 3 * M_WIDTH + 2 * M_HEADS
MIX_WIDTH = ATT_WIDTH + M_WIDTH

X_HEADS = 4
X_HEAD_DIM = 64
X_WIDTH = X_HEADS * X_HEAD_DIM

N_GROUPS = 4
EXPERTS_PER_GROUP = 4
N_EXPERTS = N_GROUPS * EXPERTS_PER_GROUP
TOP_K = 2
EXPERT_FF = 512
MOE_BLOCK = 128


def rms_norm(x, g):
    xf = x.astype(jnp.float32)
    y = xf * lax.rsqrt(jnp.mean(xf * xf, axis=-1, keepdims=True) + EPS)
    return (y * g.astype(jnp.float32)).astype(x.dtype)

def partial_rotary(t, positions):
    half = ROPE_DIM // 2
    inv_freq = ROPE_THETA ** (-jnp.arange(0, ROPE_DIM, 2, dtype=jnp.float32) / ROPE_DIM)
    ang = positions.astype(jnp.float32)[..., None] * inv_freq
    cos = jnp.cos(ang)[:, :, None, :]
    sin = jnp.sin(ang)[:, :, None, :]
    tr = t[..., :ROPE_DIM].astype(jnp.float32)
    t1, t2 = tr[..., :half], tr[..., half:]
    rot = jnp.concatenate([t1 * cos - t2 * sin, t2 * cos + t1 * sin], axis=-1)
    return jnp.concatenate([rot.astype(t.dtype), t[..., ROPE_DIM:]], axis=-1)

def causal_window_attention(q, k, v, window, blk):
    N, L, H, Dh = q.shape
    assert window <= blk
    nb = -(-L // blk)
    Lp = nb * blk
    pad = ((0, 0), (0, Lp - L), (0, 0), (0, 0))
    qb, kb, vb = (jnp.pad(t, pad).reshape(N, nb, blk, H, Dh) for t in (q, k, v))

    def with_prev(t):
        prev = jnp.pad(t, ((0, 0), (1, 0), (0, 0), (0, 0), (0, 0)))[:, :-1]
        return jnp.concatenate([prev, t], axis=2)

    kk, vv = with_prev(kb), with_prev(vb)
    s = jnp.einsum('nbqhd,nbkhd->nbhqk', qb, kk).astype(jnp.float32) * (Dh ** -0.5)
    qi = jnp.arange(blk)[:, None] + blk
    ki = jnp.arange(2 * blk)[None, :]
    dist = qi - ki
    band = (dist >= 0) & (dist <= window)
    valid_key = (jnp.arange(nb)[:, None, None] * blk + ki[None] - blk) >= 0
    mask = band[None] & valid_key
    s = jnp.where(mask[None, :, None, :, :], s, -jnp.inf)
    lse = jax.nn.logsumexp(s, axis=-1)
    p = jnp.exp(s - lse[..., None])
    o = jnp.einsum('nbhqk,nbkhd->nbqhd', p.astype(v.dtype), vv).astype(jnp.float32)
    o = o.reshape(N, Lp, H, Dh)[:, :L]
    lse = lse.transpose(0, 1, 3, 2).reshape(N, Lp, H)[:, :L]
    return o, lse

def dilated_attention(q, k, v):
    B, S, H, Dh = q.shape
    outs, lses = [], []
    for window, d in DILATED_CONFIGS:
        L = S // d

        def to_sub(t):
            return t.reshape(B, L, d, H, Dh).transpose(0, 2, 1, 3, 4).reshape(B * d, L, H, Dh)

        o, lse = causal_window_attention(to_sub(q), to_sub(k), to_sub(v), window // d, ATT_BLOCK)
        outs.append(o.reshape(B, d, L, H, Dh).transpose(0, 2, 1, 3, 4).reshape(B, S, H, Dh))
        lses.append(lse.reshape(B, d, L, H).transpose(0, 2, 1, 3).reshape(B, S, H))
    w = jax.nn.softmax(jnp.stack(lses, axis=0), axis=0)
    return jnp.einsum('cbsh,cbshd->bshd', w, jnp.stack(outs, axis=0))

def mlstm_chunkwise(q, k, v, i_pre, f_pre):
    B, H, S, Dh = q.shape
    L = M_CHUNK
    nc = S // L
    q, k, v = (t.reshape(B, H, nc, L, Dh) for t in (q, k, v))
    ig = i_pre.reshape(B, H, nc, L)
    lf = jax.nn.log_sigmoid(f_pre).reshape(B, H, nc, L)
    b = jnp.cumsum(lf, axis=-1)
    b_last = b[..., -1]

    g = b_last[..., None] - b + ig
    m_loc = jnp.max(g, axis=-1)
    wk = jnp.exp(g - m_loc[..., None])
    C_loc = jnp.einsum('bhcl,bhcld,bhcle->bhcde', wk, k, v)
    n_loc = jnp.einsum('bhcl,bhcld->bhcd', wk, k)

    def step(carry, inp):
        C, n, m = carry
        Cl, nl, ml, bl = inp
        m_new = jnp.maximum(bl + m, ml)
        a = jnp.exp(bl + m - m_new)
        c = jnp.exp(ml - m_new)
        C_new = a[..., None, None] * C + c[..., None, None] * Cl
        n_new = a[..., None] * n + c[..., None] * nl
        return (C_new, n_new, m_new), (C, n, m)

    init = (jnp.zeros((B, H, Dh, Dh), jnp.float32), jnp.zeros((B, H, Dh), jnp.float32),
            jnp.zeros((B, H), jnp.float32))
    xs = (jnp.moveaxis(C_loc, 2, 0), jnp.moveaxis(n_loc, 2, 0),
          jnp.moveaxis(m_loc, 2, 0), jnp.moveaxis(b_last, 2, 0))
    _, (C_prev, n_prev, m_prev) = lax.scan(step, init, xs)
    C_prev = jnp.moveaxis(C_prev, 0, 2)
    n_prev = jnp.moveaxis(n_prev, 0, 2)
    m_prev = jnp.moveaxis(m_prev, 0, 2)

    causal = jnp.tril(jnp.ones((L, L), dtype=bool))
    Dlog = b[..., :, None] - b[..., None, :] + ig[..., None, :]
    Dlog = jnp.where(causal, Dlog, -jnp.inf)
    m_intra = jnp.max(Dlog, axis=-1)
    m_inter = b + m_prev[..., None]
    m_t = jnp.maximum(m_inter, m_intra)
    Dw = jnp.exp(Dlog - m_t[..., None])
    inter_w = jnp.exp(m_inter - m_t)
    s = jnp.einsum('bhcld,bhcsd->bhcls', q, k) * Dw
    num = jnp.einsum('bhcls,bhcse->bhcle', s, v) + \
        inter_w[..., None] * jnp.einsum('bhcld,bhcde->bhcle', q, C_prev)
    den = jnp.sum(s, axis=-1) + inter_w * jnp.einsum('bhcld,bhcd->bhcl', q, n_prev)
    h = num / jnp.maximum(jnp.abs(den), jnp.exp(-m_t))[..., None]
    return h.reshape(B, H, S, Dh)

def hybrid_mixer(h, positions, w_in, conv_w, conv_b, w_q_m, w_k_m, b_i, b_f, g_mhn, skip_m, w_out):
    B, S, _ = h.shape
    sizes = [ATT_WIDTH] * 3 + [M_WIDTH] * 3 + [M_HEADS, M_HEADS]
    splits = [int(c) for c in np.cumsum(sizes)[:-1]]
    z = h @ w_in
    aq, ak, av, mu, mv, mo, mi, mf = jnp.split(z, splits, axis=-1)

    aq = partial_rotary(aq.reshape(B, S, ATT_HEADS, ATT_HEAD_DIM), positions)
    ak = partial_rotary(ak.reshape(B, S, ATT_HEADS, ATT_HEAD_DIM), positions)
    av = av.reshape(B, S, ATT_HEADS, ATT_HEAD_DIM)
    y_att = dilated_attention(aq, ak, av).reshape(B, S, ATT_WIDTH).astype(h.dtype)

    f32 = jnp.float32
    mu_pad = jnp.pad(mu.astype(f32), ((0, 0), (CONV_WIDTH - 1, 0), (0, 0)))
    c = sum(mu_pad[:, j:j + S] * conv_w[j].astype(f32) for j in range(CONV_WIDTH)) + conv_b.astype(f32)
    c = jax.nn.silu(c)
    ch = c.reshape(B, S, M_HEADS, M_HEAD_DIM)
    mq = jnp.einsum('bshd,hde->bhse', ch, w_q_m.astype(f32))
    mk = jnp.einsum('bshd,hde->bhse', ch, w_k_m.astype(f32)) * (M_HEAD_DIM ** -0.5)
    mvh = mv.astype(f32).reshape(B, S, M_HEADS, M_HEAD_DIM).transpose(0, 2, 1, 3)
    ig = (mi.astype(f32) + b_i.astype(f32)).transpose(0, 2, 1)
    fg = (mf.astype(f32) + b_f.astype(f32)).transpose(0, 2, 1)
    hc = mlstm_chunkwise(mq, mk, mvh, ig, fg).transpose(0, 2, 1, 3)
    hn = hc * lax.rsqrt(jnp.mean(hc * hc, axis=-1, keepdims=True) + EPS)
    hn = hn.reshape(B, S, M_WIDTH) * g_mhn.astype(f32)
    y_m = jax.nn.sigmoid(mo.astype(f32)) * (hn + skip_m.astype(f32) * c)

    y = jnp.concatenate([y_att, y_m.astype(h.dtype)], axis=-1)
    return y @ w_out

def memory_cross_attention(h, mem_n, w_q, w_kv, w_o):
    B, S, _ = h.shape
    M = mem_n.shape[1]
    q = (h @ w_q).reshape(B, S, X_HEADS, X_HEAD_DIM)
    kv = (mem_n @ w_kv).reshape(B, M, 2, X_HEADS, X_HEAD_DIM)
    k, v = kv[:, :, 0], kv[:, :, 1]
    s = jnp.einsum('bshd,bmhd->bhsm', q, k).astype(jnp.float32) * (X_HEAD_DIM ** -0.5)
    p = jax.nn.softmax(s, axis=-1).astype(v.dtype)
    o = jnp.einsum('bhsm,bmhd->bshd', p, v).reshape(B, S, X_WIDTH)
    return o @ w_o

def hierarchical_moe(h, w_rg, b_rg, w_re, b_re, w1, w3, w2):
    N, D = h.shape
    f32 = jnp.float32
    glog = (h @ w_rg).astype(f32) + b_rg.astype(f32)
    gprob = jax.nn.softmax(glog, axis=-1)
    g_idx = jnp.argmax(glog, axis=-1)
    g_w = jnp.take_along_axis(gprob, g_idx[:, None], axis=-1)[:, 0]
    elog = ((h @ w_re).astype(f32) + b_re.astype(f32)).reshape(N, N_GROUPS, EXPERTS_PER_GROUP)
    elog = jnp.take_along_axis(elog, g_idx[:, None, None], axis=1)[:, 0]
    top_v, top_i = lax.top_k(elog, TOP_K)
    e_w = jax.nn.softmax(top_v, axis=-1) * g_w[:, None]
    e_id = g_idx[:, None] * EXPERTS_PER_GROUP + top_i

    A = N * TOP_K
    flat_e = e_id.reshape(A)
    flat_tok = jnp.repeat(jnp.arange(N, dtype=jnp.int32), TOP_K)
    flat_w = e_w.reshape(A)
    order = jnp.argsort(flat_e)
    se, stok, sw = flat_e[order], flat_tok[order], flat_w[order]
    counts = jnp.bincount(flat_e, length=N_EXPERTS)
    starts = jnp.cumsum(counts) - counts
    padded = ((counts + MOE_BLOCK - 1) // MOE_BLOCK) * MOE_BLOCK
    pends = jnp.cumsum(padded)
    pstarts = pends - padded
    dest = pstarts[se] + (jnp.arange(A) - starts[se])
    P = (-(-A // MOE_BLOCK) + N_EXPERTS) * MOE_BLOCK
    nblk = P // MOE_BLOCK
    row_tok = jnp.full((P,), N, dtype=jnp.int32).at[dest].set(stok)
    row_w = jnp.zeros((P,), f32).at[dest].set(sw)
    blk_e = jnp.minimum(jnp.searchsorted(pends, jnp.arange(nblk) * MOE_BLOCK, side='right'),
                        N_EXPERTS - 1)
    h_pad = jnp.concatenate([h, jnp.zeros((1, D), h.dtype)], axis=0)
    xb = h_pad[row_tok].reshape(nblk, MOE_BLOCK, D)

    def expert_block(args):
        xblk, e = args
        return (jax.nn.silu(xblk @ w1[e]) * (xblk @ w3[e])) @ w2[e]

    yb = lax.map(expert_block, (xb, blk_e)).reshape(P, D)
    out = jnp.zeros((N + 1, D), f32).at[row_tok].add(yb.astype(f32) * row_w[:, None])
    return out[:N]

def first_inputs(seed: int = 0) -> dict:
    key = jax.random.key(seed)
    ks = jax.random.split(key, 32)
    f32 = jnp.float32
    L, D = DEPTH, D_MODEL

    def nrm(k, shape, scale):
        return jax.random.normal(k, shape, f32) * scale

    def gain(k, shape):
        return 1.0 + 0.02 * jax.random.normal(k, shape, f32)

    return {
        'x': nrm(ks[0], (BATCH, SEQ, D), 1.0),
        'mem': nrm(ks[1], (BATCH, MEM_LEN, D), 1.0),
        'positions': jnp.tile(jnp.arange(SEQ, dtype=jnp.int32)[None, :], (BATCH, 1)),
        'g_mix': gain(ks[2], (L, D)),
        'w_in': nrm(ks[3], (L, D, IN_WIDTH), D ** -0.5),
        'conv_w': nrm(ks[4], (L, CONV_WIDTH, M_WIDTH), CONV_WIDTH ** -0.5),
        'conv_b': nrm(ks[5], (L, M_WIDTH), 0.02),
        'w_q_m': nrm(ks[6], (L, M_HEADS, M_HEAD_DIM, M_HEAD_DIM), M_HEAD_DIM ** -0.5),
        'w_k_m': nrm(ks[7], (L, M_HEADS, M_HEAD_DIM, M_HEAD_DIM), M_HEAD_DIM ** -0.5),
        'b_i': nrm(ks[8], (L, M_HEADS), 0.1),
        'b_f': 3.0 + 3.0 * jax.random.uniform(ks[9], (L, M_HEADS), f32),
        'g_mhn': gain(ks[10], (L, M_WIDTH)),
        'skip_m': gain(ks[11], (L, M_WIDTH)),
        'w_out': nrm(ks[12], (L, MIX_WIDTH, D), MIX_WIDTH ** -0.5),
        'g_cross': gain(ks[13], (L, D)),
        'g_mem': gain(ks[14], (L, D)),
        'w_q_x': nrm(ks[15], (L, D, X_WIDTH), D ** -0.5),
        'w_kv_x': nrm(ks[16], (L, D, 2 * X_WIDTH), D ** -0.5),
        'w_o_x': nrm(ks[17], (L, X_WIDTH, D), X_WIDTH ** -0.5),
        'g_ffn': gain(ks[18], (L, D)),
        'w_router_g': nrm(ks[19], (L, D, N_GROUPS), D ** -0.5),
        'b_router_g': nrm(ks[20], (L, N_GROUPS), 0.01),
        'w_router_e': nrm(ks[21], (L, D, N_EXPERTS), D ** -0.5),
        'b_router_e': nrm(ks[22], (L, N_EXPERTS), 0.01),
        'w1': nrm(ks[23], (L, N_EXPERTS, D, EXPERT_FF), D ** -0.5),
        'w3': nrm(ks[24], (L, N_EXPERTS, D, EXPERT_FF), D ** -0.5),
        'w2': nrm(ks[25], (L, N_EXPERTS, EXPERT_FF, D), EXPERT_FF ** -0.5),
        'g_final': gain(ks[26], (D,)),
    }

def first_block(x, mem, positions, g_mix, w_in, conv_w, conv_b, w_q_m, w_k_m, b_i, b_f, g_mhn,
              skip_m, w_out, g_cross, g_mem, w_q_x, w_kv_x, w_o_x, g_ffn, w_router_g,
              b_router_g, w_router_e, b_router_e, w1, w3, w2, g_final):
    B, S, D = x.shape
    for l in range(DEPTH):
        h = rms_norm(x, g_mix[l])
        x = x + hybrid_mixer(h, positions, w_in[l], conv_w[l], conv_b[l], w_q_m[l], w_k_m[l],
                             b_i[l], b_f[l], g_mhn[l], skip_m[l], w_out[l]).astype(x.dtype)
        h = rms_norm(x, g_cross[l])
        x = x + memory_cross_attention(h, rms_norm(mem, g_mem[l]), w_q_x[l], w_kv_x[l],
                                       w_o_x[l]).astype(x.dtype)
        h = rms_norm(x, g_ffn[l]).reshape(B * S, D)
        x = x + hierarchical_moe(h, w_router_g[l], b_router_g[l], w_router_e[l], b_router_e[l],
                                 w1[l], w3[l], w2[l]).reshape(B, S, D).astype(x.dtype)
    return rms_norm(x, g_final)


DEPTH_2 = 2

GRID_W = 64
NA_HEADS = 8
NA_HEAD_DIM = 64
NA_WIDTH = NA_HEADS * NA_HEAD_DIM
NA_ROWS = 8
NA_COLS = 16
Q_BLOCK_COLS = 16
KEY_BAND_COLS = Q_BLOCK_COLS + NA_COLS
N_COL_BLOCKS = GRID_W // Q_BLOCK_COLS
F_GROUPS = 4
F_GROUP_DIM = 128
F_WIDTH = F_GROUPS * F_GROUP_DIM
IN_COLS = 3 * NA_WIDTH + F_WIDTH + 2 * D_MODEL
D_FF = 2816
RMS_EPS = 1e-6


def rms_norm_2(x, g):
    xf = x.astype(jnp.float32)
    y = xf * lax.rsqrt(jnp.mean(xf * xf, axis=-1, keepdims=True) + RMS_EPS)
    return (y * g.astype(jnp.float32)).astype(x.dtype)

def swiglu(x, w_in, w_out):
    gu = x @ w_in
    g, u = jnp.split(gu, 2, axis=-1)
    return (jax.nn.silu(g) * u) @ w_out

def neighbourhood_attention(q, k, v, rpb):
    B, T, H, Dh = q.shape
    rows = T // GRID_W
    kh = min(NA_ROWS, rows)
    r = jnp.arange(rows)
    row_start = jnp.clip(r - kh // 2, 0, rows - kh)
    row_idx = row_start[:, None] + jnp.arange(kh)
    j = jnp.arange(N_COL_BLOCKS)
    band_start = jnp.clip(j * Q_BLOCK_COLS - NA_COLS // 2, 0, GRID_W - KEY_BAND_COLS)
    key_col = band_start[:, None] + jnp.arange(KEY_BAND_COLS)
    q_col = j[:, None] * Q_BLOCK_COLS + jnp.arange(Q_BLOCK_COLS)
    win_start = jnp.clip(q_col - NA_COLS // 2, 0, GRID_W - NA_COLS)
    col_ok = (key_col[:, None, :] >= win_start[..., None]) & (
        key_col[:, None, :] < win_start[..., None] + NA_COLS)

    qg = q.reshape(B, rows, N_COL_BLOCKS, Q_BLOCK_COLS, H, Dh)
    kg = k.reshape(B, rows, GRID_W, H, Dh)
    vg = v.reshape(B, rows, GRID_W, H, Dh)
    gi_r = row_idx[:, None, :, None]
    gi_c = key_col[None, :, None, :]
    k_win = kg[:, gi_r, gi_c]
    v_win = vg[:, gi_r, gi_c]

    dr = row_idx - r[:, None] + (NA_ROWS - 1)
    dc = jnp.clip(key_col[:, None, :] - q_col[..., None], -(NA_COLS - 1), NA_COLS - 1) + (NA_COLS - 1)
    bias = rpb[:, dr[:, None, None, :, None], dc[None, :, :, None, :]]
    bias = jnp.transpose(bias, (1, 2, 0, 3, 4, 5)).astype(jnp.float32)

    scale = Dh ** -0.5
    s = jnp.einsum('brjqhd,brjuvhd->brjhquv', qg, k_win).astype(jnp.float32) * scale + bias[None]
    s = jnp.where(col_ok[None, None, :, None, :, None, :], s, -jnp.inf)
    sh = s.shape
    p = jax.nn.softmax(s.reshape(sh[:-2] + (kh * KEY_BAND_COLS,)), axis=-1).reshape(sh)
    o = jnp.einsum('brjhquv,brjuvhd->brjqhd', p.astype(v.dtype), v_win)
    return o.reshape(B, T, H * Dh)

def fourier_mix(u):
    B, T, _ = u.shape
    ug = u.astype(jnp.float32).reshape(B, T, F_GROUPS, F_GROUP_DIM)
    f = jnp.fft.fft2(ug, axes=(1, 3), norm="ortho").real
    return f.reshape(B, T, F_WIDTH).astype(u.dtype)

def mixer(h, w_in, gate_bias, rpb, w_na_out, w_f_out, w_o):
    B, T, _ = h.shape
    z = h @ w_in
    s1 = NA_WIDTH
    q = z[..., :s1]
    k = z[..., s1:2 * s1]
    v = z[..., 2 * s1:3 * s1]
    uf = z[..., 3 * s1:3 * s1 + F_WIDTH]
    ga = z[..., 3 * s1 + F_WIDTH:3 * s1 + F_WIDTH + D_MODEL]
    gf = z[..., 3 * s1 + F_WIDTH + D_MODEL:]
    shp = (B, T, NA_HEADS, NA_HEAD_DIM)
    y_na = neighbourhood_attention(q.reshape(shp), k.reshape(shp), v.reshape(shp), rpb) @ w_na_out
    y_f = fourier_mix(uf) @ w_f_out
    g_na = jax.nn.sigmoid(ga + gate_bias[0])
    g_f = jax.nn.sigmoid(gf + gate_bias[1])
    return (g_na * y_na + g_f * y_f) @ w_o

def second_inputs(seed: int = 0) -> dict:
    key = jax.random.key(seed)
    ks = jax.random.split(key, 20)
    L, D, F = DEPTH_2, D_MODEL, D_FF

    def w(k, shape, fan_in, mult=1.0):
        return jax.random.normal(k, shape, jnp.float32) * (mult * fan_in ** -0.5)

    def gain(k, shape):
        return 1.0 + 0.05 * jax.random.normal(k, shape, jnp.float32)

    return {
        "x": jax.random.normal(ks[0], (BATCH, SEQ, D), jnp.float32),
        "ffn1_norm": gain(ks[1], (L, D)),
        "ffn1_w_in": w(ks[2], (L, D, 2 * F), D),
        "ffn1_w_out": w(ks[3], (L, F, D), F),
        "mix_norm": gain(ks[4], (L, D)),
        "mix_w_in": w(ks[5], (L, D, IN_COLS), D),
        "mix_gate_bias": 0.1 * jax.random.normal(ks[6], (L, 2, D), jnp.float32),
        "na_rpb": 0.5 * jax.random.normal(ks[7], (L, NA_HEADS, 2 * NA_ROWS - 1, 2 * NA_COLS - 1), jnp.float32),
        "na_w_out": w(ks[8], (L, NA_WIDTH, D), NA_WIDTH),
        "f_w_out": w(ks[9], (L, F_WIDTH, D), F_WIDTH),
        "mix_w_o": w(ks[10], (L, D, D), D),
        "ffn2_norm": gain(ks[11], (L, D)),
        "ffn2_w_in": w(ks[12], (L, D, 2 * F), D),
        "ffn2_w_out": w(ks[13], (L, F, D), F),
        "final_norm": gain(ks[14], (D,)),
    }

def second_block(x, ffn1_norm, ffn1_w_in, ffn1_w_out, mix_norm, mix_w_in, mix_gate_bias,
              na_rpb, na_w_out, f_w_out, mix_w_o, ffn2_norm, ffn2_w_in, ffn2_w_out,
              final_norm):
    for l in range(DEPTH_2):
        x = x + 0.5 * swiglu(rms_norm_2(x, ffn1_norm[l]), ffn1_w_in[l], ffn1_w_out[l])
        x = x + mixer(rms_norm_2(x, mix_norm[l]), mix_w_in[l], mix_gate_bias[l], na_rpb[l],
                      na_w_out[l], f_w_out[l], mix_w_o[l])
        x = x + 0.5 * swiglu(rms_norm_2(x, ffn2_norm[l]), ffn2_w_in[l], ffn2_w_out[l])
    return rms_norm_2(x, final_norm)


def setup_inputs(seed=0):
    out = dict(first_inputs(seed))
    for name, value in second_inputs(seed + 1).items():
        if name != "x":
            out[name + "_2"] = value
    return out


def reference(
    x, mem, positions, g_mix, w_in, conv_w, conv_b, w_q_m, w_k_m, b_i, b_f, g_mhn, skip_m,
    w_out, g_cross, g_mem, w_q_x, w_kv_x, w_o_x, g_ffn, w_router_g, b_router_g, w_router_e,
    b_router_e, w1, w3, w2, g_final, ffn1_norm_2, ffn1_w_in_2, ffn1_w_out_2, mix_norm_2,
    mix_w_in_2, mix_gate_bias_2, na_rpb_2, na_w_out_2, f_w_out_2, mix_w_o_2, ffn2_norm_2,
    ffn2_w_in_2, ffn2_w_out_2, final_norm_2,
):
    x = first_block(
        x, mem, positions, g_mix, w_in, conv_w, conv_b, w_q_m, w_k_m, b_i, b_f, g_mhn, skip_m,
        w_out, g_cross, g_mem, w_q_x, w_kv_x, w_o_x, g_ffn, w_router_g, b_router_g, w_router_e,
        b_router_e, w1, w3, w2, g_final,
    )
    return second_block(
        x, ffn1_norm_2, ffn1_w_in_2, ffn1_w_out_2, mix_norm_2, mix_w_in_2, mix_gate_bias_2,
        na_rpb_2, na_w_out_2, f_w_out_2, mix_w_o_2, ffn2_norm_2, ffn2_w_in_2, ffn2_w_out_2,
        final_norm_2,
    )


_drawn_inputs = setup_inputs


def setup_inputs(seed=0):
    import zlib

    import numpy as np

    out = dict(_drawn_inputs(seed))
    spreads = {}
    factors = {'b_i': 64.0,
     'g_mhn': 3.216,
     'skip_m': 2.984,
     'g_cross': 6.892,
     'g_mem': 6.278,
     'b_router_g': 33.408,
     'b_router_e': 26.032,
     'mix_gate_bias_2': 2.873,
     'g_ffn': 8.0}
    for name, (base, spread) in spreads.items():
        noise = np.random.default_rng([zlib.crc32(name.encode()), seed]).standard_normal(out[name].shape)
        drawn = base * np.exp(spread * noise) if base else spread * noise
        out[name] = __import__('jax').numpy.asarray(drawn.astype(out[name].dtype))
    for name, factor in factors.items():
        out[name] = (out[name] * factor).astype(out[name].dtype)
    return out
```

```python
from contextlib import ExitStack, contextmanager

import concourse.bass as bass
from concourse import mybir
import numpy as np

F32 = mybir.dt.float32
F32R = mybir.dt.float32r
I32 = mybir.dt.int32
ALU = mybir.AluOpType
ACT = mybir.ActivationFunctionType
AX_X = mybir.AxisListType.X

P = 128
T = 512
D = 1024
KD = D // P
MEM = 256
EPS = 1e-6
LAYERS = 2
HEAD = 64
PAIRS = 4
XPAIRS = 2
QT = T // P
M_HEADS = 4
GROUPS = 4
EXPERTS = 16
FF_MOE = 512
FT_MOE = FF_MOE // P
D_FF = 2816
HALF_FT = D_FF // P // 2
PANEL = KD * P
WIDE = HALF_FT * P
GRID_W = 64
NA_ROWS, NA_COLS = 8, 16
BIAS_ROWS = 14
F_GROUPS = 4
ATT_SCALE = HEAD ** -0.5
M_SCALE = P ** -0.5
NEG = -1e30

PI_LOW = 3.1415925
TWO_PI_PARTS = (6.28125, 0.0019340515136718750, float(2 * np.pi - 6.28125 - 0.0019340515136718750))

N_PANELS1 = 2 * XPAIRS + 2 + 6 * PAIRS + KD + XPAIRS + 2 + 1
E_PANELS = 3 * FT_MOE
E_SLOTS = 6
MIX2 = 4 * PAIRS + 3 * KD + KD

SEMS = (
    "consts_in x_in mem_in pos_in raw_in0 raw_in1 heads_in bias_in0 bias_in1 dft_in stored "
    "split_hi split_lo gemm_done gemm_taken scores_full scores_taken turned_full turned_taken "
    "out_full out_taken den_full den_taken operand_ready sumsq_ready ms_ready std_ready "
    "dve_step act_step logits_ready exp_done probs_ready turn_ready qk_ready conv_done conv_ready "
    "sin_ready sin_done gate_ready gate_done rows_ready m_args_ready m_exp_ready "
    "act_out route_args route_done out_ready "
    "xn_ready mask_ready rounds_ready weights_in0 weights_in1 weights_in2 weights_in3 weights_in4 weights_in5 "
    "panel_done select_step select_ready select_turned slots_turned gathered gathered_taken0 gathered_taken1 gate_act hidden_ready half_done "
    "result_ready scattered added experts_done"
).split()


RINGS = ("split_hi", "split_lo", "gemm_done", "gemm_taken", "scores_full", "scores_taken", "turned_full", "turned_taken")


class Counts:

    def __init__(self, eng, who, trips):
        self.eng, self.who, self.trips = eng, who, trips
        self.n = {name: 0 for name in SEMS}
        self.open = []

    def at(self, sem):
        return self.n[sem.name]

    def add(self, sem, by=1):
        self.n[sem.name] += by
        return by

    def skip(self, sem, by=1):
        self.n[sem.name] += by

    def now(self, sem, off=0):
        value = self.n[sem.name] + off
        assert value > 0, (self.who, sem.name)
        for label, reg in self.open:
            per_trip = self.trips.get((self.who, label, sem.name), 0)
            if per_trip:
                value = reg * per_trip + value
        return value

    def next(self, sem, by=1):
        self.n[sem.name] += by
        return self.now(sem)

    @contextmanager
    def loop(self, label, trips):
        before = dict(self.n)
        with self.eng.Fori(0, trips) as reg:
            self.open.append((label, reg))
            yield reg
            self.open.pop()
        for name, start in before.items():
            per_trip = self.n[name] - start if self.n[name] is not None else 0
            assert per_trip % 2 == 0 or name not in RINGS, (self.who, label, name, per_trip)
            self.trips[self.who, label, name] = per_trip
            if start is None:
                continue
            if isinstance(trips, int):
                self.n[name] = start + trips * per_trip
            elif per_trip:
                self.n[name] = None


def build(nc, a, trips):
    ctx = ExitStack()
    with ctx:
        def sb(name, cols, dt=F32):
            return ctx.enter_context(nc.sbuf_tensor(name, [P, cols], dt))

        def f32(ap):
            return ap.bitcast(F32)

        X = sb("X", KD * T)
        XH = sb("XH", KD * T, F32R)
        XL = sb("XL", KD * T, F32R)
        RAW = [sb(f"RAW{i}", WIDE) for i in range(2)]
        with ExitStack() as products:
            def rounded(name, cols):
                return products.enter_context(nc.sbuf_tensor(name, [P, cols], F32R))

            AH = rounded("AH", 2 * KD * T)
            AL = rounded("AL", 2 * KD * T)
            WH = [rounded(f"WH{i}", WIDE) for i in range(2)]
            WL = [rounded(f"WL{i}", WIDE) for i in range(2)]
        with ExitStack() as experts:
            def plain(name, cols):
                return experts.enter_context(nc.sbuf_tensor(name, [P, cols], F32))[:, :]

            XN = plain("XN", KD * T)
            XT = plain("XT", KD * T)
            SEL, WSEL, SLOTS_T, HID, GACT = (plain(n, T) for n in ("SEL", "WSEL", "SLOTS_T", "HID", "GACT"))
            XG = plain("XG", KD * P)
            Y = plain("Y", D)
            IOTA, BEFORE = plain("IOTA", P), plain("BEFORE", P)
            RANK, SHARE = (plain(n, QT * (EXPERTS + 1)) for n in ("RANK", "SHARE"))
            E_PANEL = [RAW[i][:, 0:PANEL] for i in range(2)] + [plain(f"E_PANEL{i}", PANEL) for i in range(2, E_SLOTS)]
        ctx.enter_context(nc.sbuf_tensor("KEPT", [P, 4 * KD * T + 4 * WIDE], F32))
        BIG = sb("BIG", 2 * QT * T)
        LN_COLS = P * QT * (QT + 1) // 2
        LN = BIG[:, 0:LN_COLS]
        COS = BIG[:, LN_COLS:LN_COLS + T]
        SIN = BIG[:, LN_COLS + T:LN_COLS + 2 * T]
        GATE = BIG[:, LN_COLS + 2 * T:LN_COLS + 3 * T]
        ENM = BIG[:, LN_COLS + 3 * T:LN_COLS + 4 * T]
        KX = BIG[:, LN_COLS + 4 * T:LN_COLS + 5 * T]
        ROT = BIG[:, LN_COLS + 5 * T:LN_COLS + 5 * T + P]
        TRI = BIG[:, LN_COLS + 5 * T + P:LN_COLS + 5 * T + 2 * P]
        CT = BIG[:, 0:QT * T]
        NST = BIG[:, QT * T:2 * QT * T]
        IDENT = sb("IDENT", P)
        COLMASK = sb("COLMASK", GRID_W)
        CS = sb("CS", 2 * P)
        ONES = sb("ONES", P)
        VEC = sb("VEC", a["vec"].shape[1])
        SMALL = sb("SMALL", 48)
        QB = sb("QB", T)
        KB = sb("KB", T)
        VB = sb("VB", T)
        VT = sb("VT", T)
        PROB = [sb(f"PROB{i}", T) for i in range(2)]
        PT = sb("PT", QT * T)
        AR = sb("AR", 6 * T)
        C, MV, MQ, MK, SG, VX = (AR[:, i * T:(i + 1) * T] for i in range(6))
        ROUNDS = SMALL[0:1, 12:13].bitcast(I32)
        PADU = sb("PADU", T + 4)
        U = PADU[:, 4:4 + T]
        BIAS = [AR[:, i * BIAS_ROWS * GRID_W:(i + 1) * BIAS_ROWS * GRID_W] for i in range(2)]
        AB = AR[:, 2 * BIAS_ROWS * GRID_W:2 * BIAS_ROWS * GRID_W + 2 * T]
        UT = U
        WQK = sb("WQK", 2 * P)
        TA = sb("TA", T)
        TB = sb("TB", T)
        RS = sb("RS", T)
        SQ = sb("SQ", T)

        def bank(name):
            return ctx.enter_context(nc.psum_tensor(name, [P, T], F32))

        GEMM = [bank(f"GEMM{i}") for i in range(2)]
        SCORE = [bank(f"SCORE{i}") for i in range(2)]
        TURN = [bank(f"TURN{i}") for i in range(2)]
        OUT = bank("OUT")
        DEN = bank("DEN")
        (consts_in, x_in, mem_in, pos_in, raw_in0, raw_in1, heads_in, bias_in0,
         bias_in1, dft_in, stored, split_hi, split_lo, gemm_done, gemm_taken, scores_full,
         scores_taken, turned_full, turned_taken, out_full, out_taken, den_full, den_taken, operand_ready,
         sumsq_ready, ms_ready, std_ready, dve_step, act_step, logits_ready, exp_done, probs_ready,
         turn_ready, qk_ready, conv_done, conv_ready, sin_ready, sin_done, gate_ready, gate_done,
         rows_ready, m_args_ready, m_exp_ready, act_out, route_args, route_done, out_ready, xn_ready,
         mask_ready, rounds_ready, weights_in0, weights_in1, weights_in2, weights_in3, weights_in4, weights_in5,
         panel_done, select_step, select_ready, select_turned, slots_turned, gathered, gathered_taken0, gathered_taken1, gate_act, hidden_ready,
         half_done, result_ready, scattered, added, experts_done) = (
            ctx.enter_context(nc.semaphore(name)) for name in SEMS)
        gathered_taken = (gathered_taken0, gathered_taken1)
        weights_in = (weights_in0, weights_in1, weights_in2, weights_in3, weights_in4, weights_in5)
        raw_in, bias_in = (raw_in0, raw_in1), (bias_in0, bias_in1)
        block = ctx.enter_context(nc.Block())

        col = a["cols"]

        def vec(name, i=0, n=1):
            return VEC[:, col[name] + i:col[name] + i + n]

        def tile(big, d, n=T):
            return big[:, d * n:(d + 1) * n] if isinstance(d, int) else big[:, bass.ds(d * n, n)]

        FREE_BIAS_OFF = [P * i * (i + 1) // 2 for i in range(QT)]

        @block.sync
        def _(sp):
            c = Counts(sp, "sp", trips)

            def load(src, width=PANEL):
                slot = c.at(split_lo) % 2
                if c.at(split_lo) > 1:
                    sp.wait_ge(split_lo, c.now(split_lo, -1))
                c.skip(split_lo)
                sp.dma_start(RAW[slot][:, 0:width], src).then_inc(raw_in[slot], c.add(raw_in[slot], 16))

            def panel(table, i, width=PANEL):
                return table[i] if isinstance(i, int) else table[bass.ds(i, 1)].rearrange("o p n -> (o p) n")

            for name, dst in (("vec", VEC), ("ident", IDENT), ("rot", ROT), ("tri", TRI), ("colmask", COLMASK),
                              ("cs", CS), ("ln", LN)):
                sp.dma_start(dst[:, :], a[name]).then_inc(consts_in, c.add(consts_in, 16))
            sp.dma_start(PT[:, 0:KD * MEM], a["memT"]).then_inc(mem_in, c.add(mem_in, 16))
            sp.dma_start(TB[:, :].bitcast(I32), a["positions"].partition_broadcast(P)).then_inc(pos_in, c.add(pos_in, 16))
            load(a["panels1"][0])
            load(a["panels1"][1])
            sp.dma_start(X[:, :], a["xT"]).then_inc(x_in, c.add(x_in, 16))
            base = 2 * XPAIRS + 2
            for i in range(2, base):
                load(a["panels1"][i])
            with c.loop("mix1", PAIRS) as i:
                for j in range(6):
                    load(panel(a["panels1"], i * 6 + (base + j)))
                    if j == 3:
                        sp.wait_ge(conv_done, c.next(conv_done))
                        sp.dma_start(WQK[:, :], panel(a["w_qk_m"], i)).then_inc(heads_in, c.add(heads_in, 16))
            base += 6 * PAIRS
            with c.loop("rest1", (N_PANELS1 - base) // 2) as i:
                load(panel(a["panels1"], i * 2 + base))
                load(panel(a["panels1"], i * 2 + (base + 1)))
            load(a["panels1"][N_PANELS1 - 1])
            sp.wait_ge(rounds_ready, c.next(rounds_ready))
            rounds = sp.value_load(ROUNDS, min_val=1, max_val=QT)
            c.skip(panel_done, E_SLOTS)
            with c.loop("rounds", rounds):
                with c.loop("experts", EXPERTS) as e:
                    for p in range(E_PANELS):
                        sp.wait_ge(panel_done, c.now(panel_done, 1 - E_SLOTS))
                        c.skip(panel_done)
                        at = weights_in[p % E_SLOTS]
                        sp.dma_start(E_PANEL[p % E_SLOTS], panel(a["experts"], e * E_PANELS + p)).then_inc(at, c.add(at, 16))
            sp.wait_ge(experts_done, c.next(experts_done))
            sp.wait_ge(route_args, c.next(route_args))
            sp.dma_start(CT, a["ct"]).then_inc(dft_in, c.add(dft_in, 16))
            sp.dma_start(NST, a["nst"]).then_inc(dft_in, c.add(dft_in, 16))

            def ffn(label, l, which):
                for half in range(2):
                    at = l * 88 + (which * 44 + half * 22)
                    with c.loop(f"up{label}{half}", HALF_FT) as f:
                        load(panel(a["up2"], f * 2 + at))
                        load(panel(a["up2"], f * 2 + (at + 1)))
                    at = l * 32 + (which * 16 + half * 8)
                    with c.loop(f"down{label}{half}", KD // 2) as d:
                        load(panel(a["down2"], d * 2 + at), WIDE)
                        load(panel(a["down2"], d * 2 + (at + 1)), WIDE)

            c.skip(probs_ready, 2 * QT * (PAIRS + XPAIRS))
            with c.loop("layers", LAYERS) as l:
                ffn("a", l, 0)
                with c.loop("na", PAIRS) as i:
                    for j in range(4):
                        load(panel(a["mix2"], i * 4 + (l * MIX2 + j)))
                        if j in (1, 2):
                            sp.wait_ge(probs_ready, c.now(probs_ready))
                            sp.dma_start(
                                BIAS[j - 1], panel(a["bias"], i * 2 + (l * 8 + (j - 1)))).then_inc(bias_in[j - 1], c.add(bias_in[j - 1], 16))
                    c.skip(probs_ready, 2 * QT)
                with c.loop("comb", KD // 2) as d:
                    for j in range(6):
                        load(panel(a["mix2"], d * 6 + (l * MIX2 + 4 * PAIRS + j)))
                with c.loop("wo", KD // 2) as d:
                    for j in range(2):
                        load(panel(a["mix2"], d * 2 + (l * MIX2 + 4 * PAIRS + 3 * KD + j)))
                ffn("b", l, 1)
            sp.wait_ge(out_ready, c.next(out_ready, KD))
            sp.dma_start(a["outT"], X[:, :]).then_inc(stored, c.add(stored, 16))
            sp.wait_ge(stored, c.now(stored))

        @block.gpsimd
        def _(pool):
            c = Counts(pool, "pool", trips)

            def subtract_lo(width=PANEL):
                slot = c.at(split_lo) % 2
                pool.wait_ge(split_hi, c.next(split_hi))
                pool.tensor_tensor(WL[slot][:, 0:width], RAW[slot][:, 0:width],
                                                      f32(WH[slot][:, 0:width]), ALU.subtract).then_inc(split_lo, c.add(split_lo))

            with c.loop("first", N_PANELS1 // 2):
                subtract_lo()
                subtract_lo()
            subtract_lo()
            def ffn(label):
                for half in range(2):
                    with c.loop(f"up{label}{half}", HALF_FT):
                        subtract_lo()
                        subtract_lo()
                    with c.loop(f"down{label}{half}", KD // 2):
                        subtract_lo(WIDE)
                        subtract_lo(WIDE)

            with c.loop("layers", LAYERS):
                ffn("a")
                with c.loop("mix2", MIX2 // 2):
                    subtract_lo()
                    subtract_lo()
                ffn("b")

        @block.tensor
        def _(pe):
            c = Counts(pe, "pe", trips)
            c.skip(out_taken)
            c.skip(den_taken)

            def next_panel():
                slot = c.at(split_lo) % 2
                pe.wait_ge(split_lo, c.next(split_lo))
                return WH[slot], WL[slot]

            def gemm(w, blocks, srcs, n=T):
                wh, wl = w
                ps = GEMM[c.at(gemm_taken) % 2][:, 0:n]
                if c.at(gemm_taken) > 1:
                    pe.wait_ge(gemm_taken, c.now(gemm_taken, -1))
                c.skip(gemm_taken)
                for j, (b, (hi, lo)) in enumerate(zip(blocks, srcs)):
                    whb, wlb = wh[:, b * P:(b + 1) * P], wl[:, b * P:(b + 1) * P]
                    pe.matmul(ps, whb, hi, start=(j == 0), stop=False)
                    pe.matmul(ps, whb, lo, start=False, stop=False)
                    mm = pe.matmul(ps, wlb, hi, start=False, stop=(j == len(blocks) - 1))
                mm.then_inc(gemm_done, c.add(gemm_done))

            def score_bank():
                at = c.at(scores_taken) % 2
                if c.at(scores_taken) > 1:
                    pe.wait_ge(scores_taken, c.now(scores_taken, -1))
                c.skip(scores_taken)
                return SCORE[at]

            def turn_bank():
                at = c.at(turned_taken) % 2
                if c.at(turned_taken) > 1:
                    pe.wait_ge(turned_taken, c.now(turned_taken, -1))
                c.skip(turned_taken)
                return TURN[at]

            x_tiles = [(tile(XH, k), tile(XL, k)) for k in range(KD)]
            a_tiles = [(tile(AH, k), tile(AL, k)) for k in range(2 * KD)]
            mem_tiles = [(tile(AH, k, MEM), tile(AL, k, MEM)) for k in range(KD)]
            eight = range(KD)

            def den_bank():
                pe.wait_ge(den_taken, c.now(den_taken))
                c.skip(den_taken)
                return DEN

            def sum_squares(n=T):
                pe.wait_ge(sumsq_ready, c.next(sumsq_ready, KD))
                ps = den_bank()
                pe.matmul(ps[:, 0:n], ONES[:, :], SQ[:, 0:n], start=True, stop=True).then_inc(den_full, c.add(den_full))

            def turn(src, blocks, rows=P):
                ps = turn_bank()
                for at, j in enumerate(blocks):
                    mm = pe.transpose(ps[:, at * rows:(at + 1) * rows], src[0:rows, j * P:(j + 1) * P],
                                      IDENT[0:rows, 0:rows])
                mm.then_inc(turned_full, c.add(turned_full))

            def attention(n_keys, causal, v, between=None, k_src=KB):
                def keys(i):
                    return (i + 1) if causal else n_keys

                jobs = [(h, i) for h in range(2) for i in range(QT)]
                for u in range(len(jobs) + 2):
                    if u < len(jobs):
                        h, i = jobs[u]
                        part = slice(h * HEAD, (h + 1) * HEAD)
                        ps = score_bank()
                        pe.matmul(
                            ps[:, 0:keys(i) * P], QB[part, i * P:(i + 1) * P], k_src[part, 0:keys(i) * P],
                            start=True, stop=True).then_inc(scores_full, c.add(scores_full))
                    if between and u in between:
                        between[u]()
                    if u in (QT + 2, len(jobs) + 2):
                        values(0, n_keys, causal, v)
                    if u >= 2:
                        h, i = jobs[u - 2]
                        pe.wait_ge(probs_ready, c.next(probs_ready))
                        turn(PROB[u % 2], range(keys(i)))
                values(1, n_keys, causal, v)

            def values(h, n_keys, causal, v):
                pe.wait_ge(turned_taken, c.now(turned_taken))
                if h == 0:
                    pe.wait_ge(out_taken, c.now(out_taken))
                part = slice(h * HEAD, (h + 1) * HEAD)
                for j in range(n_keys):
                    at = j * P if causal else 0
                    mm = pe.matmul(OUT[part, at:T], v[:, j * P + h * HEAD:j * P + (h + 1) * HEAD],
                                   PT[:, j * T + at:(j + 1) * T], start=(j == 0), stop=(j == n_keys - 1))
                mm.then_inc(out_full, c.add(out_full))
                if h == 1:
                    c.skip(out_taken)

            def ffn(label):
                for half in range(2):
                    if half == 0:
                        pe.wait_ge(operand_ready, c.next(operand_ready, KD))
                        sum_squares()
                    with c.loop(f"up{label}{half}", HALF_FT):
                        gemm(next_panel(), eight, x_tiles)
                        gemm(next_panel(), eight, x_tiles)
                    c.skip(operand_ready, HALF_FT)
                    with c.loop(f"down{label}{half}", KD // 2):
                        pe.wait_ge(operand_ready, c.now(operand_ready))
                        gemm(next_panel(), range(HALF_FT), a_tiles)
                        gemm(next_panel(), range(HALF_FT), a_tiles)

            def expert():
                pe.wait_ge(select_ready, c.next(select_ready))
                for half in range(2):
                    for k in range(KD // 2):
                        d = half * (KD // 2) + k
                        for t in range(QT):
                            mm = pe.matmul(SCORE[half][:, k * P:(k + 1) * P], XT[:, t * D + d * P:t * D + (d + 1) * P],
                                           tile(SEL, t, P), start=(t == 0), stop=(t == QT - 1))
                    mm.then_inc(gathered, c.add(gathered))
                for t in range(QT):
                    mm = pe.transpose(DEN[:, t * P:(t + 1) * P], tile(WSEL, t, P), IDENT[:, :])
                mm.then_inc(select_turned, c.add(select_turned))
                for p in range(2 * FT_MOE):
                    up, f = divmod(p, FT_MOE)
                    ps = TURN[0][:, f * P:(f + 1) * P] if not up else (TURN[1], SCORE[0])[f // 2][:, f % 2 * P:(f % 2 + 1) * P]
                    at = weights_in[p % E_SLOTS]
                    pe.wait_ge(at, c.next(at, 16))
                    for k in range(KD):
                        if p == 0 and k % (KD // 2) == 0:
                            half = gathered_taken[k // (KD // 2)]
                            pe.wait_ge(half, c.next(half))
                        mm = pe.matmul(ps, tile(E_PANEL[p % E_SLOTS], k, P), tile(XG, k, P),
                                       start=(k == 0), stop=(k == KD - 1))
                    mm.then_inc(panel_done, c.add(panel_done))
                for half, ps in enumerate((OUT, DEN)):
                    for f in range(FT_MOE):
                        slot = (2 * FT_MOE + f) % E_SLOTS
                        if half == 0:
                            if f % 2 == 0:
                                pe.wait_ge(hidden_ready, c.next(hidden_ready))
                            pe.wait_ge(weights_in[slot], c.next(weights_in[slot], 16))
                        mm = pe.matmul(ps[:, :], tile(HID, f, P), tile(E_PANEL[slot], half), start=(f == 0), stop=(f == FT_MOE - 1))
                        if half == 1:
                            mm.then_inc(panel_done, c.add(panel_done))
                        elif f == FT_MOE - 1:
                            mm.then_inc(half_done, c.add(half_done))
                pe.wait_ge(slots_turned, c.next(slots_turned))
                for d in range(KD):
                    if d % (KD // 2) == 0:
                        pe.wait_ge(result_ready, c.next(result_ready))
                    if d >= 2:
                        pe.wait_ge(added, c.next(added))
                    pe.matmul(GEMM[d % 2][:, :], tile(Y, d, P), SLOTS_T, start=True, stop=True).then_inc(
                        scattered, c.add(scattered))
                c.skip(added, 2)

            pe.wait_ge(consts_in, c.next(consts_in, 7 * 16))
            sum_squares(MEM)
            pe.wait_ge(operand_ready, c.next(operand_ready, KD))
            for pair in range(XPAIRS):
                gemm(next_panel(), eight, mem_tiles, MEM)
                gemm(next_panel(), eight, mem_tiles, MEM)
                pe.wait_ge(gemm_taken, c.now(gemm_taken))
                turn(VT, range(MEM // P))
            sum_squares()
            pe.wait_ge(operand_ready, c.next(operand_ready, KD))
            gemm(next_panel(), eight, x_tiles)
            gemm(next_panel(), eight, x_tiles)
            pe.wait_ge(turn_ready, c.next(turn_ready))
            turn(VB, range(QT), M_HEADS)
            with c.loop("mix1", PAIRS):
                gemm(next_panel(), eight, x_tiles)
                gemm(next_panel(), eight, x_tiles)
                gemm(next_panel(), eight, x_tiles)
                pe.wait_ge(gemm_taken, c.now(gemm_taken, -1))
                turn(VT, range(QT))
                gemm(next_panel(), eight, x_tiles)
                pe.wait_ge(gemm_taken, c.now(gemm_taken, -1))
                pe.matmul(score_bank()[:, :], ROT[:, :], QB[:, :], start=True, stop=True).then_inc(scores_full, c.add(scores_full))
                gemm(next_panel(), eight, x_tiles)
                pe.wait_ge(gemm_taken, c.now(gemm_taken, -1))
                pe.matmul(score_bank()[:, :], ROT[:, :], KB[:, :], start=True, stop=True).then_inc(scores_full, c.add(scores_full))
                pe.wait_ge(gemm_taken, c.now(gemm_taken))
                turn(VT, range(QT))
                pe.wait_ge(conv_ready, c.next(conv_ready))
                pe.wait_ge(heads_in, c.next(heads_in, 16))
                for j in range(2):
                    pe.matmul(score_bank()[:, :], WQK[:, j * P:(j + 1) * P], C,
                                                    start=True, stop=True).then_inc(scores_full, c.add(scores_full))
                pe.wait_ge(qk_ready, c.next(qk_ready))
                attention(QT, True, VB, {2: lambda: gemm(next_panel(), eight, x_tiles)})
                for at in (0, 32):
                    pe.wait_ge(rows_ready, c.next(rows_ready))
                    pe.matmul(score_bank()[:, :], ONES[at:at + M_HEADS, :],
                                                    TB[at:at + M_HEADS, :], start=True, stop=True).then_inc(scores_full, c.add(scores_full))
                pe.wait_ge(scores_taken, c.now(scores_taken))
                for j in range(QT):
                    pe.matmul(score_bank()[:, j * P:T], MK[:, j * P:(j + 1) * P],
                                                    MQ[:, j * P:T], start=True, stop=True).then_inc(scores_full, c.add(scores_full))
                pe.wait_ge(out_taken, c.now(out_taken))
                c.skip(out_taken)
                den_bank()
                for j in range(QT):
                    pe.wait_ge(scores_taken, c.now(scores_taken, j + 1 - QT))
                    w = PT[:, j * T + j * P:(j + 1) * T]
                    num = pe.matmul(OUT[:, j * P:T], MV[:, j * P:(j + 1) * P], w, start=(j == 0), stop=(j == QT - 1))
                    den = pe.matmul(DEN[:, j * P:T], ONES[:, :], w, start=(j == 0), stop=(j == QT - 1))
                num.then_inc(out_full, c.add(out_full))
                den.then_inc(den_full, c.add(den_full))
                pe.wait_ge(sumsq_ready, c.next(sumsq_ready))
                pe.matmul(den_bank()[:, :], ONES[:, :], TB[:, :], start=True, stop=True).then_inc(den_full, c.add(den_full))
                c.skip(operand_ready)
            pe.wait_ge(operand_ready, c.now(operand_ready))
            pe.wait_ge(out_taken, c.now(out_taken))
            with c.loop("wout", KD // 2):
                gemm(next_panel(), eight, a_tiles)
                gemm(next_panel(), eight, a_tiles)
            sum_squares()
            pe.wait_ge(operand_ready, c.next(operand_ready, KD))
            for pair in range(XPAIRS):
                gemm(next_panel(), eight, x_tiles)
                pe.wait_ge(gemm_taken, c.now(gemm_taken))
                attention(MEM // P, False, VX[:, pair * MEM:(pair + 1) * MEM],
                          k_src=KX[:, pair * MEM:(pair + 1) * MEM])
            pe.wait_ge(out_taken, c.now(out_taken))
            for half in range(2):
                w = next_panel()
                for d in range(KD // 2):
                    gemm(w, (2 * d, 2 * d + 1), a_tiles)
            sum_squares()
            pe.wait_ge(operand_ready, c.next(operand_ready, KD))
            gemm(next_panel(), eight, x_tiles)
            pe.wait_ge(turn_ready, c.next(turn_ready))
            turn(TA, range(QT), GROUPS + EXPERTS)
            for d in range(KD):
                pe.wait_ge(xn_ready, c.next(xn_ready))
                turn(tile(XN, d), range(QT))
            pe.wait_ge(mask_ready, c.next(mask_ready))
            ps = score_bank()
            mask = [TB[:, 192 + t * EXPERTS:192 + (t + 1) * EXPERTS] for t in range(QT)]
            for t in range(QT):
                rank = ps[:, t * EXPERTS:(t + 1) * EXPERTS]
                for s in range(t):
                    pe.matmul(rank, ONES[:, :], mask[s], start=(s == 0), stop=False)
                mm = pe.matmul(rank, BEFORE, mask[t], start=(t == 0), stop=True)
                if t == 0:
                    mm.then_inc(panel_done, c.add(panel_done, E_SLOTS))
            for t in range(QT):
                pe.matmul(ps[:, QT * EXPERTS:(QT + 1) * EXPERTS], ONES[:, :], mask[t], start=(t == 0), stop=(t == QT - 1))
            pe.matmul(ps[:, P:2 * P], ONES[:, :], BEFORE, start=True, stop=True).then_inc(scores_full, c.add(scores_full))
            pe.wait_ge(turned_taken, c.now(turned_taken))
            pe.wait_ge(rounds_ready, c.next(rounds_ready))
            rounds = pe.value_load(ROUNDS, min_val=1, max_val=QT)
            with c.loop("rounds", rounds):
                with c.loop("experts", EXPERTS):
                    expert()
            sum_squares()
            pe.wait_ge(dft_in, c.next(dft_in, 32))
            with c.loop("layers", LAYERS):
                ffn("a")
                pe.wait_ge(operand_ready, c.next(operand_ready, KD))
                sum_squares()
                with c.loop("na", PAIRS):
                    gemm(next_panel(), eight, x_tiles)
                    gemm(next_panel(), eight, x_tiles)
                    gemm(next_panel(), eight, x_tiles)
                    pe.wait_ge(gemm_taken, c.now(gemm_taken))
                    turn(VT, range(0, 2))
                    turn(VT, range(2, 4))
                    gemm(next_panel(), eight, x_tiles)
                    pe.wait_ge(gemm_taken, c.now(gemm_taken))
                    for b in range(2):
                        ps = score_bank()
                        for t in range(2):
                            mm = pe.matmul(ps[:, t * 2 * P:(t + 1) * 2 * P],
                                           UT[:, (2 * b + t) * P:(2 * b + t + 1) * P], CS[:, :],
                                           start=True, stop=True)
                        mm.then_inc(scores_full, c.add(scores_full))

                    def dft():
                        pe.wait_ge(scores_taken, c.now(scores_taken, -3))
                        den_bank()
                        for t in range(QT):
                            pe.matmul(DEN[:, :], AB[:, t * 2 * P:t * 2 * P + P], tile(CT, t),
                                      start=(t == 0), stop=False)
                            mm = pe.matmul(DEN[:, :], AB[:, t * 2 * P + P:(t + 1) * 2 * P], tile(NST, t),
                                           start=False, stop=(t == QT - 1))
                        mm.then_inc(den_full, c.add(den_full))

                    attention(QT, False, VB, {2: dft})
                    c.skip(operand_ready)
                with c.loop("comb", KD // 2):
                    pe.wait_ge(out_taken, c.now(out_taken))
                    pe.wait_ge(operand_ready, c.now(operand_ready))
                    for d in range(2):
                        gemm(next_panel(), eight, x_tiles)
                        gemm(next_panel(), eight, x_tiles)
                        w = next_panel()
                        gemm(w, range(0, PAIRS), a_tiles[0:PAIRS])
                        gemm(w, range(PAIRS, 2 * PAIRS), a_tiles[PAIRS:KD])
                    c.skip(operand_ready, 2)
                with c.loop("wo", KD // 2):
                    pe.wait_ge(operand_ready, c.now(operand_ready))
                    gemm(next_panel(), eight, a_tiles[KD:])
                    gemm(next_panel(), eight, a_tiles[KD:])
                ffn("b")
            c.skip(operand_ready, KD)
            sum_squares()

        @block.scalar
        def _(act):
            c = Counts(act, "act", trips)
            c.skip(out_full)

            def round_hi(width=PANEL, units=1):
                slot = c.at(split_hi) % 2
                act.wait_ge(raw_in[slot], c.next(raw_in[slot], 16))
                if c.at(gemm_done) > 1:
                    act.wait_ge(gemm_done, c.now(gemm_done, -1))
                c.skip(gemm_done, units)
                act.activation(WH[slot][:, 0:width], RAW[slot][:, 0:width], ACT.Copy).then_inc(split_hi, c.add(split_hi))

            def root(n=T):
                act.wait_ge(ms_ready, c.next(ms_ready))
                act.activation(RS[:, 0:n], RS[:, 0:n], ACT.Sqrt).then_inc(std_ready, c.add(std_ready))

            def turned(dst, src_cols, rows=P):
                at = c.at(turned_full) % 2
                act.wait_ge(turned_full, c.next(turned_full))
                act.copy(dst, TURN[at][0:rows, src_cols]).then_inc(turned_taken, c.add(turned_taken))

            def attention(n_keys, causal, between=None):
                def keys(i):
                    return (i + 1) if causal else n_keys

                jobs = [(h, i) for h in range(2) for i in range(QT)]
                for u in range(len(jobs) + 2):
                    if u >= 2:
                        h, i = jobs[u - 2]
                        if i == 0:
                            act.wait_ge(out_full, c.now(out_full))
                        n = keys(i)
                        at = c.at(turned_full) % 2
                        act.wait_ge(turned_full, c.next(turned_full))
                        dst = PT[:, :].rearrange("p (j t) -> p j t", j=QT)[:, 0:n, i * P:(i + 1) * P]
                        act.copy(dst, TURN[at][:, 0:n * P].rearrange("p (j t) -> p j t", j=n)).then_inc(turned_taken, c.add(turned_taken))
                        if i == QT - 1:
                            c.skip(out_full)
                    if u < len(jobs):
                        h, i = jobs[u]
                        act.wait_ge(logits_ready, c.next(logits_ready))
                        p = PROB[u % 2][:, 0:keys(i) * P]
                        act.activation(p, p, ACT.Exp, bias=SMALL[:, u % 2:u % 2 + 1],
                                                          accum_out=SMALL[:, 2 + u % 2:3 + u % 2]).then_inc(exp_done, c.add(exp_done))
                    if between and u in between:
                        between[u]()

            def silu_unit():
                act.wait_ge(gemm_taken, c.now(gemm_done, -1))
                act.activation(TB[:, :], TA[:, :], ACT.Silu).then_inc(act_out, c.add(act_out))

            def sigmoid_unit(dst, src, off, **bias):
                act.wait_ge(gemm_taken, c.now(gemm_done, off))
                act.activation(dst, src, ACT.Sigmoid, **bias).then_inc(act_out, c.add(act_out))

            def ffn(label):
                for half in range(2):
                    if half == 0:
                        root()
                    with c.loop(f"up{label}{half}", HALF_FT):
                        round_hi()
                        round_hi()
                        silu_unit()
                    with c.loop(f"down{label}{half}", KD // 2):
                        round_hi(WIDE)
                        round_hi(WIDE)

            act.wait_ge(sin_ready, c.next(sin_ready))
            act.activation(SIN, SIN, ACT.Sin).then_inc(sin_done, c.add(sin_done))
            act.wait_ge(sin_ready, c.next(sin_ready))
            act.activation(COS, COS, ACT.Sin).then_inc(sin_done, c.add(sin_done))
            round_hi()
            round_hi()
            root(MEM)
            for pair in range(XPAIRS):
                if pair:
                    round_hi()
                    round_hi()
                turned(VX[:, pair * MEM:(pair + 1) * MEM], slice(0, MEM))
            round_hi()
            round_hi()
            root()
            act.wait_ge(gate_ready, c.next(gate_ready))
            act.activation(TB[0:M_HEADS, :], TB[0:M_HEADS, :], ACT.Exp).then_inc(gate_done, c.add(gate_done))
            act.wait_ge(gate_ready, c.next(gate_ready))
            act.activation(TB[0:M_HEADS, :], TB[0:M_HEADS, :], ACT.Ln).then_inc(gate_done, c.add(gate_done))
            act.wait_ge(gate_ready, c.next(gate_ready))
            act.activation(GATE[32:32 + M_HEADS, :], GATE[32:32 + M_HEADS, :], ACT.Exp, scale=-1.0).then_inc(gate_done, c.add(gate_done))
            turned(SMALL[:, 16:16 + QT * M_HEADS], slice(0, QT * M_HEADS))
            with c.loop("mix1", PAIRS) as m:
                round_hi()
                round_hi()
                round_hi()
                round_hi()
                turned(MV, slice(0, T))
                act.wait_ge(conv_done, c.next(conv_done))
                act.activation(SG, C, ACT.Sigmoid).then_inc(act_out, c.add(act_out))
                round_hi()
                round_hi()
                turned(VB[:, :], slice(0, T))
                attention(QT, True, {6: lambda: sigmoid_unit(SG, TA[:, :], 0)})
                act.wait_ge(out_full, c.now(out_full))
                for j in range(QT):
                    bias = SMALL[:, bass.ds(m + (16 + j * M_HEADS), 1)]
                    if j == 0:
                        act.wait_ge(m_args_ready, c.next(m_args_ready))
                    ins = act.activation(PT[:, j * T + j * P:j * T + (j + 1) * P], VT[:, j * P:(j + 1) * P], ACT.Exp, bias=bias)
                    if j < QT - 1:
                        ins.then_inc(act_step, c.add(act_step))
                        ins = act.activation(PT[:, j * T + (j + 1) * P:(j + 1) * T], U[:, (j + 1) * P:T], ACT.Exp, bias=bias)
                    ins.then_inc(m_exp_ready, c.add(m_exp_ready))
                c.skip(out_full)
                act.wait_ge(ms_ready, c.next(ms_ready))
                act.activation(TB[:, :], TB[:, :], ACT.Sqrt).then_inc(std_ready, c.add(std_ready))
            with c.loop("wout", KD // 2):
                round_hi()
                round_hi()
            round_hi()
            root()
            for pair in range(XPAIRS):
                if pair == 0:
                    round_hi()
                attention(MEM // P, False)
            for half in range(2):
                round_hi(units=KD // 2)
            round_hi()
            root()
            turned(QB[:, 0:QT * (GROUPS + EXPERTS)], slice(0, QT * (GROUPS + EXPERTS)))
            c.skip(panel_done, E_SLOTS)
            for d in range(KD):
                at = c.at(turned_full) % 2
                act.wait_ge(turned_full, c.next(turned_full))
                act.copy(XT.rearrange("p (t f) -> p t f", t=QT)[:, :, d * P:(d + 1) * P],
                         TURN[at][:, :].rearrange("p (t f) -> p t f", t=QT)).then_inc(turned_taken, c.add(turned_taken))
            for k in range(2):
                act.wait_ge(route_args, c.next(route_args))
                ap = SMALL[:, 0:QT] if k else TA[:, 0:QT * GROUPS]
                act.activation(ap, ap, ACT.Exp).then_inc(route_done, c.add(route_done))
            act.wait_ge(rounds_ready, c.next(rounds_ready))
            rounds = act.value_load(ROUNDS, min_val=1, max_val=QT)
            with c.loop("rounds", rounds):
                with c.loop("experts", EXPERTS):
                    act.wait_ge(gathered, c.next(gathered))
                    act.copy(XG[:, 0:T], SCORE[0][:, :]).then_inc(gathered_taken0, c.add(gathered_taken0))
                    c.skip(gathered)
                    act.wait_ge(select_turned, c.next(select_turned))
                    act.copy(SLOTS_T, DEN[:, :]).then_inc(slots_turned, c.add(slots_turned))
                    act.wait_ge(panel_done, c.next(panel_done, FT_MOE))
                    act.activation(GACT, TURN[0][:, :], ACT.Silu).then_inc(gate_act, c.add(gate_act))
                    c.skip(panel_done, 2 * FT_MOE)
                    act.wait_ge(half_done, c.next(half_done))
                    act.copy(Y[:, 0:T], OUT[:, :]).then_inc(result_ready, c.add(result_ready))
                    act.wait_ge(panel_done, c.now(panel_done))
                    act.copy(Y[:, T:2 * T], DEN[:, :]).then_inc(result_ready, c.add(result_ready))
            root()
            with c.loop("layers", LAYERS) as l:
                ffn("a")
                root()
                with c.loop("na", PAIRS):
                    round_hi()
                    round_hi()
                    round_hi()
                    round_hi()
                    turned(VB[:, 0:T // 2], slice(0, T // 2))
                    turned(VB[:, T // 2:T], slice(0, T // 2))
                    attention(QT, False)
                with c.loop("comb", KD // 2) as d:
                    def gate_bias(s, j):
                        return VEC[:, bass.ds(l * 16 + (d * 2) + (col["gate_b"] + 8 * s + j), 1)]

                    for j in range(2):
                        round_hi()
                        round_hi()
                        sigmoid_unit(TA[:, :], TA[:, :], -1, bias=gate_bias(0, j))
                        round_hi(units=2)
                        sigmoid_unit(TB[:, :], TB[:, :], -2, bias=gate_bias(1, j))
                with c.loop("wo", KD // 2):
                    round_hi()
                    round_hi()
                ffn("b")
            root()

        @block.vector
        def _(v):
            c = Counts(v, "dve", trips)
            small = SMALL

            def step(ins):
                ins.then_inc(dve_step, c.add(dve_step))

            def chain(ins):
                ins.then_inc(dve_step, c.add(dve_step))
                v.wait_ge(dve_step, c.now(dve_step))

            def prep(x, gain, hi, lo, n=T):
                step(v.tensor_tensor(TA[:, 0:n], x, x, ALU.mult))
                chain(v.tensor_scalar(hi, x, gain, None, ALU.mult))
                v.scalar_tensor_tensor(lo, x, gain, f32(hi), ALU.mult, ALU.subtract).then_inc(operand_ready, c.add(operand_ready))
                v.tensor_tensor(SQ[:, 0:n], SQ[:, 0:n], TA[:, 0:n], ALU.add).then_inc(sumsq_ready, c.add(sumsq_ready))
                v.wait_ge(sumsq_ready, c.now(sumsq_ready))

            def clear_squares():
                step(v.memset(SQ[:, :], 0.0))

            def scores_in():
                at = c.at(scores_full) % 2
                v.wait_ge(scores_full, c.next(scores_full))
                return SCORE[at]

            def den_in():
                v.wait_ge(den_full, c.next(den_full))
                return DEN

            def rstd(n=T):
                ps = den_in()
                v.tensor_scalar(RS[:, 0:n], ps[:, 0:n], 1.0 / D, None, ALU.mult).then_inc(den_taken, c.add(den_taken))
                v.wait_ge(den_taken, c.now(den_taken))
                v.tensor_scalar(RS[:, 0:n], RS[:, 0:n], EPS, None, ALU.add).then_inc(ms_ready, c.add(ms_ready))
                v.wait_ge(std_ready, c.next(std_ready))
                step(v.reciprocal(RS[:, 0:n], RS[:, 0:n]))

            def gemm_in(n=T):
                at = c.at(gemm_done) % 2
                v.wait_ge(gemm_done, c.next(gemm_done))
                return GEMM[at][:, 0:n]

            def take(dst, scale=1.0, by=None, n=T):
                ps = gemm_in(n)
                by = RS[:, 0:n] if by is None else by
                v.scalar_tensor_tensor(dst, ps, scale, by, ALU.mult, ALU.mult).then_inc(gemm_taken, c.add(gemm_taken))

            def add_to(x, scale=1.0):
                ps = gemm_in()
                v.scalar_tensor_tensor(x, ps, scale, x, ALU.mult, ALU.add).then_inc(gemm_taken, c.add(gemm_taken))
                v.wait_ge(gemm_taken, c.now(gemm_taken))

            def halves(hi, lo, src):
                chain(v.tensor_copy(hi, src))
                v.tensor_tensor(lo, src, f32(hi), ALU.subtract).then_inc(operand_ready, c.add(operand_ready))

            def attention(n_keys, causal, bias, hi, lo, between=None):
                def keys(i):
                    return (i + 1) if causal else n_keys

                jobs = [(h, i) for h in range(2) for i in range(QT)]
                for u in range(len(jobs) + 1):
                    if u < len(jobs):
                        h, i = jobs[u]
                        n = keys(i) * P
                        prob = PROB[u % 2][:, 0:n]
                        if u >= 2:
                            v.wait_ge(turned_full, c.next(turned_full))
                        ps = scores_in()[:, 0:n]
                        if bias is None:
                            v.tensor_copy(prob, ps).then_inc(scores_taken, c.add(scores_taken))
                        else:
                            v.tensor_tensor(prob, ps, bias(h, i), ALU.add).then_inc(scores_taken, c.add(scores_taken))
                        v.wait_ge(scores_taken, c.now(scores_taken))
                        v.tensor_reduce(small[:, u % 2:u % 2 + 1], prob, AX_X, ALU.max, negate=True).then_inc(logits_ready, c.add(logits_ready))
                    if u >= 1:
                        h, i = jobs[u - 1]
                        s = (u - 1) % 2
                        prob = PROB[s][:, 0:keys(i) * P]
                        v.wait_ge(exp_done, c.next(exp_done))
                        chain(v.reciprocal(small[:, 4 + s:5 + s], small[:, 2 + s:3 + s]))
                        v.tensor_scalar(prob, prob, small[:, 4 + s:5 + s], None, ALU.mult).then_inc(probs_ready, c.add(probs_ready))
                    if between and u in between:
                        between[u]()
                v.wait_ge(turned_full, c.next(turned_full, 2))
                v.wait_ge(out_full, c.next(out_full, 2))
                chain(v.tensor_copy(hi, OUT[:, :]))
                v.tensor_tensor(lo, OUT[:, :], f32(hi), ALU.subtract).then_inc(out_taken, c.add(out_taken))

            def ffn(label, gain):
                rstd()
                for half in range(2):
                    with c.loop(f"up{label}{half}", HALF_FT) as f:
                        v.wait_ge(dve_step, c.now(dve_step))
                        v.wait_ge(gemm_taken, c.now(gemm_taken))
                        hidden_unit(tile(AH, f), tile(AL, f), RS[:, :])
                    if half == 0:
                        with c.loop(f"down{label}{half}", KD // 2) as d:
                            add_to(tile(X, d * 2), 0.5)
                            add_to(tile(X, d * 2 + 1), 0.5)
                    else:
                        clear_squares()
                        with c.loop(f"down{label}{half}", KD // 2) as d:
                            v.wait_ge(dve_step, c.now(dve_step))
                            for j in range(2):
                                e = d * 2 + j
                                add_to(tile(X, e), 0.5)
                                prep(tile(X, e), gain(e), tile(XH, e), tile(XL, e))

            def hidden_unit(hi, lo, by):
                take(TA[:, :])
                take(PROB[0][:, :], by=by)
                v.wait_ge(act_out, c.next(act_out))
                v.wait_ge(gemm_taken, c.now(gemm_taken))
                chain(v.tensor_tensor(PROB[0][:, :], PROB[0][:, :], TB[:, :], ALU.mult))
                halves(hi, lo, PROB[0][:, :])
                v.wait_ge(operand_ready, c.now(operand_ready))

            v.memset(ONES[:, :], 1.0).then_inc(out_taken, c.add(out_taken))
            v.memset(PADU[:, 0:4], 0.0).then_inc(den_taken, c.add(den_taken))
            v.memset(SMALL[:, :], 0.0).then_inc(out_full, c.add(out_full))
            clear_squares()
            v.wait_ge(dve_step, c.now(dve_step))
            v.wait_ge(mem_in, c.next(mem_in, 16))
            v.wait_ge(consts_in, c.next(consts_in, 7 * 16))
            for k in range(KD):
                prep(tile(PT, k, MEM), vec("g_mem", k), tile(AH, k, MEM), tile(AL, k, MEM), MEM)
            v.wait_ge(pos_in, c.next(pos_in, 16))
            chain(v.tensor_copy(VB[:, :], TB[:, :].bitcast(I32)))
            chain(v.tensor_scalar(VB[:, :], VB[:, :], vec("invf"), None, ALU.mult))
            chain(v.tensor_scalar(TB[:, :], VB[:, :], float(np.float32(1 / (2 * np.pi))), None, ALU.mult))
            chain(v.tensor_scalar(TB[:, :], TB[:, :], 12582912.0, None, ALU.add))
            chain(v.tensor_scalar(TB[:, :], TB[:, :], -12582912.0, None, ALU.add))
            for part in TWO_PI_PARTS:
                chain(v.scalar_tensor_tensor(VB[:, :], TB[:, :], -part, VB[:, :], ALU.mult, ALU.add))
            v.tensor_scalar(SIN, VB[:, :], PI_LOW, -PI_LOW, ALU.min, ALU.max).then_inc(sin_ready, c.add(sin_ready))
            chain(v.tensor_scalar(VB[:, :], VB[:, :], float(np.pi / 2), None, ALU.add))
            chain(v.tensor_scalar(TB[:, :], VB[:, :], float(np.pi), float(-2 * np.pi), ALU.is_gt, ALU.mult))
            chain(v.tensor_tensor(VB[:, :], VB[:, :], TB[:, :], ALU.add))
            v.tensor_scalar(COS, VB[:, :], PI_LOW, -PI_LOW, ALU.min, ALU.max).then_inc(sin_ready, c.add(sin_ready))
            rstd(MEM)
            v.wait_ge(dve_step, c.now(dve_step))
            for pair in range(XPAIRS):
                take(KX[:, pair * MEM:(pair + 1) * MEM], n=MEM)
                if pair:
                    v.wait_ge(turned_full, c.next(turned_full))
                take(VT[:, 0:MEM], n=MEM)
            v.wait_ge(gemm_taken, c.now(gemm_taken))
            clear_squares()
            v.wait_ge(x_in, c.next(x_in, 16))
            with c.loop("prep_x", KD) as k:
                v.wait_ge(dve_step, c.now(dve_step))
                prep(tile(X, k), VEC[:, bass.ds(k + col["g_mix"], 1)], tile(XH, k), tile(XL, k))
            rstd()
            v.wait_ge(dve_step, c.now(dve_step))
            H4 = slice(0, M_HEADS)
            ig, fg, mn, one = VB[H4, :], PROB[0][H4, :], PROB[1][H4, :], KB[H4, :]
            for dst, b in ((ig, "b_i"), (fg, "b_f")):
                ps = gemm_in()
                v.tensor_tensor(dst, ps[H4, :], RS[H4, :], ALU.mult).then_inc(gemm_taken, c.add(gemm_taken))
                v.wait_ge(gemm_taken, c.now(gemm_taken))
                chain(v.tensor_scalar(dst, dst, vec(b)[H4, :], None, ALU.add))
            step(v.memset(one, 0.0))
            chain(v.tensor_scalar(mn, fg, 0.0, None, ALU.min))
            v.scalar_tensor_tensor(TB[H4, :], mn, 2.0, fg, ALU.mult, ALU.subtract).then_inc(gate_ready, c.add(gate_ready))
            v.wait_ge(gate_done, c.next(gate_done))
            v.tensor_scalar(TB[H4, :], TB[H4, :], 1.0, None, ALU.add).then_inc(gate_ready, c.add(gate_ready))
            v.wait_ge(gate_done, c.next(gate_done))
            chain(v.tensor_tensor(fg, mn, TB[H4, :], ALU.subtract))
            chain(v.tensor_tensor_scan(mn, fg, one, 0.0, ALU.add, ALU.add))
            v.tensor_tensor(ig, ig, mn, ALU.subtract).then_inc(turn_ready, c.add(turn_ready))
            v.wait_ge(turn_ready, c.now(turn_ready))
            chain(v.tensor_tensor_scan(fg, ig, ig, 0.0, ALU.max, ALU.max))
            chain(v.tensor_scalar(GATE[H4, :], fg, -1.0, None, ALU.mult))
            chain(v.tensor_tensor(mn, mn, fg, ALU.add))
            v.tensor_copy(GATE[32:32 + M_HEADS, :], mn).then_inc(gate_ready, c.add(gate_ready))
            v.wait_ge(gate_done, c.next(gate_done))
            v.wait_ge(turned_full, c.next(turned_full, 2))
            v.wait_ge(sin_done, c.next(sin_done, 2))
            with c.loop("mix1", PAIRS) as m:
                def mv(name, j):
                    return VEC[:, bass.ds(m * 8 + (col["mvec"] + j), 1)]

                take(PADU[:, 4:4 + T])
                v.wait_ge(gemm_taken, c.now(gemm_taken))
                chain(v.tensor_scalar(C, PADU[:, 1:1 + T], mv("w", 0), mv("b", 4), ALU.mult, ALU.add))
                for j in range(1, 3):
                    chain(v.scalar_tensor_tensor(C, PADU[:, 1 + j:1 + j + T], mv("w", j), C, ALU.mult, ALU.add))
                v.scalar_tensor_tensor(C, PADU[:, 4:4 + T], mv("w", 3), C, ALU.mult, ALU.add).then_inc(conv_done, c.add(conv_done))
                take(VT[:, :])
                take(QB[:, :], ATT_SCALE)
                v.wait_ge(act_out, c.next(act_out))
                v.tensor_tensor(C, C, SG, ALU.mult).then_inc(conv_ready, c.add(conv_ready))
                take(KB[:, :])
                v.wait_ge(turned_full, c.next(turned_full))
                take(VT[:, :])
                v.wait_ge(gemm_taken, c.now(gemm_taken))
                for j, buf in enumerate((QB, KB)):
                    ps = scores_in()
                    v.tensor_tensor(TA[:, :], ps[:, :], SIN, ALU.mult).then_inc(scores_taken, c.add(scores_taken))
                    chain(v.tensor_tensor(buf[:, :], buf[:, :], COS, ALU.mult))
                    if j == 0:
                        chain(v.tensor_tensor(buf[:, :], buf[:, :], TA[:, :], ALU.add))
                    else:
                        v.tensor_tensor(buf[:, :], buf[:, :], TA[:, :], ALU.add).then_inc(qk_ready, c.add(qk_ready))
                for dst, scale in ((MQ, 1.0), (MK, M_SCALE)):
                    ps = scores_in()
                    v.tensor_scalar(dst, ps[:, :], scale, None, ALU.mult).then_inc(scores_taken, c.add(scores_taken))
                v.wait_ge(scores_taken, c.now(scores_taken))
                v.wait_ge(turned_full, c.next(turned_full))

                attention(QT, True, lambda h, i: LN[:, FREE_BIAS_OFF[i]:FREE_BIAS_OFF[i] + (i + 1) * P],
                          tile(AH, m), tile(AL, m), {4: lambda: take(TA[:, :])})
                v.wait_ge(act_out, c.next(act_out))
                for dst, at in ((U, 0), (ENM, 32)):
                    rows = slice(at, at + M_HEADS)
                    v.tensor_scalar(TB[rows, :], GATE[rows, :], IDENT[rows, bass.ds(m + at, 1)], None, ALU.mult).then_inc(rows_ready, c.add(rows_ready))
                    ps = scores_in()
                    v.tensor_copy(dst, ps[:, :]).then_inc(scores_taken, c.add(scores_taken))
                v.wait_ge(scores_taken, c.now(scores_taken))
                v.tensor_tensor(
                    VT[:, :].rearrange("p (j t) -> p j t", j=QT), U.rearrange("p (j t) -> p j t", j=QT),
                    TRI[:, :].unsqueeze(1).to_broadcast([P, QT, P]), ALU.add).then_inc(m_args_ready, c.add(m_args_ready))
                for j in range(QT):
                    ps = scores_in()
                    v.wait_ge(m_exp_ready, c.next(m_exp_ready))
                    w = PT[:, j * T + j * P:(j + 1) * T]
                    v.tensor_tensor(w, ps[:, j * P:T], w, ALU.mult).then_inc(scores_taken, c.add(scores_taken))
                v.wait_ge(out_full, c.next(out_full))
                v.wait_ge(den_full, c.next(den_full))
                chain(v.tensor_scalar(TA[:, :], DEN[:, :], -1.0, None, ALU.mult))
                v.tensor_tensor(TA[:, :], DEN[:, :], TA[:, :], ALU.max).then_inc(den_taken, c.add(den_taken))
                v.wait_ge(den_taken, c.now(den_taken))
                chain(v.tensor_tensor(TA[:, :], TA[:, :], ENM, ALU.max))
                chain(v.reciprocal(TA[:, :], TA[:, :]))
                v.tensor_tensor(TA[:, :], OUT[:, :], TA[:, :], ALU.mult).then_inc(out_taken, c.add(out_taken))
                v.wait_ge(out_taken, c.now(out_taken))
                v.tensor_tensor(TB[:, :], TA[:, :], TA[:, :], ALU.mult).then_inc(sumsq_ready, c.add(sumsq_ready))
                ps = den_in()
                v.tensor_scalar(TB[:, :], ps[:, :], 1.0 / P, None, ALU.mult).then_inc(den_taken, c.add(den_taken))
                v.wait_ge(den_taken, c.now(den_taken))
                v.tensor_scalar(TB[:, :], TB[:, :], EPS, None, ALU.add).then_inc(ms_ready, c.add(ms_ready))
                v.wait_ge(std_ready, c.next(std_ready))
                chain(v.reciprocal(TB[:, :], TB[:, :]))
                chain(v.tensor_tensor(TA[:, :], TA[:, :], TB[:, :], ALU.mult))
                chain(v.tensor_scalar(TA[:, :], TA[:, :], mv("g", 5), None, ALU.mult))
                chain(v.scalar_tensor_tensor(TA[:, :], C, mv("skip", 6), TA[:, :], ALU.mult, ALU.add))
                chain(v.tensor_tensor(TA[:, :], TA[:, :], SG, ALU.mult))
                halves(tile(AH, m + PAIRS), tile(AL, m + PAIRS), TA[:, :])
                v.wait_ge(operand_ready, c.now(operand_ready))
            clear_squares()
            with c.loop("wout", KD // 2) as d:
                v.wait_ge(dve_step, c.now(dve_step))
                for j in range(2):
                    e = d * 2 + j
                    add_to(tile(X, e))
                    prep(tile(X, e), VEC[:, bass.ds(e + col["g_cross"], 1)], tile(XH, e), tile(XL, e))
            rstd()
            v.wait_ge(dve_step, c.now(dve_step))
            for pair in range(XPAIRS):
                take(QB[:, :], ATT_SCALE)
                attention(MEM // P, False, None, tile(AH, pair), tile(AL, pair))
            clear_squares()
            v.wait_ge(dve_step, c.now(dve_step))
            for d in range(KD):
                add_to(tile(X, d))
                prep(tile(X, d), vec("g_ffn", d), tile(XH, d), tile(XL, d))
            rstd()
            v.wait_ge(dve_step, c.now(dve_step))
            NR = GROUPS + EXPERTS
            ps = gemm_in()
            v.tensor_tensor(TB[0:NR, :], ps[0:NR, :], RS[0:NR, :], ALU.mult).then_inc(gemm_taken, c.add(gemm_taken))
            v.wait_ge(gemm_taken, c.now(gemm_taken))
            v.tensor_scalar(TA[0:NR, :], TB[0:NR, :], vec("b_route")[0:NR, :], None, ALU.add).then_inc(turn_ready, c.add(turn_ready))
            for k in range(KD):
                v.scalar_tensor_tensor(tile(XN, k), tile(X, k), vec("g_ffn", k), RS[:, :], ALU.mult, ALU.mult).then_inc(
                    xn_ready, c.add(xn_ready))
            chain(v.tensor_scalar(BEFORE, TRI[:, :], 0.0, None, ALU.is_ge))
            chain(v.tensor_tensor(BEFORE, BEFORE, IDENT[:, :], ALU.subtract))
            v.wait_ge(turned_full, c.next(turned_full))
            v.wait_ge(turned_taken, c.now(turned_full))
            c.skip(turned_full, KD)

            def b3(ap, k):
                return ap.unsqueeze(2).to_broadcast([P, QT, k])

            LG = QB[:, 0:QT * NR].rearrange("p (t e) -> p t e", t=QT)
            lg, le = LG[:, :, 0:GROUPS], LG[:, :, GROUPS:NR]
            g4 = TA[:, 0:QT * GROUPS].rearrange("p (t e) -> p t e", t=QT)

            def e16(i):
                return TB[:, i * 64:(i + 1) * 64].rearrange("p (t e) -> p t e", t=QT)

            gmax, gsum, gw, first, v1, v2, w1, w2 = (SMALL[:, 4 * i:4 * i + 4] for i in range(4, 12))
            d2 = SMALL[:, 0:4]
            pen = TA[:, 32:48].rearrange("p (t e) -> p t e", t=QT)
            desc = vec("desc", 0, EXPERTS)

            def desc_b(k):
                return desc[:, EXPERTS - k:EXPERTS].unsqueeze(1).to_broadcast([P, QT, k])

            def first_of(hot, eq, k):
                chain(v.tensor_tensor(eq, eq, desc_b(k), ALU.mult))
                chain(v.tensor_reduce(first, eq, AX_X, ALU.max))
                chain(v.tensor_tensor(hot, eq, b3(first, k), ALU.is_equal))

            chain(v.tensor_reduce(gmax, lg, AX_X, ALU.max))
            v.tensor_tensor(g4, lg, b3(gmax, GROUPS), ALU.subtract).then_inc(route_args, c.add(route_args))
            chain(v.tensor_tensor(pen, lg, b3(gmax, GROUPS), ALU.is_equal))
            first_of(pen, pen, GROUPS)
            chain(v.tensor_scalar(pen, pen, -1.0, -NEG, ALU.add, ALU.mult))
            chain(v.tensor_tensor(
                TB[:, 0:64].rearrange("p (t g e) -> p t g e", t=QT, g=GROUPS),
                le.rearrange("p t (g e) -> p t g e", g=GROUPS),
                pen.unsqueeze(3).to_broadcast([P, QT, GROUPS, EXPERTS // GROUPS]), ALU.add))
            for k, (best, hot) in enumerate(((v1, e16(1)), (v2, e16(2)))):
                chain(v.tensor_reduce(best, e16(0), AX_X, ALU.max))
                chain(v.tensor_tensor(hot, e16(0), b3(best, EXPERTS), ALU.is_equal))
                first_of(hot, hot, EXPERTS)
                if k == 0:
                    chain(v.scalar_tensor_tensor(e16(0), hot, 2 * NEG, e16(0), ALU.mult, ALU.add))
            v.tensor_tensor(d2, v2, v1, ALU.subtract).then_inc(route_args, c.add(route_args))
            v.tensor_tensor(e16(3), e16(1), e16(2), ALU.add).then_inc(mask_ready, c.add(mask_ready))
            v.wait_ge(route_done, c.next(route_done, 2))
            chain(v.tensor_reduce(gsum, g4, AX_X, ALU.add))
            chain(v.reciprocal(gw, gsum))
            chain(v.tensor_scalar(w1, d2, 1.0, None, ALU.add))
            chain(v.reciprocal(w1, w1))
            chain(v.tensor_tensor(w1, w1, gw, ALU.mult))
            chain(v.tensor_tensor(w2, w1, d2, ALU.mult))
            chain(v.tensor_tensor(e16(1), e16(1), b3(w1, EXPERTS), ALU.mult))
            chain(v.tensor_tensor(e16(2), e16(2), b3(w2, EXPERTS), ALU.mult))
            rank3, share3 = (ap.rearrange("p (t e) -> p t e", t=QT) for ap in (RANK, SHARE))
            chain(v.tensor_tensor(share3[:, :, 0:EXPERTS], e16(1), e16(2), ALU.add))
            ps = scores_in()
            chain(v.tensor_reduce(gmax[:, 0:1], ps[:, QT * EXPERTS:(QT + 1) * EXPERTS], AX_X, ALU.max))
            step(v.tensor_copy(IOTA, ps[:, P:2 * P]))
            v.scalar_tensor_tensor(rank3[:, :, 0:EXPERTS], ps[:, 0:QT * EXPERTS].rearrange("p (t e) -> p t e", t=QT), 1.0,
                                   e16(3), ALU.add, ALU.mult).then_inc(scores_taken, c.add(scores_taken))
            v.wait_ge(scores_taken, c.now(scores_taken))
            chain(v.tensor_scalar(rank3[:, :, 0:EXPERTS], rank3[:, :, 0:EXPERTS], -1.0, None, ALU.add))
            step(v.tensor_scalar(rank3[:, :, EXPERTS:], rank3[:, :, 0:1], float(-P), None, ALU.add))
            step(v.tensor_copy(share3[:, :, EXPERTS:], share3[:, :, 0:1]))
            chain(v.tensor_scalar(first[:, 0:1], gmax[:, 0:1], float(P), 1.0, ALU.is_gt, ALU.add))
            for k in range(2, QT):
                chain(v.scalar_tensor_tensor(first[:, 0:1], gmax[:, 0:1], float(k * P), first[:, 0:1], ALU.is_gt, ALU.add))
            v.tensor_copy(ROUNDS, first[0:1, 0:1]).then_inc(rounds_ready, c.add(rounds_ready))
            v.wait_ge(rounds_ready, c.now(rounds_ready))
            rounds = v.value_load(ROUNDS, min_val=1, max_val=QT)

            def select(e):
                for t in range(QT):
                    at = e + t * (EXPERTS + 1)
                    rank, share = ((buf[:, at:at + 1] if isinstance(at, int) else buf[:, bass.ds(at, 1)]) for buf in (RANK, SHARE))
                    v.tensor_scalar(tile(SEL, t, P), IOTA, rank, None, ALU.is_equal).then_inc(select_step, c.add(select_step))
                    ins = v.tensor_scalar(tile(WSEL, t, P), IOTA, rank, share, ALU.is_equal, ALU.mult)
                    if t < QT - 1:
                        ins.then_inc(select_step, c.add(select_step))
                ins.then_inc(select_ready, c.add(select_ready))

            select(0)
            c.skip(panel_done, E_SLOTS)
            with c.loop("rounds", rounds):
                with c.loop("experts", EXPERTS) as e:
                    v.wait_ge(gathered, c.next(gathered, 2))
                    v.tensor_copy(XG[:, T:2 * T], SCORE[1][:, :]).then_inc(gathered_taken1, c.add(gathered_taken1))
                    v.wait_ge(select_turned, c.next(select_turned))
                    select(e + 1)
                    c.skip(panel_done, FT_MOE)
                    v.wait_ge(gate_act, c.next(gate_act))
                    for j, ps in enumerate((TURN[1], SCORE[0])):
                        v.wait_ge(panel_done, c.next(panel_done, 2))
                        v.tensor_tensor(tile(HID, j, 2 * P), ps[:, 0:2 * P], tile(GACT, j, 2 * P), ALU.mult).then_inc(
                            hidden_ready, c.add(hidden_ready))
                    c.skip(panel_done, FT_MOE)
                    for d in range(KD):
                        v.wait_ge(scattered, c.next(scattered))
                        v.tensor_tensor(tile(X, d), GEMM[d % 2][:, :], tile(X, d), ALU.add).then_inc(added, c.add(added))
                v.tensor_scalar(RANK, RANK, float(-P), None, ALU.add).then_inc(select_step, c.add(select_step))
                v.wait_ge(select_step, c.now(select_step))
            v.memset(SQ[:, :], 0.0).then_inc(experts_done, c.add(experts_done))
            with c.loop("sq_final", KD) as k:
                v.wait_ge(experts_done, c.now(experts_done))
                chain(v.tensor_tensor(TA[:, :], tile(X, k), tile(X, k), ALU.mult))
                v.tensor_tensor(SQ[:, :], SQ[:, :], TA[:, :], ALU.add).then_inc(sumsq_ready, c.add(sumsq_ready))
                v.wait_ge(sumsq_ready, c.now(sumsq_ready))
            rstd()
            clear_squares()
            with c.loop("final1", KD) as k:
                v.wait_ge(dve_step, c.now(dve_step))
                chain(v.scalar_tensor_tensor(tile(X, k), tile(X, k), VEC[:, bass.ds(k + col["g_final"], 1)],
                                             RS[:, :], ALU.mult, ALU.mult))
                prep(tile(X, k), VEC[:, bass.ds(k + col["gains2"], 1)], tile(XH, k), tile(XL, k))
            with c.loop("layers", LAYERS) as l:
                def gain(s):
                    return lambda e: VEC[:, bass.ds(l * 24 + e + (col["gains2"] + 8 * s), 1)]

                ffn("a", gain(1))
                rstd()
                with c.loop("na", PAIRS) as i:
                    v.wait_ge(dve_step, c.now(dve_step))
                    take(QB[:, :], ATT_SCALE)
                    take(KB[:, :])
                    take(VT[:, :])
                    take(UT)
                    for b in range(2):
                        ps = scores_in()
                        v.tensor_copy(AB[:, b * T:(b + 1) * T], ps[:, :]).then_inc(scores_taken, c.add(scores_taken))
                    for h in range(2):
                        v.wait_ge(bias_in[h], c.next(bias_in[h], 16))
                        t3 = BIAS[h].rearrange("p (e k) -> p e k", k=GRID_W)
                        chain(v.tensor_tensor(t3, t3, COLMASK[:, :].unsqueeze(1).to_broadcast([P, BIAS_ROWS, GRID_W]), ALU.add))
                    v.wait_ge(turned_full, c.next(turned_full, 2))

                    def fourier_out():
                        v.tensor_copy(TA[:, :], den_in()[:, :]).then_inc(den_taken, c.add(den_taken))
                        v.wait_ge(den_taken, c.now(den_taken))
                        halves(tile(AH, i + PAIRS), tile(AL, i + PAIRS), TA[:, :])
                        v.wait_ge(operand_ready, c.now(operand_ready))

                    def bias_of(h, t):
                        at = (BIAS_ROWS // 2 - 1 - 2 * t) * GRID_W
                        return BIAS[h][:, at:at + T]

                    attention(QT, False, bias_of, tile(AH, i), tile(AL, i), {7: fourier_out})
                with c.loop("comb", KD // 2) as d:
                    for j in range(2):
                        e = d * 2 + j
                        take(TA[:, :])
                        take(TB[:, :])
                        for s, buf in ((0, TA), (1, TB)):
                            ps = gemm_in()
                            v.wait_ge(act_out, c.next(act_out))
                            v.tensor_tensor(PROB[s][:, :], ps, buf[:, :], ALU.mult).then_inc(gemm_taken, c.add(gemm_taken))
                        v.wait_ge(gemm_taken, c.now(gemm_taken))
                        chain(v.tensor_tensor(PROB[0][:, :], PROB[0][:, :], PROB[1][:, :], ALU.add))
                        halves(tile(AH, e + KD), tile(AL, e + KD), PROB[0][:, :])
                        v.wait_ge(operand_ready, c.now(operand_ready))
                clear_squares()
                with c.loop("wo", KD // 2) as d:
                    v.wait_ge(dve_step, c.now(dve_step))
                    for j in range(2):
                        e = d * 2 + j
                        add_to(tile(X, e))
                        prep(tile(X, e), gain(2)(e), tile(XH, e), tile(XL, e))
                ffn("b", gain(3))
            rstd()
            with c.loop("last", KD) as k:
                v.wait_ge(dve_step, c.now(dve_step))
                v.scalar_tensor_tensor(tile(X, k), tile(X, k), VEC[:, bass.ds(k + col["last_gain"], 1)],
                                                           RS[:, :], ALU.mult, ALU.mult).then_inc(out_ready, c.add(out_ready))


def panels(w):
    k, n = w.shape
    return w.reshape(k // P, P, n // P, P).transpose(2, 1, 0, 3).reshape(n // P, P, k)


def columns(g):
    return g.reshape(-1, P).T


def feature_major(x):
    t, d = x.shape
    return np.ascontiguousarray(x.T.reshape(d // P, P, t).transpose(1, 0, 2).reshape(P, d // P * t))


def constants():
    f = np.float32
    q, k = np.arange(T)[:, None], np.arange(T)[None]
    far = q - k
    times = ((far >= 0) & (far <= 128)).astype(int) + ((far >= 0) & (far % 4 == 0)) + ((far >= 0) & (far % 16 == 0))
    ln = np.where(times > 0, np.log(np.maximum(times, 1)), NEG).astype(f)
    ln = np.concatenate([ln[i * P:(i + 1) * P, :(i + 1) * P] for i in range(QT)], axis=1)
    rot = np.zeros((P, P), f)
    invf = np.zeros((P, 1), f)
    half = HEAD // 8
    inv = (f(500000.0) ** (-np.arange(0, 2 * half, 2, dtype=f) / f(2 * half))).astype(f)
    for h in range(2):
        for j in range(half):
            lo, hi = h * HEAD + j, h * HEAD + half + j
            rot[hi, lo], rot[lo, hi] = -1, 1
            invf[lo] = invf[hi] = inv[j]
    s, t = np.arange(P)[:, None], np.arange(P)[None]
    tri = np.where(t >= s, 0, NEG).astype(f)
    qc, kc = np.arange(P)[:, None] % GRID_W, np.arange(GRID_W)[None]
    start = np.clip(qc - NA_COLS // 2, 0, GRID_W - NA_COLS)
    colmask = np.where((kc >= start) & (kc < start + NA_COLS), 0, NEG).astype(f)
    ang = 2 * np.pi * (s * t % P) / P
    cs = np.concatenate([np.cos(ang), np.sin(ang)], axis=1).astype(f)
    ang = 2 * np.pi * (q * k % T) / T
    norm = (T * P) ** -0.5
    ct, nst = ((m * norm).astype(f).reshape(QT, P, T).transpose(1, 0, 2).reshape(P, QT * T) for m in (np.cos(ang), -np.sin(ang)))
    return {"ident": np.eye(P, dtype=f), "rot": rot, "tri": tri, "colmask": colmask, "cs": cs, "ln": ln,
            "ct": np.ascontiguousarray(ct), "nst": np.ascontiguousarray(nst)}, invf


def lay_out(x):
    f = np.float32
    arrays, invf = constants()
    vecs, cols, at = [], {}, 0

    def put(name, part):
        nonlocal at
        whole = np.zeros((P, part.shape[1]), f)
        whole[:part.shape[0]] = part
        vecs.append(whole)
        cols[name] = at
        at += part.shape[1]

    for name in ("g_mix", "g_mem", "g_cross", "g_ffn"):
        put(name, columns(x[name][0]))
    put("g_final", columns(x["g_final"]))
    put("gains2", np.concatenate([columns(x[n][l]) for l in range(LAYERS) for n in ("ffn1_norm_2", "mix_norm_2", "ffn2_norm_2")]
                                 + [columns(x["final_norm_2"])], axis=1))
    cols["last_gain"] = cols["gains2"] + 24 * LAYERS
    put("gate_b", np.concatenate([columns(x["mix_gate_bias_2"][l, s]) for l in range(LAYERS) for s in range(2)], axis=1))
    heads = [columns(x["conv_w"][0, j]) for j in range(4)] + [columns(x[n][0]) for n in ("conv_b", "g_mhn", "skip_m", "skip_m")]
    put("mvec", np.stack(heads, axis=2).reshape(P, M_HEADS * 8))
    put("b_i", x["b_i"][0][:, None])
    put("b_f", x["b_f"][0][:, None])
    put("b_route", np.concatenate([x["b_router_g"][0], x["b_router_e"][0]])[:, None])
    put("invf", invf)
    put("desc", np.tile(np.arange(EXPERTS, 0, -1, dtype=f), (P, 1)))
    arrays["vec"] = np.concatenate(vecs, axis=1)

    arrays["xT"] = feature_major(x["x"][0])
    arrays["memT"] = feature_major(x["mem"][0])
    arrays["positions"] = np.ascontiguousarray(x["positions"])

    def padded(*ws):
        w = np.concatenate(ws, axis=1)
        return np.pad(w, ((0, 0), (0, P - w.shape[1])))

    kv = panels(x["w_kv_x"][0])
    w_in = panels(x["w_in"][0][:, :6 * PAIRS * P])
    gates = x["w_in"][0][:, 6 * PAIRS * P:]
    order = [w_in[part * PAIRS + i] for i in range(PAIRS) for part in (3, 4, 0, 1, 2, 5)]
    experts = []
    for e in range(EXPERTS):
        w1, w3 = panels(x["w1"][0, e]), panels(x["w3"][0, e])
        experts += list(w1) + list(w3)
        experts += list(x["w2"][0, e].reshape(FT_MOE, P, D))
    wo = panels(x["w_o_x"][0]).reshape(2, KD // 2, P, 2 * P).transpose(0, 2, 1, 3).reshape(2, P, KD * P)
    first = [kv[0], kv[2], kv[1], kv[3], panels(padded(gates[:, :M_HEADS]))[0], panels(padded(gates[:, M_HEADS:]))[0]]
    first += order + list(panels(x["w_out"][0])) + list(panels(x["w_q_x"][0])) + list(wo)
    first += [panels(padded(x["w_router_g"][0], x["w_router_e"][0]))[0]]
    arrays["experts"] = np.stack(experts)
    arrays["panels1"] = np.stack(first)
    arrays["w_qk_m"] = np.concatenate([x["w_q_m"][0], x["w_k_m"][0]], axis=2)

    up, down, mix, bias = [], [], [], []
    for l in range(LAYERS):
        for which in ("ffn1", "ffn2"):
            wi = panels(x[f"{which}_w_in_2"][l]).reshape(2, 2 * HALF_FT, P, PANEL).transpose(1, 0, 2, 3)
            up.append(wi.reshape(4 * HALF_FT, P, PANEL))
            wo = panels(x[f"{which}_w_out_2"][l]).reshape(KD, P, 2, WIDE).transpose(2, 0, 1, 3)
            down.append(wo.reshape(2 * KD, P, WIDE))
        wi = panels(x["mix_w_in_2"][l])
        mix += [wi[part * PAIRS + i] for i in range(PAIRS) for part in range(4)]
        both = np.concatenate([panels(x["na_w_out_2"][l]), panels(x["f_w_out_2"][l])], axis=2)
        for d in range(KD):
            mix += [wi[16 + d], wi[16 + KD + d], both[d]]
        mix += list(panels(x["mix_w_o_2"][l]))
        rpb = x["na_rpb_2"][l]
        wide = np.pad(rpb, ((0, 0), (0, 0), (GRID_W - NA_COLS, GRID_W - NA_COLS)))
        for h in range(rpb.shape[0]):
            tab = np.empty((2, GRID_W, BIAS_ROWS, GRID_W), f)
            for r in range(2):
                for qc in range(GRID_W):
                    tab[r, qc] = wide[h, 1 - r:1 - r + BIAS_ROWS, GRID_W - 1 - qc:2 * GRID_W - 1 - qc]
            bias.append(tab.reshape(P, BIAS_ROWS * GRID_W))
    arrays["up2"], arrays["down2"] = np.concatenate(up), np.concatenate(down)
    arrays["mix2"], arrays["bias"] = np.stack(mix), np.stack(bias)
    return arrays, cols


def kernel(**inputs):
    import concourse.bacc as bacc
    from concourse.bass_utils import run_bass_kernel_spmd

    arrays, cols = lay_out({k: np.asarray(v) for k, v in inputs.items()})

    def program(trips):
        nc = bacc.Bacc("TRN2", target_bir_lowering=False, num_devices=1)
        a = {n: nc.dram_tensor(n, v.shape, mybir.dt.from_np(v.dtype), kind="ExternalInput").ap() for n, v in arrays.items()}
        a["cols"] = cols
        a["outT"] = nc.dram_tensor("outT", (P, KD * T), F32, kind="ExternalOutput").ap()
        build(nc, a, trips)
        return nc

    trips = {}
    program(trips)
    nc = program(trips)
    r = run_bass_kernel_spmd(nc, [arrays], core_ids=[0])
    out = np.asarray(r.results[0]["outT"]).reshape(P, KD, T).transpose(2, 1, 0).reshape(1, T, D)
    return np.ascontiguousarray(out)
```

```python
from contextlib import ExitStack, contextmanager

import concourse.bass as bass
from concourse import mybir
import numpy as np

F32 = mybir.dt.float32
F32R = mybir.dt.float32r
I32 = mybir.dt.int32
ALU = mybir.AluOpType
ACT = mybir.ActivationFunctionType
AX_X = mybir.AxisListType.X

P = 128
T = 512
D = 1024
KD = D // P
MEM = 256
EPS = 1e-6
LAYERS = 2
HEAD = 64
PAIRS = 4
XPAIRS = 2
QT = T // P
M_HEADS = 4
GROUPS = 4
EXPERTS = 16
FF_MOE = 512
FT_MOE = FF_MOE // P
D_FF = 2816
HALF_FT = D_FF // P // 2
PANEL = KD * P
WIDE = HALF_FT * P
GRID_W = 64
NA_ROWS, NA_COLS = 8, 16
F_GROUPS = 4
ATT_SCALE = HEAD ** -0.5
M_SCALE = P ** -0.5
NEG = -1e30

CAUSAL = [[(j, j * P, P) for j in range(i + 1)] for i in range(QT)]
CROSS = [[(j, j * P, P) for j in range(MEM // P)]] * QT
NA_EDGES = [0, *range(P // 2, T, P), T]
NEAR_BLOCKS = [(j, at, end - at) for j, (at, end) in enumerate(zip(NA_EDGES, NA_EDGES[1:]))]
NEAR = [NEAR_BLOCKS[i:i + 2] for i in range(QT)]
NEAR_TABLES = [sum(n for _, _, n in NEAR[i]) for i in (0, 1, QT - 1)]
NEAR_AT = [0] + [NEAR_TABLES[0]] * (QT - 2) + [NEAR_TABLES[0] + NEAR_TABLES[1]]
BIAS_COLS = sum(NEAR_TABLES)

PI_LOW = 3.1415925
TWO_PI_PARTS = (6.28125, 0.0019340515136718750, float(2 * np.pi - 6.28125 - 0.0019340515136718750))

N_PANELS1 = 2 * XPAIRS + 2 + 6 * PAIRS + KD + XPAIRS + 2 + 1
E_PANELS = 3 * FT_MOE
E_SLOTS = 6
MIX2 = 4 * PAIRS + 3 * KD + KD

SEMS = (
    "consts_in x_in mem_in pos_in raw_in0 raw_in1 heads_in bias_in0 bias_in1 dft_in stored "
    "split_hi split_lo gemm_done gemm_taken scores_full scores_taken turned_full turned_taken "
    "out_full out_taken den_full den_taken operand_ready sumsq_ready ms_ready std_ready "
    "dve_step act_step logits_ready exp_done probs_ready turn_ready qk_ready conv_done conv_ready "
    "sin_ready sin_done gate_ready gate_done rows_ready m_args_ready m_exp_ready "
    "act_out route_args route_done out_ready "
    "xn_ready mask_ready rounds_ready weights_in0 weights_in1 weights_in2 weights_in3 weights_in4 weights_in5 "
    "panel_done select_step select_ready select_turned slots_turned gathered gathered_taken0 gathered_taken1 gate_act hidden_ready half_done "
    "result_ready scattered added experts_done"
).split()


RINGS = ("split_hi", "split_lo", "gemm_done", "gemm_taken", "scores_full", "scores_taken", "turned_full", "turned_taken")


def span(blocks):
    return blocks[0][1], sum(n for _, _, n in blocks)


class Counts:

    def __init__(self, eng, who, trips):
        self.eng, self.who, self.trips = eng, who, trips
        self.n = {name: 0 for name in SEMS}
        self.open = []

    def at(self, sem):
        return self.n[sem.name]

    def add(self, sem, by=1):
        self.n[sem.name] += by
        return by

    def skip(self, sem, by=1):
        self.n[sem.name] += by

    def now(self, sem, off=0):
        value = self.n[sem.name] + off
        assert value > 0, (self.who, sem.name)
        for label, reg in self.open:
            per_trip = self.trips.get((self.who, label, sem.name), 0)
            if per_trip:
                value = reg * per_trip + value
        return value

    def next(self, sem, by=1):
        self.n[sem.name] += by
        return self.now(sem)

    @contextmanager
    def loop(self, label, trips):
        before = dict(self.n)
        with self.eng.Fori(0, trips) as reg:
            self.open.append((label, reg))
            yield reg
            self.open.pop()
        for name, start in before.items():
            per_trip = self.n[name] - start if self.n[name] is not None else 0
            assert per_trip % 2 == 0 or name not in RINGS, (self.who, label, name, per_trip)
            self.trips[self.who, label, name] = per_trip
            if start is None:
                continue
            if isinstance(trips, int):
                self.n[name] = start + trips * per_trip
            elif per_trip:
                self.n[name] = None


def build(nc, a, trips):
    ctx = ExitStack()
    with ctx:
        def sb(name, cols, dt=F32):
            return ctx.enter_context(nc.sbuf_tensor(name, [P, cols], dt))

        def f32(ap):
            return ap.bitcast(F32)

        X = sb("X", KD * T)
        XH = sb("XH", KD * T, F32R)
        XL = sb("XL", KD * T, F32R)
        RAW = [sb(f"RAW{i}", WIDE) for i in range(2)]
        with ExitStack() as products:
            def rounded(name, cols):
                return products.enter_context(nc.sbuf_tensor(name, [P, cols], F32R))

            AH = rounded("AH", 2 * KD * T)
            AL = rounded("AL", 2 * KD * T)
            WH = [rounded(f"WH{i}", WIDE) for i in range(2)]
            WL = [rounded(f"WL{i}", WIDE) for i in range(2)]
        with ExitStack() as experts:
            def plain(name, cols):
                return experts.enter_context(nc.sbuf_tensor(name, [P, cols], F32))[:, :]

            XN = plain("XN", KD * T)
            XT = plain("XT", KD * T)
            SEL, WSEL, SLOTS_T, HID, GACT = (plain(n, T) for n in ("SEL", "WSEL", "SLOTS_T", "HID", "GACT"))
            XG = plain("XG", KD * P)
            Y = plain("Y", D)
            IOTA, BEFORE = plain("IOTA", P), plain("BEFORE", P)
            RANK, SHARE = (plain(n, QT * (EXPERTS + 1)) for n in ("RANK", "SHARE"))
            E_PANEL = [RAW[i][:, 0:PANEL] for i in range(2)] + [plain(f"E_PANEL{i}", PANEL) for i in range(2, E_SLOTS)]
        with ExitStack() as gates:
            GATE_A, GATE_B = ([gates.enter_context(nc.sbuf_tensor(f"{n}{i}", [P, KD * T], F32))[:, :] for i in range(2)][1]
                              for n in ("GATE_A", "GATE_B"))
        ctx.enter_context(nc.sbuf_tensor("KEPT", [P, 4 * KD * T + 4 * WIDE], F32))
        BIG = sb("BIG", 2 * QT * T)
        LN_COLS = P * QT * (QT + 1) // 2
        LN = BIG[:, 0:LN_COLS]
        COS = BIG[:, LN_COLS:LN_COLS + T]
        SIN = BIG[:, LN_COLS + T:LN_COLS + 2 * T]
        GATE = BIG[:, LN_COLS + 2 * T:LN_COLS + 3 * T]
        ENM = BIG[:, LN_COLS + 3 * T:LN_COLS + 4 * T]
        KX = BIG[:, LN_COLS + 4 * T:LN_COLS + 5 * T]
        ROT = BIG[:, LN_COLS + 5 * T:LN_COLS + 5 * T + P]
        TRI = BIG[:, LN_COLS + 5 * T + P:LN_COLS + 5 * T + 2 * P]
        CT = BIG[:, 0:QT * T]
        NST = BIG[:, QT * T:2 * QT * T]
        IDENT = sb("IDENT", P)
        CS = sb("CS", 2 * P)
        ONES = sb("ONES", P)
        VEC = sb("VEC", a["vec"].shape[1])
        SMALL = sb("SMALL", 48)
        QB = sb("QB", T)
        KB = sb("KB", T)
        VB = sb("VB", len(NEAR_BLOCKS) * P)
        VT = sb("VT", T)
        PROB = [sb(f"PROB{i}", T) for i in range(2)]
        PT = sb("PT", QT * T)
        AR = sb("AR", 6 * T)
        C, MV, MQ, MK, SG, VX = (AR[:, i * T:(i + 1) * T] for i in range(6))
        ROUNDS = SMALL[0:1, 12:13].bitcast(I32)
        PADU = sb("PADU", T + 4)
        U = PADU[:, 4:4 + T]
        BIAS = [AR[:, i * BIAS_COLS:(i + 1) * BIAS_COLS] for i in range(2)]
        AB = AR[:, 2 * BIAS_COLS:2 * BIAS_COLS + 2 * T]
        MASK = AR[:, 2 * BIAS_COLS + 2 * T:3 * BIAS_COLS + 2 * T]
        UT = U
        WQK = sb("WQK", 2 * P)
        TA = sb("TA", T)
        TB = sb("TB", T)
        DIAG = [TB[:, i * P:(i + 1) * P] for i in range(2)]
        RS = sb("RS", T)
        SQ = sb("SQ", T)

        def bank(name):
            return ctx.enter_context(nc.psum_tensor(name, [P, T], F32))

        GEMM = [bank(f"GEMM{i}") for i in range(2)]
        SCORE = [bank(f"SCORE{i}") for i in range(2)]
        TURN = [bank(f"TURN{i}") for i in range(2)]
        OUT = bank("OUT")
        DEN = bank("DEN")
        (consts_in, x_in, mem_in, pos_in, raw_in0, raw_in1, heads_in, bias_in0,
         bias_in1, dft_in, stored, split_hi, split_lo, gemm_done, gemm_taken, scores_full,
         scores_taken, turned_full, turned_taken, out_full, out_taken, den_full, den_taken, operand_ready,
         sumsq_ready, ms_ready, std_ready, dve_step, act_step, logits_ready, exp_done, probs_ready,
         turn_ready, qk_ready, conv_done, conv_ready, sin_ready, sin_done, gate_ready, gate_done,
         rows_ready, m_args_ready, m_exp_ready, act_out, route_args, route_done, out_ready, xn_ready,
         mask_ready, rounds_ready, weights_in0, weights_in1, weights_in2, weights_in3, weights_in4, weights_in5,
         panel_done, select_step, select_ready, select_turned, slots_turned, gathered, gathered_taken0, gathered_taken1, gate_act, hidden_ready,
         half_done, result_ready, scattered, added, experts_done) = (
            ctx.enter_context(nc.semaphore(name)) for name in SEMS)
        gathered_taken = (gathered_taken0, gathered_taken1)
        weights_in = (weights_in0, weights_in1, weights_in2, weights_in3, weights_in4, weights_in5)
        raw_in, bias_in = (raw_in0, raw_in1), (bias_in0, bias_in1)
        block = ctx.enter_context(nc.Block())

        col = a["cols"]

        def vec(name, i=0, n=1):
            return VEC[:, col[name] + i:col[name] + i + n]

        def tile(big, d, n=T):
            return big[:, d * n:(d + 1) * n] if isinstance(d, int) else big[:, bass.ds(d * n, n)]

        LN_AT = [P * i * (i + 1) // 2 for i in range(QT)]

        @block.sync
        def _(sp):
            c = Counts(sp, "sp", trips)

            def load(src, width=PANEL):
                slot = c.at(split_lo) % 2
                if c.at(split_lo) > 1:
                    sp.wait_ge(split_lo, c.now(split_lo, -1))
                c.skip(split_lo)
                sp.dma_start(RAW[slot][:, 0:width], src).then_inc(raw_in[slot], c.add(raw_in[slot], 16))

            def panel(table, i, width=PANEL):
                return table[i] if isinstance(i, int) else table[bass.ds(i, 1)].rearrange("o p n -> (o p) n")

            for name, dst in (("vec", VEC), ("ident", IDENT), ("rot", ROT), ("tri", TRI),
                              ("cs", CS), ("ln", LN)):
                sp.dma_start(dst[:, :], a[name]).then_inc(consts_in, c.add(consts_in, 16))
            sp.dma_start(PT[:, 0:KD * MEM], a["memT"]).then_inc(mem_in, c.add(mem_in, 16))
            sp.dma_start(TB[:, :].bitcast(I32), a["positions"].partition_broadcast(P)).then_inc(pos_in, c.add(pos_in, 16))
            load(a["panels1"][0])
            load(a["panels1"][1])
            sp.dma_start(X[:, :], a["xT"]).then_inc(x_in, c.add(x_in, 16))
            base = 2 * XPAIRS + 2
            for i in range(2, base):
                load(a["panels1"][i])
            with c.loop("mix1", PAIRS) as i:
                for j in range(6):
                    load(panel(a["panels1"], i * 6 + (base + j)))
                    if j == 3:
                        sp.wait_ge(conv_done, c.next(conv_done))
                        sp.dma_start(WQK[:, :], panel(a["w_qk_m"], i)).then_inc(heads_in, c.add(heads_in, 16))
            base += 6 * PAIRS
            with c.loop("rest1", (N_PANELS1 - base) // 2) as i:
                load(panel(a["panels1"], i * 2 + base))
                load(panel(a["panels1"], i * 2 + (base + 1)))
            load(a["panels1"][N_PANELS1 - 1])
            sp.wait_ge(rounds_ready, c.next(rounds_ready))
            rounds = sp.value_load(ROUNDS, min_val=1, max_val=QT)
            c.skip(panel_done, E_SLOTS)
            with c.loop("rounds", rounds):
                with c.loop("experts", EXPERTS) as e:
                    for p in range(E_PANELS):
                        sp.wait_ge(panel_done, c.now(panel_done, 1 - E_SLOTS))
                        c.skip(panel_done)
                        at = weights_in[p % E_SLOTS]
                        sp.dma_start(E_PANEL[p % E_SLOTS], panel(a["experts"], e * E_PANELS + p)).then_inc(at, c.add(at, 16))
            sp.wait_ge(experts_done, c.next(experts_done))
            sp.wait_ge(route_args, c.next(route_args))
            sp.dma_start(CT, a["ct"]).then_inc(dft_in, c.add(dft_in, 16))
            sp.dma_start(NST, a["nst"]).then_inc(dft_in, c.add(dft_in, 16))
            sp.dma_start(MASK, a["near"]).then_inc(dft_in, c.add(dft_in, 16))

            def ffn(label, l, which):
                for half in range(2):
                    at = l * 88 + (which * 44 + half * 22)
                    with c.loop(f"up{label}{half}", HALF_FT) as f:
                        load(panel(a["up2"], f * 2 + at))
                        load(panel(a["up2"], f * 2 + (at + 1)))
                    at = l * 32 + (which * 16 + half * 8)
                    with c.loop(f"down{label}{half}", KD // 2) as d:
                        load(panel(a["down2"], d * 2 + at), WIDE)
                        load(panel(a["down2"], d * 2 + (at + 1)), WIDE)

            c.skip(probs_ready, 2 * QT * (PAIRS + XPAIRS))
            with c.loop("layers", LAYERS) as l:
                ffn("a", l, 0)
                with c.loop("na", PAIRS) as i:
                    for j in range(8):
                        load(panel(a["mix2"], i * 8 + (l * MIX2 + j)))
                        if j in (1, 2):
                            sp.wait_ge(probs_ready, c.now(probs_ready))
                            sp.dma_start(
                                BIAS[j - 1], panel(a["bias"], i * 2 + (l * 8 + (j - 1)))).then_inc(bias_in[j - 1], c.add(bias_in[j - 1], 16))
                    c.skip(probs_ready, 2 * QT)
                with c.loop("out", KD) as d:
                    for j in range(2):
                        load(panel(a["mix2"], d * 2 + (l * MIX2 + 8 * PAIRS + j)))
                ffn("b", l, 1)
            sp.wait_ge(out_ready, c.next(out_ready, KD))
            sp.dma_start(a["outT"], X[:, :]).then_inc(stored, c.add(stored, 16))
            sp.wait_ge(stored, c.now(stored))

        @block.gpsimd
        def _(pool):
            c = Counts(pool, "pool", trips)

            def subtract_lo(width=PANEL):
                slot = c.at(split_lo) % 2
                pool.wait_ge(split_hi, c.next(split_hi))
                pool.tensor_tensor(WL[slot][:, 0:width], RAW[slot][:, 0:width],
                                                      f32(WH[slot][:, 0:width]), ALU.subtract).then_inc(split_lo, c.add(split_lo))

            with c.loop("first", N_PANELS1 // 2):
                subtract_lo()
                subtract_lo()
            subtract_lo()
            def ffn(label):
                for half in range(2):
                    with c.loop(f"up{label}{half}", HALF_FT):
                        subtract_lo()
                        subtract_lo()
                    with c.loop(f"down{label}{half}", KD // 2):
                        subtract_lo(WIDE)
                        subtract_lo(WIDE)

            with c.loop("layers", LAYERS):
                ffn("a")
                with c.loop("mix2", MIX2 // 2):
                    subtract_lo()
                    subtract_lo()
                ffn("b")

        @block.tensor
        def _(pe):
            c = Counts(pe, "pe", trips)
            c.skip(out_taken)
            c.skip(den_taken)

            def next_panel():
                slot = c.at(split_lo) % 2
                pe.wait_ge(split_lo, c.next(split_lo))
                return WH[slot], WL[slot]

            def gemm(w, blocks, srcs, n=T):
                wh, wl = w
                ps = GEMM[c.at(gemm_taken) % 2][:, 0:n]
                if c.at(gemm_taken) > 1:
                    pe.wait_ge(gemm_taken, c.now(gemm_taken, -1))
                c.skip(gemm_taken)
                for j, (b, (hi, lo)) in enumerate(zip(blocks, srcs)):
                    whb, wlb = wh[:, b * P:(b + 1) * P], wl[:, b * P:(b + 1) * P]
                    pe.matmul(ps, whb, hi, start=(j == 0), stop=False)
                    pe.matmul(ps, whb, lo, start=False, stop=False)
                    mm = pe.matmul(ps, wlb, hi, start=False, stop=(j == len(blocks) - 1))
                mm.then_inc(gemm_done, c.add(gemm_done))

            def score_bank():
                at = c.at(scores_taken) % 2
                if c.at(scores_taken) > 1:
                    pe.wait_ge(scores_taken, c.now(scores_taken, -1))
                c.skip(scores_taken)
                return SCORE[at]

            def turn_bank():
                at = c.at(turned_taken) % 2
                if c.at(turned_taken) > 1:
                    pe.wait_ge(turned_taken, c.now(turned_taken, -1))
                c.skip(turned_taken)
                return TURN[at]

            x_tiles = [(tile(XH, k), tile(XL, k)) for k in range(KD)]
            a_tiles = [(tile(AH, k), tile(AL, k)) for k in range(2 * KD)]
            mem_tiles = [(tile(AH, k, MEM), tile(AL, k, MEM)) for k in range(KD)]
            eight = range(KD)

            def den_bank():
                pe.wait_ge(den_taken, c.now(den_taken))
                c.skip(den_taken)
                return DEN

            def sum_squares(n=T):
                pe.wait_ge(sumsq_ready, c.next(sumsq_ready, KD))
                ps = den_bank()
                pe.matmul(ps[:, 0:n], ONES[:, :], SQ[:, 0:n], start=True, stop=True).then_inc(den_full, c.add(den_full))

            def turn(src, blocks, rows=P):
                ps = turn_bank()
                for at, j in enumerate(blocks):
                    mm = pe.transpose(ps[:, at * rows:(at + 1) * rows], src[0:rows, j * P:(j + 1) * P],
                                      IDENT[0:rows, 0:rows])
                mm.then_inc(turned_full, c.add(turned_full))

            jobs = [(h, i) for h in range(2) for i in range(QT)]

            def attention(tiles, v, between=None, k_src=KB):
                for u in range(len(jobs) + 3):
                    if u < len(jobs):
                        h, i = jobs[u]
                        part = slice(h * HEAD, (h + 1) * HEAD)
                        first, n = span(tiles[i])
                        pe.matmul(score_bank()[:, 0:n], QB[part, i * P:(i + 1) * P], k_src[part, first:first + n],
                                  start=True, stop=True).then_inc(scores_full, c.add(scores_full))
                    if between and u in between:
                        between[u]()
                    if 2 <= u < len(jobs) + 2:
                        h, i = jobs[u - 2]
                        pe.wait_ge(probs_ready, c.next(probs_ready))
                        ps = turn_bank()
                        first, n = span(tiles[i])
                        for at, (_, key, size) in enumerate(tiles[i]):
                            mm = pe.matmul(ps[0:size, at * P:(at + 1) * P], PROB[u % 2][:, key - first:key - first + size],
                                           DIAG[u % 2], start=True, stop=True)
                        mm.then_inc(turned_full, c.add(turned_full))
                    if u >= 3:
                        pe.wait_ge(turned_taken, c.now(turned_taken, -1 if u < len(jobs) + 2 else 0))
                        values(*jobs[u - 3], tiles, v)
                c.skip(out_taken)

            def values(h, i, tiles, v):
                if h == 0 and i == 0:
                    pe.wait_ge(out_taken, c.now(out_taken))
                out = OUT[h * HEAD:(h + 1) * HEAD, i * P:(i + 1) * P]
                order = sorted(enumerate(tiles[i]), key=lambda block: -block[1][2])
                for n, (at, (place, _, size)) in enumerate(order):
                    mm = pe.matmul(out, v[0:size, place * P + h * HEAD:place * P + (h + 1) * HEAD],
                                   PT[0:size, i * T + at * P:i * T + (at + 1) * P], start=(n == 0), stop=(n == len(order) - 1))
                mm.then_inc(out_full, c.add(out_full))

            def ffn(label):
                for half in range(2):
                    if half == 0:
                        pe.wait_ge(operand_ready, c.next(operand_ready, KD))
                        sum_squares()
                    with c.loop(f"up{label}{half}", HALF_FT):
                        gemm(next_panel(), eight, x_tiles)
                        gemm(next_panel(), eight, x_tiles)
                    c.skip(operand_ready, HALF_FT)
                    with c.loop(f"down{label}{half}", KD // 2):
                        pe.wait_ge(operand_ready, c.now(operand_ready))
                        gemm(next_panel(), range(HALF_FT), a_tiles)
                        gemm(next_panel(), range(HALF_FT), a_tiles)

            def expert():
                pe.wait_ge(select_ready, c.next(select_ready))
                for half in range(2):
                    for k in range(KD // 2):
                        d = half * (KD // 2) + k
                        for t in range(QT):
                            mm = pe.matmul(SCORE[half][:, k * P:(k + 1) * P], XT[:, t * D + d * P:t * D + (d + 1) * P],
                                           tile(SEL, t, P), start=(t == 0), stop=(t == QT - 1))
                    mm.then_inc(gathered, c.add(gathered))
                for t in range(QT):
                    mm = pe.transpose(DEN[:, t * P:(t + 1) * P], tile(WSEL, t, P), IDENT[:, :])
                mm.then_inc(select_turned, c.add(select_turned))
                for p in range(2 * FT_MOE):
                    up, f = divmod(p, FT_MOE)
                    ps = TURN[0][:, f * P:(f + 1) * P] if not up else (TURN[1], SCORE[0])[f // 2][:, f % 2 * P:(f % 2 + 1) * P]
                    at = weights_in[p % E_SLOTS]
                    pe.wait_ge(at, c.next(at, 16))
                    for k in range(KD):
                        if p == 0 and k % (KD // 2) == 0:
                            half = gathered_taken[k // (KD // 2)]
                            pe.wait_ge(half, c.next(half))
                        mm = pe.matmul(ps, tile(E_PANEL[p % E_SLOTS], k, P), tile(XG, k, P),
                                       start=(k == 0), stop=(k == KD - 1))
                    mm.then_inc(panel_done, c.add(panel_done))
                for half, ps in enumerate((OUT, DEN)):
                    for f in range(FT_MOE):
                        slot = (2 * FT_MOE + f) % E_SLOTS
                        if half == 0:
                            if f % 2 == 0:
                                pe.wait_ge(hidden_ready, c.next(hidden_ready))
                            pe.wait_ge(weights_in[slot], c.next(weights_in[slot], 16))
                        mm = pe.matmul(ps[:, :], tile(HID, f, P), tile(E_PANEL[slot], half), start=(f == 0), stop=(f == FT_MOE - 1))
                        if half == 1:
                            mm.then_inc(panel_done, c.add(panel_done))
                        elif f == FT_MOE - 1:
                            mm.then_inc(half_done, c.add(half_done))
                pe.wait_ge(slots_turned, c.next(slots_turned))
                for d in range(KD):
                    if d % (KD // 2) == 0:
                        pe.wait_ge(result_ready, c.next(result_ready))
                    if d >= 2:
                        pe.wait_ge(added, c.next(added))
                    pe.matmul(GEMM[d % 2][:, :], tile(Y, d, P), SLOTS_T, start=True, stop=True).then_inc(
                        scattered, c.add(scattered))
                c.skip(added, 2)

            pe.wait_ge(consts_in, c.next(consts_in, 6 * 16))
            sum_squares(MEM)
            pe.wait_ge(operand_ready, c.next(operand_ready, KD))
            for pair in range(XPAIRS):
                gemm(next_panel(), eight, mem_tiles, MEM)
                gemm(next_panel(), eight, mem_tiles, MEM)
                pe.wait_ge(gemm_taken, c.now(gemm_taken))
                turn(VT, range(MEM // P))
            sum_squares()
            pe.wait_ge(operand_ready, c.next(operand_ready, KD))
            gemm(next_panel(), eight, x_tiles)
            gemm(next_panel(), eight, x_tiles)
            pe.wait_ge(turn_ready, c.next(turn_ready))
            turn(VB, range(QT), M_HEADS)
            with c.loop("mix1", PAIRS):
                gemm(next_panel(), eight, x_tiles)
                gemm(next_panel(), eight, x_tiles)
                gemm(next_panel(), eight, x_tiles)
                pe.wait_ge(gemm_taken, c.now(gemm_taken, -1))
                turn(VT, range(QT))
                gemm(next_panel(), eight, x_tiles)
                pe.wait_ge(gemm_taken, c.now(gemm_taken, -1))
                pe.matmul(score_bank()[:, :], ROT[:, :], QB[:, :], start=True, stop=True).then_inc(scores_full, c.add(scores_full))
                gemm(next_panel(), eight, x_tiles)
                pe.wait_ge(gemm_taken, c.now(gemm_taken, -1))
                pe.matmul(score_bank()[:, :], ROT[:, :], KB[:, :], start=True, stop=True).then_inc(scores_full, c.add(scores_full))
                pe.wait_ge(gemm_taken, c.now(gemm_taken))
                turn(VT, range(QT))
                pe.wait_ge(conv_ready, c.next(conv_ready))
                pe.wait_ge(heads_in, c.next(heads_in, 16))
                for j in range(2):
                    pe.matmul(score_bank()[:, :], WQK[:, j * P:(j + 1) * P], C,
                                                    start=True, stop=True).then_inc(scores_full, c.add(scores_full))
                pe.wait_ge(qk_ready, c.next(qk_ready))
                attention(CAUSAL, VB, {2: lambda: gemm(next_panel(), eight, x_tiles)})
                for at in (0, 32):
                    pe.wait_ge(rows_ready, c.next(rows_ready))
                    pe.matmul(score_bank()[:, :], ONES[at:at + M_HEADS, :],
                                                    TB[at:at + M_HEADS, :], start=True, stop=True).then_inc(scores_full, c.add(scores_full))
                pe.wait_ge(scores_taken, c.now(scores_taken))
                for j in range(QT):
                    pe.matmul(score_bank()[:, j * P:T], MK[:, j * P:(j + 1) * P],
                                                    MQ[:, j * P:T], start=True, stop=True).then_inc(scores_full, c.add(scores_full))
                pe.wait_ge(out_taken, c.now(out_taken))
                c.skip(out_taken)
                den_bank()
                for j in range(QT):
                    pe.wait_ge(scores_taken, c.now(scores_taken, j + 1 - QT))
                    w = PT[:, j * T + j * P:(j + 1) * T]
                    num = pe.matmul(OUT[:, j * P:T], MV[:, j * P:(j + 1) * P], w, start=(j == 0), stop=(j == QT - 1))
                    den = pe.matmul(DEN[:, j * P:T], ONES[:, :], w, start=(j == 0), stop=(j == QT - 1))
                num.then_inc(out_full, c.add(out_full))
                den.then_inc(den_full, c.add(den_full))
                pe.wait_ge(sumsq_ready, c.next(sumsq_ready))
                pe.matmul(den_bank()[:, :], ONES[:, :], TB[:, :], start=True, stop=True).then_inc(den_full, c.add(den_full))
                c.skip(operand_ready)
            pe.wait_ge(operand_ready, c.now(operand_ready))
            pe.wait_ge(out_taken, c.now(out_taken))
            with c.loop("wout", KD // 2):
                gemm(next_panel(), eight, a_tiles)
                gemm(next_panel(), eight, a_tiles)
            sum_squares()
            pe.wait_ge(operand_ready, c.next(operand_ready, KD))
            for pair in range(XPAIRS):
                gemm(next_panel(), eight, x_tiles)
                pe.wait_ge(gemm_taken, c.now(gemm_taken))
                attention(CROSS, VX[:, pair * MEM:(pair + 1) * MEM],
                          k_src=KX[:, pair * MEM:(pair + 1) * MEM])
            pe.wait_ge(out_taken, c.now(out_taken))
            for half in range(2):
                w = next_panel()
                for d in range(KD // 2):
                    gemm(w, (2 * d, 2 * d + 1), a_tiles)
            sum_squares()
            pe.wait_ge(operand_ready, c.next(operand_ready, KD))
            gemm(next_panel(), eight, x_tiles)
            pe.wait_ge(turn_ready, c.next(turn_ready))
            turn(TA, range(QT), GROUPS + EXPERTS)
            for d in range(KD):
                pe.wait_ge(xn_ready, c.next(xn_ready))
                turn(tile(XN, d), range(QT))
            pe.wait_ge(mask_ready, c.next(mask_ready))
            ps = score_bank()
            mask = [TB[:, 192 + t * EXPERTS:192 + (t + 1) * EXPERTS] for t in range(QT)]
            for t in range(QT):
                rank = ps[:, t * EXPERTS:(t + 1) * EXPERTS]
                for s in range(t):
                    pe.matmul(rank, ONES[:, :], mask[s], start=(s == 0), stop=False)
                mm = pe.matmul(rank, BEFORE, mask[t], start=(t == 0), stop=True)
                if t == 0:
                    mm.then_inc(panel_done, c.add(panel_done, E_SLOTS))
            for t in range(QT):
                pe.matmul(ps[:, QT * EXPERTS:(QT + 1) * EXPERTS], ONES[:, :], mask[t], start=(t == 0), stop=(t == QT - 1))
            pe.matmul(ps[:, P:2 * P], ONES[:, :], BEFORE, start=True, stop=True).then_inc(scores_full, c.add(scores_full))
            pe.wait_ge(turned_taken, c.now(turned_taken))
            pe.wait_ge(rounds_ready, c.next(rounds_ready))
            rounds = pe.value_load(ROUNDS, min_val=1, max_val=QT)
            with c.loop("rounds", rounds):
                with c.loop("experts", EXPERTS):
                    expert()
            sum_squares()
            pe.wait_ge(dft_in, c.next(dft_in, 3 * 16))
            with c.loop("layers", LAYERS):
                ffn("a")
                pe.wait_ge(operand_ready, c.next(operand_ready, KD))
                sum_squares()
                with c.loop("na", PAIRS):
                    gemm(next_panel(), eight, x_tiles)
                    gemm(next_panel(), eight, x_tiles)
                    gemm(next_panel(), eight, x_tiles)
                    pe.wait_ge(gemm_taken, c.now(gemm_taken))
                    for part in (NEAR_BLOCKS[1::-1], NEAR_BLOCKS[2:]):
                        ps = turn_bank()
                        for place, key, size in part:
                            at = (place - min(part)[0]) * P
                            mm = pe.transpose(ps[0:size, at:at + P], VT[:, key:key + size], IDENT[:, :])
                        mm.then_inc(turned_full, c.add(turned_full))
                    gemm(next_panel(), eight, x_tiles)
                    pe.wait_ge(gemm_taken, c.now(gemm_taken))
                    for b in range(2):
                        ps = score_bank()
                        for t in range(2):
                            mm = pe.matmul(ps[:, t * 2 * P:(t + 1) * 2 * P],
                                           UT[:, (2 * b + t) * P:(2 * b + t + 1) * P], CS[:, :],
                                           start=True, stop=True)
                        mm.then_inc(scores_full, c.add(scores_full))

                    def dft():
                        pe.wait_ge(scores_taken, c.now(scores_taken, -3))
                        den_bank()
                        for t in range(QT):
                            pe.matmul(DEN[:, :], AB[:, t * 2 * P:t * 2 * P + P], tile(CT, t),
                                      start=(t == 0), stop=False)
                            mm = pe.matmul(DEN[:, :], AB[:, t * 2 * P + P:(t + 1) * 2 * P], tile(NST, t),
                                           start=False, stop=(t == QT - 1))
                        mm.then_inc(den_full, c.add(den_full))

                    def gate():
                        gemm(next_panel(), eight, x_tiles)

                    attention(NEAR, VB, {1: gate, 2: dft, 4: gate, 6: gate, 8: gate})
                    c.skip(operand_ready)
                branches = c.now(operand_ready)
                with c.loop("comb", KD // 2):
                    pe.wait_ge(out_taken, c.now(out_taken))
                    pe.wait_ge(operand_ready, branches)
                    for d in range(2):
                        w = next_panel()
                        gemm(w, range(0, PAIRS), a_tiles[0:PAIRS])
                        gemm(w, range(PAIRS, 2 * PAIRS), a_tiles[PAIRS:KD])
                    c.skip(operand_ready, 2)
                with c.loop("wo", KD // 2):
                    pe.wait_ge(operand_ready, c.now(operand_ready))
                    gemm(next_panel(), eight, a_tiles[KD:])
                    gemm(next_panel(), eight, a_tiles[KD:])
                ffn("b")
            c.skip(operand_ready, KD)
            sum_squares()

        @block.scalar
        def _(act):
            c = Counts(act, "act", trips)
            c.skip(out_full)

            results = [1]

            def round_hi(width=PANEL, units=1):
                slot = c.at(split_hi) % 2
                act.wait_ge(raw_in[slot], c.next(raw_in[slot], 16))
                if c.at(gemm_done) > results[0]:
                    act.wait_ge(gemm_done, c.now(gemm_done, -results[0]))
                c.skip(gemm_done, units)
                results[0] = units
                act.copy(WH[slot][:, 0:width], RAW[slot][:, 0:width]).then_inc(split_hi, c.add(split_hi))

            def root(n=T):
                act.wait_ge(ms_ready, c.next(ms_ready))
                act.activation(RS[:, 0:n], RS[:, 0:n], ACT.Sqrt).then_inc(std_ready, c.add(std_ready))

            def turned(dst, src_cols, rows=P):
                at = c.at(turned_full) % 2
                act.wait_ge(turned_full, c.next(turned_full))
                act.copy(dst, TURN[at][0:rows, src_cols]).then_inc(turned_taken, c.add(turned_taken))

            jobs = [(h, i) for h in range(2) for i in range(QT)]

            def attention(tiles, between=None):
                for u in range(len(jobs) + 2):
                    if u >= 2:
                        h, i = jobs[u - 2]
                        n = len(tiles[i]) * P
                        act.wait_ge(out_full, c.now(out_full))
                        if u >= len(jobs) // 2 + 1:
                            c.skip(out_full)
                        turned(PT[:, i * T:i * T + n], slice(0, n))
                    if u < len(jobs):
                        h, i = jobs[u]
                        act.wait_ge(logits_ready, c.next(logits_ready))
                        p = PROB[u % 2][:, 0:span(tiles[i])[1]]
                        act.activation(p, p, ACT.Exp, bias=SMALL[:, u % 2:u % 2 + 1],
                                       accum_out=SMALL[:, 2 + u % 2:3 + u % 2]).then_inc(exp_done, c.add(exp_done))
                    if between and u in between:
                        between[u]()
                c.skip(out_full, len(jobs) // 2 - 1)

            def table(func):
                act.activation(SMALL[:, 13:14], SMALL[:, 13:14], func)

            def silu_unit():
                act.wait_ge(gemm_taken, c.now(gemm_done, -1))
                act.activation(TB[:, :], TA[:, :], ACT.Silu).then_inc(act_out, c.add(act_out))

            def sigmoid_unit(dst, src, off, **bias):
                act.wait_ge(gemm_taken, c.now(gemm_done, off))
                act.activation(dst, src, ACT.Sigmoid, **bias).then_inc(act_out, c.add(act_out))

            def ffn(label):
                for half in range(2):
                    if half == 0:
                        root()
                        table(ACT.Silu)
                    with c.loop(f"up{label}{half}", HALF_FT):
                        round_hi()
                        round_hi()
                        silu_unit()
                    with c.loop(f"down{label}{half}", KD // 2):
                        round_hi(WIDE)
                        round_hi(WIDE)

            act.wait_ge(sin_ready, c.next(sin_ready))
            act.activation(SIN, SIN, ACT.Sin).then_inc(sin_done, c.add(sin_done))
            act.wait_ge(sin_ready, c.next(sin_ready))
            act.activation(COS, COS, ACT.Sin).then_inc(sin_done, c.add(sin_done))
            round_hi()
            round_hi()
            root(MEM)
            for pair in range(XPAIRS):
                if pair:
                    round_hi()
                    round_hi()
                turned(VX[:, pair * MEM:(pair + 1) * MEM], slice(0, MEM))
            round_hi()
            round_hi()
            root()
            act.wait_ge(gate_ready, c.next(gate_ready))
            act.activation(TB[0:M_HEADS, :], TB[0:M_HEADS, :], ACT.Exp).then_inc(gate_done, c.add(gate_done))
            act.wait_ge(gate_ready, c.next(gate_ready))
            act.activation(TB[0:M_HEADS, :], TB[0:M_HEADS, :], ACT.Ln).then_inc(gate_done, c.add(gate_done))
            act.wait_ge(gate_ready, c.next(gate_ready))
            act.activation(GATE[32:32 + M_HEADS, :], GATE[32:32 + M_HEADS, :], ACT.Exp, scale=-1.0).then_inc(gate_done, c.add(gate_done))
            turned(SMALL[:, 16:16 + QT * M_HEADS], slice(0, QT * M_HEADS))
            round_hi()
            round_hi()
            with c.loop("mix1", PAIRS) as m:
                round_hi()
                round_hi()
                turned(MV, slice(0, T))
                act.wait_ge(conv_done, c.next(conv_done))
                act.activation(SG, C, ACT.Sigmoid).then_inc(act_out, c.add(act_out))
                round_hi()
                round_hi()
                turned(VB[:, 0:T], slice(0, T))
                attention(CAUSAL, {3: round_hi, 5: round_hi, 6: lambda: sigmoid_unit(SG, TA[:, :], -2)})
                act.wait_ge(out_full, c.now(out_full))
                for j in range(QT):
                    bias = SMALL[:, bass.ds(m + (16 + j * M_HEADS), 1)]
                    if j == 0:
                        act.wait_ge(m_args_ready, c.next(m_args_ready))
                    ins = act.activation(PT[:, j * T + j * P:j * T + (j + 1) * P], VT[:, j * P:(j + 1) * P], ACT.Exp, bias=bias)
                    if j < QT - 1:
                        ins.then_inc(act_step, c.add(act_step))
                        ins = act.activation(PT[:, j * T + (j + 1) * P:(j + 1) * T], U[:, (j + 1) * P:T], ACT.Exp, bias=bias)
                    ins.then_inc(m_exp_ready, c.add(m_exp_ready))
                c.skip(out_full)
                act.wait_ge(ms_ready, c.next(ms_ready))
                act.activation(TB[:, :], TB[:, :], ACT.Sqrt).then_inc(std_ready, c.add(std_ready))
            with c.loop("wout", KD // 2 - 1):
                round_hi()
                round_hi()
            round_hi()
            root()
            for pair in range(XPAIRS):
                if pair == 0:
                    round_hi()
                attention(CROSS)
            for half in range(2):
                round_hi(units=KD // 2)
            round_hi()
            root()
            turned(QB[:, 0:QT * (GROUPS + EXPERTS)], slice(0, QT * (GROUPS + EXPERTS)))
            c.skip(panel_done, E_SLOTS)
            for d in range(KD):
                at = c.at(turned_full) % 2
                act.wait_ge(turned_full, c.next(turned_full))
                act.copy(XT.rearrange("p (t f) -> p t f", t=QT)[:, :, d * P:(d + 1) * P],
                         TURN[at][:, :].rearrange("p (t f) -> p t f", t=QT)).then_inc(turned_taken, c.add(turned_taken))
            for k in range(2):
                act.wait_ge(route_args, c.next(route_args))
                ap = SMALL[:, 0:QT] if k else TA[:, 0:QT * GROUPS]
                act.activation(ap, ap, ACT.Exp).then_inc(route_done, c.add(route_done))
            act.wait_ge(rounds_ready, c.next(rounds_ready))
            rounds = act.value_load(ROUNDS, min_val=1, max_val=QT)
            table(ACT.Silu)
            with c.loop("rounds", rounds):
                with c.loop("experts", EXPERTS):
                    act.wait_ge(gathered, c.next(gathered))
                    act.copy(XG[:, 0:T], SCORE[0][:, :]).then_inc(gathered_taken0, c.add(gathered_taken0))
                    c.skip(gathered)
                    act.wait_ge(select_turned, c.next(select_turned))
                    act.copy(SLOTS_T, DEN[:, :]).then_inc(slots_turned, c.add(slots_turned))
                    act.wait_ge(panel_done, c.next(panel_done, FT_MOE))
                    act.activation(GACT, TURN[0][:, :], ACT.Silu).then_inc(gate_act, c.add(gate_act))
                    c.skip(panel_done, 2 * FT_MOE)
                    act.wait_ge(half_done, c.next(half_done))
                    act.copy(Y[:, 0:T], OUT[:, :]).then_inc(result_ready, c.add(result_ready))
                    act.wait_ge(panel_done, c.now(panel_done))
                    act.copy(Y[:, T:2 * T], DEN[:, :]).then_inc(result_ready, c.add(result_ready))
            root()
            with c.loop("layers", LAYERS) as l:
                ffn("a")
                root()
                round_hi()
                round_hi()
                table(ACT.Exp)
                with c.loop("na", PAIRS):
                    round_hi()
                    round_hi()
                    turned(VB[:, 0:2 * P], slice(0, 2 * P))
                    turned(VB[:, 2 * P:], slice(0, 3 * P))
                    round_hi()
                    round_hi()
                    attention(NEAR, {2: round_hi, 5: round_hi, 7: round_hi, 8: round_hi})
                act.wait_ge(gemm_taken, c.now(gemm_done, -2))
                c.skip(gemm_done, 2)
                results[0] = 2
                table(ACT.Sigmoid)
                with c.loop("comb", KD // 2) as d:
                    def gate_bias(s, j):
                        return VEC[:, bass.ds(l * 16 + (d * 2) + (col["gate_b"] + 8 * s + j), 1)]

                    for j in range(2):
                        for g, gates in enumerate((GATE_A, GATE_B)):
                            gate = tile(gates, d * 2 + j)
                            act.activation(gate, gate, ACT.Sigmoid, bias=gate_bias(g, j)).then_inc(act_out, c.add(act_out))
                        round_hi(units=2)
                c.skip(gemm_done, -2)
                results[0] = 1
                with c.loop("wo", KD // 2 - 1):
                    round_hi()
                    round_hi()
                ffn("b")
            root()

        @block.vector
        def _(v):
            c = Counts(v, "dve", trips)

            def step(ins):
                ins.then_inc(dve_step, c.add(dve_step))

            def chain(ins):
                ins.then_inc(dve_step, c.add(dve_step))
                v.wait_ge(dve_step, c.now(dve_step))

            def prep(x, gain, hi, lo, n=T):
                step(v.tensor_tensor(TA[:, 0:n], x, x, ALU.mult))
                chain(v.tensor_scalar(hi, x, gain, None, ALU.mult))
                v.scalar_tensor_tensor(lo, x, gain, f32(hi), ALU.mult, ALU.subtract).then_inc(operand_ready, c.add(operand_ready))
                v.tensor_tensor(SQ[:, 0:n], SQ[:, 0:n], TA[:, 0:n], ALU.add).then_inc(sumsq_ready, c.add(sumsq_ready))
                v.wait_ge(sumsq_ready, c.now(sumsq_ready))

            def clear_squares():
                step(v.memset(SQ[:, :], 0.0))

            def scores_in():
                at = c.at(scores_full) % 2
                v.wait_ge(scores_full, c.next(scores_full))
                return SCORE[at]

            def den_in():
                v.wait_ge(den_full, c.next(den_full))
                return DEN

            def rstd(n=T):
                ps = den_in()
                v.tensor_scalar(RS[:, 0:n], ps[:, 0:n], 1.0 / D, None, ALU.mult).then_inc(den_taken, c.add(den_taken))
                v.wait_ge(den_taken, c.now(den_taken))
                v.tensor_scalar(RS[:, 0:n], RS[:, 0:n], EPS, None, ALU.add).then_inc(ms_ready, c.add(ms_ready))
                v.wait_ge(std_ready, c.next(std_ready))
                step(v.reciprocal(RS[:, 0:n], RS[:, 0:n]))

            def gemm_in(n=T):
                at = c.at(gemm_done) % 2
                v.wait_ge(gemm_done, c.next(gemm_done))
                return GEMM[at][:, 0:n]

            def take(dst, scale=1.0, by=None, n=T):
                ps = gemm_in(n)
                by = RS[:, 0:n] if by is None else by
                v.scalar_tensor_tensor(dst, ps, scale, by, ALU.mult, ALU.mult).then_inc(gemm_taken, c.add(gemm_taken))

            def add_to(x, scale=1.0):
                ps = gemm_in()
                v.scalar_tensor_tensor(x, ps, scale, x, ALU.mult, ALU.add).then_inc(gemm_taken, c.add(gemm_taken))
                v.wait_ge(gemm_taken, c.now(gemm_taken))

            def halves(hi, lo, src):
                chain(v.tensor_copy(hi, src))
                v.tensor_tensor(lo, src, f32(hi), ALU.subtract).then_inc(operand_ready, c.add(operand_ready))

            jobs = [(h, i) for h in range(2) for i in range(QT)]

            def attention(tiles, bias, hi, lo, between=None):
                for u in range(len(jobs) + 1):
                    if u < len(jobs):
                        h, i = jobs[u]
                        n = span(tiles[i])[1]
                        prob = PROB[u % 2][:, 0:n]
                        if u >= 2:
                            v.wait_ge(turned_full, c.next(turned_full))
                        ps = scores_in()[:, 0:n]
                        if bias is None:
                            v.tensor_copy(prob, ps).then_inc(scores_taken, c.add(scores_taken))
                        else:
                            v.tensor_tensor(prob, ps, bias(h, i), ALU.add).then_inc(scores_taken, c.add(scores_taken))
                        v.wait_ge(scores_taken, c.now(scores_taken))
                        v.tensor_reduce(SMALL[:, u % 2:u % 2 + 1], prob, AX_X, ALU.max, negate=True).then_inc(
                            logits_ready, c.add(logits_ready))
                    if u >= 1:
                        s = (u - 1) % 2
                        v.wait_ge(exp_done, c.next(exp_done))
                        chain(v.reciprocal(SMALL[:, 4 + s:5 + s], SMALL[:, 2 + s:3 + s]))
                        v.tensor_scalar(DIAG[s], IDENT[:, :], SMALL[:, 4 + s:5 + s], None, ALU.mult).then_inc(
                            probs_ready, c.add(probs_ready))
                    if between and u in between:
                        between[u]()
                v.wait_ge(turned_full, c.next(turned_full, 2))
                v.wait_ge(out_full, c.next(out_full, len(jobs)))
                chain(v.tensor_copy(hi, OUT[:, :]))
                v.tensor_tensor(lo, OUT[:, :], f32(hi), ALU.subtract).then_inc(out_taken, c.add(out_taken))

            def ffn(label, gain):
                rstd()
                for half in range(2):
                    with c.loop(f"up{label}{half}", HALF_FT) as f:
                        v.wait_ge(dve_step, c.now(dve_step))
                        v.wait_ge(gemm_taken, c.now(gemm_taken))
                        hidden_unit(tile(AH, f), tile(AL, f), RS[:, :])
                    if half == 0:
                        with c.loop(f"down{label}{half}", KD // 2) as d:
                            add_to(tile(X, d * 2), 0.5)
                            add_to(tile(X, d * 2 + 1), 0.5)
                    else:
                        clear_squares()
                        with c.loop(f"down{label}{half}", KD // 2) as d:
                            v.wait_ge(dve_step, c.now(dve_step))
                            for j in range(2):
                                e = d * 2 + j
                                add_to(tile(X, e), 0.5)
                                prep(tile(X, e), gain(e), tile(XH, e), tile(XL, e))

            def hidden_unit(hi, lo, by):
                take(TA[:, :])
                take(PROB[0][:, :], by=by)
                v.wait_ge(act_out, c.next(act_out))
                v.wait_ge(gemm_taken, c.now(gemm_taken))
                chain(v.tensor_tensor(PROB[0][:, :], PROB[0][:, :], TB[:, :], ALU.mult))
                halves(hi, lo, PROB[0][:, :])
                v.wait_ge(operand_ready, c.now(operand_ready))

            v.memset(ONES[:, :], 1.0).then_inc(out_taken, c.add(out_taken))
            v.memset(PADU[:, 0:4], 0.0).then_inc(den_taken, c.add(den_taken))
            v.memset(SMALL[:, :], 0.0).then_inc(out_full, c.add(out_full))
            clear_squares()
            v.wait_ge(dve_step, c.now(dve_step))
            v.wait_ge(mem_in, c.next(mem_in, 16))
            v.wait_ge(consts_in, c.next(consts_in, 6 * 16))
            for k in range(KD):
                prep(tile(PT, k, MEM), vec("g_mem", k), tile(AH, k, MEM), tile(AL, k, MEM), MEM)
            v.wait_ge(pos_in, c.next(pos_in, 16))
            chain(v.tensor_copy(VB[:, 0:T], TB[:, :].bitcast(I32)))
            chain(v.tensor_scalar(VB[:, 0:T], VB[:, 0:T], vec("invf"), None, ALU.mult))
            chain(v.tensor_scalar(TB[:, :], VB[:, 0:T], float(np.float32(1 / (2 * np.pi))), None, ALU.mult))
            chain(v.tensor_scalar(TB[:, :], TB[:, :], 12582912.0, None, ALU.add))
            chain(v.tensor_scalar(TB[:, :], TB[:, :], -12582912.0, None, ALU.add))
            for part in TWO_PI_PARTS:
                chain(v.scalar_tensor_tensor(VB[:, 0:T], TB[:, :], -part, VB[:, 0:T], ALU.mult, ALU.add))
            v.tensor_scalar(SIN, VB[:, 0:T], PI_LOW, -PI_LOW, ALU.min, ALU.max).then_inc(sin_ready, c.add(sin_ready))
            chain(v.tensor_scalar(VB[:, 0:T], VB[:, 0:T], float(np.pi / 2), None, ALU.add))
            chain(v.tensor_scalar(TB[:, :], VB[:, 0:T], float(np.pi), float(-2 * np.pi), ALU.is_gt, ALU.mult))
            chain(v.tensor_tensor(VB[:, 0:T], VB[:, 0:T], TB[:, :], ALU.add))
            v.tensor_scalar(COS, VB[:, 0:T], PI_LOW, -PI_LOW, ALU.min, ALU.max).then_inc(sin_ready, c.add(sin_ready))
            rstd(MEM)
            v.wait_ge(dve_step, c.now(dve_step))
            for pair in range(XPAIRS):
                take(KX[:, pair * MEM:(pair + 1) * MEM], n=MEM)
                if pair:
                    v.wait_ge(turned_full, c.next(turned_full))
                take(VT[:, 0:MEM], n=MEM)
            v.wait_ge(gemm_taken, c.now(gemm_taken))
            clear_squares()
            v.wait_ge(x_in, c.next(x_in, 16))
            with c.loop("prep_x", KD) as k:
                v.wait_ge(dve_step, c.now(dve_step))
                prep(tile(X, k), VEC[:, bass.ds(k + col["g_mix"], 1)], tile(XH, k), tile(XL, k))
            rstd()
            v.wait_ge(dve_step, c.now(dve_step))
            H4 = slice(0, M_HEADS)
            ig, fg, mn, one = VB[H4, 0:T], PROB[0][H4, :], PROB[1][H4, :], KB[H4, :]
            for dst, b in ((ig, "b_i"), (fg, "b_f")):
                ps = gemm_in()
                v.tensor_tensor(dst, ps[H4, :], RS[H4, :], ALU.mult).then_inc(gemm_taken, c.add(gemm_taken))
                v.wait_ge(gemm_taken, c.now(gemm_taken))
                chain(v.tensor_scalar(dst, dst, vec(b)[H4, :], None, ALU.add))
            step(v.memset(one, 0.0))
            chain(v.tensor_scalar(mn, fg, 0.0, None, ALU.min))
            v.scalar_tensor_tensor(TB[H4, :], mn, 2.0, fg, ALU.mult, ALU.subtract).then_inc(gate_ready, c.add(gate_ready))
            v.wait_ge(gate_done, c.next(gate_done))
            v.tensor_scalar(TB[H4, :], TB[H4, :], 1.0, None, ALU.add).then_inc(gate_ready, c.add(gate_ready))
            v.wait_ge(gate_done, c.next(gate_done))
            chain(v.tensor_tensor(fg, mn, TB[H4, :], ALU.subtract))
            chain(v.tensor_tensor_scan(mn, fg, one, 0.0, ALU.add, ALU.add))
            v.tensor_tensor(ig, ig, mn, ALU.subtract).then_inc(turn_ready, c.add(turn_ready))
            v.wait_ge(turn_ready, c.now(turn_ready))
            chain(v.tensor_tensor_scan(fg, ig, ig, 0.0, ALU.max, ALU.max))
            chain(v.tensor_scalar(GATE[H4, :], fg, -1.0, None, ALU.mult))
            chain(v.tensor_tensor(mn, mn, fg, ALU.add))
            v.tensor_copy(GATE[32:32 + M_HEADS, :], mn).then_inc(gate_ready, c.add(gate_ready))
            v.wait_ge(gate_done, c.next(gate_done))
            v.wait_ge(turned_full, c.next(turned_full, 2))
            v.wait_ge(sin_done, c.next(sin_done, 2))
            with c.loop("mix1", PAIRS) as m:
                def mv(name, j):
                    return VEC[:, bass.ds(m * 8 + (col["mvec"] + j), 1)]

                take(PADU[:, 4:4 + T])
                v.wait_ge(gemm_taken, c.now(gemm_taken))
                chain(v.tensor_scalar(C, PADU[:, 1:1 + T], mv("w", 0), mv("b", 4), ALU.mult, ALU.add))
                for j in range(1, 3):
                    chain(v.scalar_tensor_tensor(C, PADU[:, 1 + j:1 + j + T], mv("w", j), C, ALU.mult, ALU.add))
                v.scalar_tensor_tensor(C, PADU[:, 4:4 + T], mv("w", 3), C, ALU.mult, ALU.add).then_inc(conv_done, c.add(conv_done))
                take(VT[:, :])
                take(QB[:, :], ATT_SCALE)
                v.wait_ge(act_out, c.next(act_out))
                v.tensor_tensor(C, C, SG, ALU.mult).then_inc(conv_ready, c.add(conv_ready))
                take(KB[:, :])
                v.wait_ge(turned_full, c.next(turned_full))
                take(VT[:, :])
                v.wait_ge(gemm_taken, c.now(gemm_taken))
                for j, buf in enumerate((QB, KB)):
                    ps = scores_in()
                    v.tensor_tensor(TA[:, :], ps[:, :], SIN, ALU.mult).then_inc(scores_taken, c.add(scores_taken))
                    chain(v.tensor_tensor(buf[:, :], buf[:, :], COS, ALU.mult))
                    if j == 0:
                        chain(v.tensor_tensor(buf[:, :], buf[:, :], TA[:, :], ALU.add))
                    else:
                        v.tensor_tensor(buf[:, :], buf[:, :], TA[:, :], ALU.add).then_inc(qk_ready, c.add(qk_ready))
                for dst, scale in ((MQ, 1.0), (MK, M_SCALE)):
                    ps = scores_in()
                    v.tensor_scalar(dst, ps[:, :], scale, None, ALU.mult).then_inc(scores_taken, c.add(scores_taken))
                v.wait_ge(scores_taken, c.now(scores_taken))
                v.wait_ge(turned_full, c.next(turned_full))

                attention(CAUSAL, lambda h, i: LN[:, LN_AT[i]:LN_AT[i] + (i + 1) * P],
                          tile(AH, m), tile(AL, m), {4: lambda: take(TA[:, :])})
                v.wait_ge(act_out, c.next(act_out))
                for dst, at in ((U, 0), (ENM, 32)):
                    rows = slice(at, at + M_HEADS)
                    v.tensor_scalar(TB[rows, :], GATE[rows, :], IDENT[rows, bass.ds(m + at, 1)], None, ALU.mult).then_inc(rows_ready, c.add(rows_ready))
                    ps = scores_in()
                    v.tensor_copy(dst, ps[:, :]).then_inc(scores_taken, c.add(scores_taken))
                v.wait_ge(scores_taken, c.now(scores_taken))
                v.tensor_tensor(
                    VT[:, :].rearrange("p (j t) -> p j t", j=QT), U.rearrange("p (j t) -> p j t", j=QT),
                    TRI[:, :].unsqueeze(1).to_broadcast([P, QT, P]), ALU.add).then_inc(m_args_ready, c.add(m_args_ready))
                for j in range(QT):
                    ps = scores_in()
                    v.wait_ge(m_exp_ready, c.next(m_exp_ready))
                    w = PT[:, j * T + j * P:(j + 1) * T]
                    v.tensor_tensor(w, ps[:, j * P:T], w, ALU.mult).then_inc(scores_taken, c.add(scores_taken))
                v.wait_ge(out_full, c.next(out_full))
                v.wait_ge(den_full, c.next(den_full))
                chain(v.tensor_scalar(TA[:, :], DEN[:, :], -1.0, None, ALU.mult))
                v.tensor_tensor(TA[:, :], DEN[:, :], TA[:, :], ALU.max).then_inc(den_taken, c.add(den_taken))
                v.wait_ge(den_taken, c.now(den_taken))
                chain(v.tensor_tensor(TA[:, :], TA[:, :], ENM, ALU.max))
                chain(v.reciprocal(TA[:, :], TA[:, :]))
                v.tensor_tensor(TA[:, :], OUT[:, :], TA[:, :], ALU.mult).then_inc(out_taken, c.add(out_taken))
                v.wait_ge(out_taken, c.now(out_taken))
                v.tensor_tensor(TB[:, :], TA[:, :], TA[:, :], ALU.mult).then_inc(sumsq_ready, c.add(sumsq_ready))
                ps = den_in()
                v.tensor_scalar(TB[:, :], ps[:, :], 1.0 / P, None, ALU.mult).then_inc(den_taken, c.add(den_taken))
                v.wait_ge(den_taken, c.now(den_taken))
                v.tensor_scalar(TB[:, :], TB[:, :], EPS, None, ALU.add).then_inc(ms_ready, c.add(ms_ready))
                v.wait_ge(std_ready, c.next(std_ready))
                chain(v.reciprocal(TB[:, :], TB[:, :]))
                chain(v.tensor_tensor(TA[:, :], TA[:, :], TB[:, :], ALU.mult))
                chain(v.tensor_scalar(TA[:, :], TA[:, :], mv("g", 5), None, ALU.mult))
                chain(v.scalar_tensor_tensor(TA[:, :], C, mv("skip", 6), TA[:, :], ALU.mult, ALU.add))
                chain(v.tensor_tensor(TA[:, :], TA[:, :], SG, ALU.mult))
                halves(tile(AH, m + PAIRS), tile(AL, m + PAIRS), TA[:, :])
                v.wait_ge(operand_ready, c.now(operand_ready))
            clear_squares()
            with c.loop("wout", KD // 2) as d:
                v.wait_ge(dve_step, c.now(dve_step))
                for j in range(2):
                    e = d * 2 + j
                    add_to(tile(X, e))
                    prep(tile(X, e), VEC[:, bass.ds(e + col["g_cross"], 1)], tile(XH, e), tile(XL, e))
            rstd()
            v.wait_ge(dve_step, c.now(dve_step))
            for pair in range(XPAIRS):
                take(QB[:, :], ATT_SCALE)
                attention(CROSS, None, tile(AH, pair), tile(AL, pair))
            clear_squares()
            v.wait_ge(dve_step, c.now(dve_step))
            for d in range(KD):
                add_to(tile(X, d))
                prep(tile(X, d), vec("g_ffn", d), tile(XH, d), tile(XL, d))
            rstd()
            v.wait_ge(dve_step, c.now(dve_step))
            NR = GROUPS + EXPERTS
            ps = gemm_in()
            v.tensor_tensor(TB[0:NR, :], ps[0:NR, :], RS[0:NR, :], ALU.mult).then_inc(gemm_taken, c.add(gemm_taken))
            v.wait_ge(gemm_taken, c.now(gemm_taken))
            v.tensor_scalar(TA[0:NR, :], TB[0:NR, :], vec("b_route")[0:NR, :], None, ALU.add).then_inc(turn_ready, c.add(turn_ready))
            for k in range(KD):
                v.scalar_tensor_tensor(tile(XN, k), tile(X, k), vec("g_ffn", k), RS[:, :], ALU.mult, ALU.mult).then_inc(
                    xn_ready, c.add(xn_ready))
            chain(v.tensor_scalar(BEFORE, TRI[:, :], 0.0, None, ALU.is_ge))
            chain(v.tensor_tensor(BEFORE, BEFORE, IDENT[:, :], ALU.subtract))
            v.wait_ge(turned_full, c.next(turned_full))
            v.wait_ge(turned_taken, c.now(turned_full))
            c.skip(turned_full, KD)

            def b3(ap, k):
                return ap.unsqueeze(2).to_broadcast([P, QT, k])

            LG = QB[:, 0:QT * NR].rearrange("p (t e) -> p t e", t=QT)
            lg, le = LG[:, :, 0:GROUPS], LG[:, :, GROUPS:NR]
            g4 = TA[:, 0:QT * GROUPS].rearrange("p (t e) -> p t e", t=QT)

            def e16(i):
                return TB[:, i * 64:(i + 1) * 64].rearrange("p (t e) -> p t e", t=QT)

            gmax, gsum, gw, first, v1, v2, w1, w2 = (SMALL[:, 4 * i:4 * i + 4] for i in range(4, 12))
            d2 = SMALL[:, 0:4]
            pen = TA[:, 32:48].rearrange("p (t e) -> p t e", t=QT)
            desc = vec("desc", 0, EXPERTS)

            def desc_b(k):
                return desc[:, EXPERTS - k:EXPERTS].unsqueeze(1).to_broadcast([P, QT, k])

            def first_of(hot, eq, k):
                chain(v.tensor_tensor(eq, eq, desc_b(k), ALU.mult))
                chain(v.tensor_reduce(first, eq, AX_X, ALU.max))
                chain(v.tensor_tensor(hot, eq, b3(first, k), ALU.is_equal))

            chain(v.tensor_reduce(gmax, lg, AX_X, ALU.max))
            v.tensor_tensor(g4, lg, b3(gmax, GROUPS), ALU.subtract).then_inc(route_args, c.add(route_args))
            chain(v.tensor_tensor(pen, lg, b3(gmax, GROUPS), ALU.is_equal))
            first_of(pen, pen, GROUPS)
            chain(v.tensor_scalar(pen, pen, -1.0, -NEG, ALU.add, ALU.mult))
            chain(v.tensor_tensor(
                TB[:, 0:64].rearrange("p (t g e) -> p t g e", t=QT, g=GROUPS),
                le.rearrange("p t (g e) -> p t g e", g=GROUPS),
                pen.unsqueeze(3).to_broadcast([P, QT, GROUPS, EXPERTS // GROUPS]), ALU.add))
            for k, (best, hot) in enumerate(((v1, e16(1)), (v2, e16(2)))):
                chain(v.tensor_reduce(best, e16(0), AX_X, ALU.max))
                chain(v.tensor_tensor(hot, e16(0), b3(best, EXPERTS), ALU.is_equal))
                first_of(hot, hot, EXPERTS)
                if k == 0:
                    chain(v.scalar_tensor_tensor(e16(0), hot, 2 * NEG, e16(0), ALU.mult, ALU.add))
            v.tensor_tensor(d2, v2, v1, ALU.subtract).then_inc(route_args, c.add(route_args))
            v.tensor_tensor(e16(3), e16(1), e16(2), ALU.add).then_inc(mask_ready, c.add(mask_ready))
            v.wait_ge(route_done, c.next(route_done, 2))
            chain(v.tensor_reduce(gsum, g4, AX_X, ALU.add))
            chain(v.reciprocal(gw, gsum))
            chain(v.tensor_scalar(w1, d2, 1.0, None, ALU.add))
            chain(v.reciprocal(w1, w1))
            chain(v.tensor_tensor(w1, w1, gw, ALU.mult))
            chain(v.tensor_tensor(w2, w1, d2, ALU.mult))
            chain(v.tensor_tensor(e16(1), e16(1), b3(w1, EXPERTS), ALU.mult))
            chain(v.tensor_tensor(e16(2), e16(2), b3(w2, EXPERTS), ALU.mult))
            rank3, share3 = (ap.rearrange("p (t e) -> p t e", t=QT) for ap in (RANK, SHARE))
            chain(v.tensor_tensor(share3[:, :, 0:EXPERTS], e16(1), e16(2), ALU.add))
            ps = scores_in()
            chain(v.tensor_reduce(gmax[:, 0:1], ps[:, QT * EXPERTS:(QT + 1) * EXPERTS], AX_X, ALU.max))
            step(v.tensor_copy(IOTA, ps[:, P:2 * P]))
            v.scalar_tensor_tensor(rank3[:, :, 0:EXPERTS], ps[:, 0:QT * EXPERTS].rearrange("p (t e) -> p t e", t=QT), 1.0,
                                   e16(3), ALU.add, ALU.mult).then_inc(scores_taken, c.add(scores_taken))
            v.wait_ge(scores_taken, c.now(scores_taken))
            chain(v.tensor_scalar(rank3[:, :, 0:EXPERTS], rank3[:, :, 0:EXPERTS], -1.0, None, ALU.add))
            step(v.tensor_scalar(rank3[:, :, EXPERTS:], rank3[:, :, 0:1], float(-P), None, ALU.add))
            step(v.tensor_copy(share3[:, :, EXPERTS:], share3[:, :, 0:1]))
            chain(v.tensor_scalar(first[:, 0:1], gmax[:, 0:1], float(P), 1.0, ALU.is_gt, ALU.add))
            for k in range(2, QT):
                chain(v.scalar_tensor_tensor(first[:, 0:1], gmax[:, 0:1], float(k * P), first[:, 0:1], ALU.is_gt, ALU.add))
            v.tensor_copy(ROUNDS, first[0:1, 0:1]).then_inc(rounds_ready, c.add(rounds_ready))
            v.wait_ge(rounds_ready, c.now(rounds_ready))
            rounds = v.value_load(ROUNDS, min_val=1, max_val=QT)

            def select(e):
                for t in range(QT):
                    at = e + t * (EXPERTS + 1)
                    rank, share = ((buf[:, at:at + 1] if isinstance(at, int) else buf[:, bass.ds(at, 1)]) for buf in (RANK, SHARE))
                    v.tensor_scalar(tile(SEL, t, P), IOTA, rank, None, ALU.is_equal).then_inc(select_step, c.add(select_step))
                    ins = v.tensor_scalar(tile(WSEL, t, P), IOTA, rank, share, ALU.is_equal, ALU.mult)
                    if t < QT - 1:
                        ins.then_inc(select_step, c.add(select_step))
                ins.then_inc(select_ready, c.add(select_ready))

            select(0)
            c.skip(panel_done, E_SLOTS)
            with c.loop("rounds", rounds):
                with c.loop("experts", EXPERTS) as e:
                    v.wait_ge(gathered, c.next(gathered, 2))
                    v.tensor_copy(XG[:, T:2 * T], SCORE[1][:, :]).then_inc(gathered_taken1, c.add(gathered_taken1))
                    v.wait_ge(select_turned, c.next(select_turned))
                    select(e + 1)
                    c.skip(panel_done, FT_MOE)
                    v.wait_ge(gate_act, c.next(gate_act))
                    for j, ps in enumerate((TURN[1], SCORE[0])):
                        v.wait_ge(panel_done, c.next(panel_done, 2))
                        v.tensor_tensor(tile(HID, j, 2 * P), ps[:, 0:2 * P], tile(GACT, j, 2 * P), ALU.mult).then_inc(
                            hidden_ready, c.add(hidden_ready))
                    c.skip(panel_done, FT_MOE)
                    for d in range(KD):
                        v.wait_ge(scattered, c.next(scattered))
                        v.tensor_tensor(tile(X, d), GEMM[d % 2][:, :], tile(X, d), ALU.add).then_inc(added, c.add(added))
                v.tensor_scalar(RANK, RANK, float(-P), None, ALU.add).then_inc(select_step, c.add(select_step))
                v.wait_ge(select_step, c.now(select_step))
            v.memset(SQ[:, :], 0.0).then_inc(experts_done, c.add(experts_done))
            with c.loop("sq_final", KD) as k:
                v.wait_ge(experts_done, c.now(experts_done))
                chain(v.tensor_tensor(TA[:, :], tile(X, k), tile(X, k), ALU.mult))
                v.tensor_tensor(SQ[:, :], SQ[:, :], TA[:, :], ALU.add).then_inc(sumsq_ready, c.add(sumsq_ready))
                v.wait_ge(sumsq_ready, c.now(sumsq_ready))
            rstd()
            clear_squares()
            with c.loop("final1", KD) as k:
                v.wait_ge(dve_step, c.now(dve_step))
                chain(v.scalar_tensor_tensor(TB[:, :], tile(X, k), VEC[:, bass.ds(k + col["g_final"], 1)],
                                             RS[:, :], ALU.mult, ALU.mult))
                chain(v.tensor_scalar(tile(X, k).rearrange("p (c r) -> p r c", r=NA_ROWS),
                                      TB[:, :].rearrange("p (r c) -> p r c", r=NA_ROWS), 1.0, None, ALU.mult))
                prep(tile(X, k), VEC[:, bass.ds(k + col["gains2"], 1)], tile(XH, k), tile(XL, k))
            with c.loop("layers", LAYERS) as l:
                def gain(s):
                    return lambda e: VEC[:, bass.ds(l * 24 + e + (col["gains2"] + 8 * s), 1)]

                ffn("a", gain(1))
                rstd()
                with c.loop("na", PAIRS) as i:
                    v.wait_ge(dve_step, c.now(dve_step))
                    take(QB[:, :], ATT_SCALE)
                    take(KB[:, :])
                    take(VT[:, :])
                    take(UT)
                    for b in range(2):
                        ps = scores_in()
                        v.tensor_copy(AB[:, b * T:(b + 1) * T], ps[:, :]).then_inc(scores_taken, c.add(scores_taken))
                    for h in range(2):
                        v.wait_ge(bias_in[h], c.next(bias_in[h], 16))
                        chain(v.tensor_tensor(BIAS[h], BIAS[h], MASK, ALU.add))
                    v.wait_ge(turned_full, c.next(turned_full, 2))

                    def fourier_out():
                        v.tensor_copy(TA[:, :], den_in()[:, :]).then_inc(den_taken, c.add(den_taken))
                        v.wait_ge(den_taken, c.now(den_taken))
                        halves(tile(AH, i + PAIRS), tile(AL, i + PAIRS), TA[:, :])
                        v.wait_ge(operand_ready, c.now(operand_ready))

                    def bias_of(h, t):
                        return BIAS[h][:, NEAR_AT[t]:NEAR_AT[t] + span(NEAR[t])[1]]

                    attention(NEAR, bias_of, tile(AH, i), tile(AL, i), {2: lambda: take(tile(GATE_A, i * 2)), 3: fourier_out, 5: lambda: take(tile(GATE_B, i * 2)),
                               7: lambda: take(tile(GATE_A, i * 2 + 1)), 8: lambda: take(tile(GATE_B, i * 2 + 1))})
                with c.loop("comb", KD // 2) as d:
                    for j in range(2):
                        e = d * 2 + j
                        for s, gates in enumerate((GATE_A, GATE_B)):
                            ps = gemm_in()
                            v.wait_ge(act_out, c.next(act_out))
                            v.tensor_tensor(PROB[s][:, :], ps, tile(gates, e), ALU.mult).then_inc(gemm_taken, c.add(gemm_taken))
                        v.wait_ge(gemm_taken, c.now(gemm_taken))
                        chain(v.tensor_tensor(PROB[0][:, :], PROB[0][:, :], PROB[1][:, :], ALU.add))
                        halves(tile(AH, e + KD), tile(AL, e + KD), PROB[0][:, :])
                        v.wait_ge(operand_ready, c.now(operand_ready))
                clear_squares()
                with c.loop("wo", KD // 2) as d:
                    v.wait_ge(dve_step, c.now(dve_step))
                    for j in range(2):
                        e = d * 2 + j
                        add_to(tile(X, e))
                        prep(tile(X, e), gain(2)(e), tile(XH, e), tile(XL, e))
                ffn("b", gain(3))
            rstd()
            with c.loop("last", KD) as k:
                v.wait_ge(dve_step, c.now(dve_step))
                v.scalar_tensor_tensor(tile(X, k), tile(X, k), VEC[:, bass.ds(k + col["last_gain"], 1)],
                                                           RS[:, :], ALU.mult, ALU.mult).then_inc(out_ready, c.add(out_ready))


def panels(w):
    k, n = w.shape
    return w.reshape(k // P, P, n // P, P).transpose(2, 1, 0, 3).reshape(n // P, P, k)


def columns(g):
    return g.reshape(-1, P).T


def feature_major(x):
    t, d = x.shape
    return np.ascontiguousarray(x.T.reshape(d // P, P, t).transpose(1, 0, 2).reshape(P, d // P * t))


def by_column():
    return np.arange(T).reshape(NA_ROWS, GRID_W).T.reshape(-1)


def near_tables():
    for i in (0, 1, QT - 1):
        key, n = span(NEAR[i])
        q, k = i * P + np.arange(P)[:, None], key + np.arange(n)[None]
        start = np.clip(q // NA_ROWS - NA_COLS // 2, 0, GRID_W - NA_COLS)
        yield k % NA_ROWS - q % NA_ROWS, k // NA_ROWS - q // NA_ROWS, k // NA_ROWS + 0 * q, start


def constants():
    f = np.float32
    q, k = np.arange(T)[:, None], np.arange(T)[None]
    far = q - k
    times = ((far >= 0) & (far <= 128)).astype(int) + ((far >= 0) & (far % 4 == 0)) + ((far >= 0) & (far % 16 == 0))
    ln = np.where(times > 0, np.log(np.maximum(times, 1)), NEG).astype(f)
    ln = np.concatenate([ln[i * P:(i + 1) * P, :(i + 1) * P] for i in range(QT)], axis=1)
    rot = np.zeros((P, P), f)
    invf = np.zeros((P, 1), f)
    half = HEAD // 8
    inv = (f(500000.0) ** (-np.arange(0, 2 * half, 2, dtype=f) / f(2 * half))).astype(f)
    for h in range(2):
        for j in range(half):
            lo, hi = h * HEAD + j, h * HEAD + half + j
            rot[hi, lo], rot[lo, hi] = -1, 1
            invf[lo] = invf[hi] = inv[j]
    s, t = np.arange(P)[:, None], np.arange(P)[None]
    tri = np.where(t >= s, 0, NEG).astype(f)
    near = []
    for _, _, dist, start in near_tables():
        near.append(np.where((dist >= start) & (dist < start + NA_COLS), 0, NEG).astype(f))
    near = np.concatenate(near, axis=1)
    ang = 2 * np.pi * (s * t % P) / P
    cs = np.concatenate([np.cos(ang), np.sin(ang)], axis=1).astype(f)
    at = by_column()
    ang = 2 * np.pi * (at[:, None] * at[None] % T) / T
    norm = (T * P) ** -0.5
    ct, nst = ((m * norm).astype(f).reshape(QT, P, T).transpose(1, 0, 2).reshape(P, QT * T) for m in (np.cos(ang), -np.sin(ang)))
    return {"ident": np.eye(P, dtype=f), "rot": rot, "tri": tri, "near": near, "cs": cs, "ln": ln,
            "ct": np.ascontiguousarray(ct), "nst": np.ascontiguousarray(nst)}, invf


def lay_out(x):
    f = np.float32
    arrays, invf = constants()
    vecs, cols, at = [], {}, 0

    def put(name, part):
        nonlocal at
        whole = np.zeros((P, part.shape[1]), f)
        whole[:part.shape[0]] = part
        vecs.append(whole)
        cols[name] = at
        at += part.shape[1]

    for name in ("g_mix", "g_mem", "g_cross", "g_ffn"):
        put(name, columns(x[name][0]))
    put("g_final", columns(x["g_final"]))
    put("gains2", np.concatenate([columns(x[n][l]) for l in range(LAYERS) for n in ("ffn1_norm_2", "mix_norm_2", "ffn2_norm_2")]
                                 + [columns(x["final_norm_2"])], axis=1))
    cols["last_gain"] = cols["gains2"] + 24 * LAYERS
    put("gate_b", np.concatenate([columns(x["mix_gate_bias_2"][l, s]) for l in range(LAYERS) for s in range(2)], axis=1))
    heads = [columns(x["conv_w"][0, j]) for j in range(4)] + [columns(x[n][0]) for n in ("conv_b", "g_mhn", "skip_m", "skip_m")]
    put("mvec", np.stack(heads, axis=2).reshape(P, M_HEADS * 8))
    put("b_i", x["b_i"][0][:, None])
    put("b_f", x["b_f"][0][:, None])
    put("b_route", np.concatenate([x["b_router_g"][0], x["b_router_e"][0]])[:, None])
    put("invf", invf)
    put("desc", np.tile(np.arange(EXPERTS, 0, -1, dtype=f), (P, 1)))
    arrays["vec"] = np.concatenate(vecs, axis=1)

    arrays["xT"] = feature_major(x["x"][0])
    arrays["memT"] = feature_major(x["mem"][0])
    arrays["positions"] = np.ascontiguousarray(x["positions"])

    def padded(*ws):
        w = np.concatenate(ws, axis=1)
        return np.pad(w, ((0, 0), (0, P - w.shape[1])))

    kv = panels(x["w_kv_x"][0])
    w_in = panels(x["w_in"][0][:, :6 * PAIRS * P])
    gates = x["w_in"][0][:, 6 * PAIRS * P:]
    order = [w_in[part * PAIRS + i] for i in range(PAIRS) for part in (3, 4, 0, 1, 2, 5)]
    experts = []
    for e in range(EXPERTS):
        w1, w3 = panels(x["w1"][0, e]), panels(x["w3"][0, e])
        experts += list(w1) + list(w3)
        experts += list(x["w2"][0, e].reshape(FT_MOE, P, D))
    wo = panels(x["w_o_x"][0]).reshape(2, KD // 2, P, 2 * P).transpose(0, 2, 1, 3).reshape(2, P, KD * P)
    first = [kv[0], kv[2], kv[1], kv[3], panels(padded(gates[:, :M_HEADS]))[0], panels(padded(gates[:, M_HEADS:]))[0]]
    first += order + list(panels(x["w_out"][0])) + list(panels(x["w_q_x"][0])) + list(wo)
    first += [panels(padded(x["w_router_g"][0], x["w_router_e"][0]))[0]]
    arrays["experts"] = np.stack(experts)
    arrays["panels1"] = np.stack(first)
    arrays["w_qk_m"] = np.concatenate([x["w_q_m"][0], x["w_k_m"][0]], axis=2)

    up, down, mix, bias = [], [], [], []
    for l in range(LAYERS):
        for which in ("ffn1", "ffn2"):
            wi = panels(x[f"{which}_w_in_2"][l]).reshape(2, 2 * HALF_FT, P, PANEL).transpose(1, 0, 2, 3)
            up.append(wi.reshape(4 * HALF_FT, P, PANEL))
            wo = panels(x[f"{which}_w_out_2"][l]).reshape(KD, P, 2, WIDE).transpose(2, 0, 1, 3)
            down.append(wo.reshape(2 * KD, P, WIDE))
        wi = panels(x["mix_w_in_2"][l])
        for i in range(PAIRS):
            mix += [wi[part * PAIRS + i] for part in range(4)]
            mix += [wi[16 + g * KD + d] for d in (2 * i, 2 * i + 1) for g in range(2)]
        both = np.concatenate([panels(x["na_w_out_2"][l]), panels(x["f_w_out_2"][l])], axis=2)
        mix += list(both)
        mix += list(panels(x["mix_w_o_2"][l]))
        rpb = x["na_rpb_2"][l]
        wide = np.pad(rpb, ((0, 0), (0, 0), (GRID_W, GRID_W)))
        for h in range(rpb.shape[0]):
            bias.append(np.concatenate([wide[h, rows + NA_ROWS - 1, cols + NA_COLS - 1 + GRID_W]
                                        for rows, cols, _, _ in near_tables()], axis=1))
    arrays["up2"], arrays["down2"] = np.concatenate(up), np.concatenate(down)
    arrays["mix2"], arrays["bias"] = np.stack(mix), np.stack(bias)
    return arrays, cols


def kernel(**inputs):
    import concourse.bacc as bacc
    from concourse.bass_utils import run_bass_kernel_spmd

    arrays, cols = lay_out({k: np.asarray(v) for k, v in inputs.items()})

    def program(trips):
        nc = bacc.Bacc("TRN2", target_bir_lowering=False, num_devices=1)
        a = {n: nc.dram_tensor(n, v.shape, mybir.dt.from_np(v.dtype), kind="ExternalInput").ap() for n, v in arrays.items()}
        a["cols"] = cols
        a["outT"] = nc.dram_tensor("outT", (P, KD * T), F32, kind="ExternalOutput").ap()
        build(nc, a, trips)
        return nc

    trips = {}
    program(trips)
    nc = program(trips)
    r = run_bass_kernel_spmd(nc, [arrays], core_ids=[0])
    by_token = np.asarray(r.results[0]["outT"]).reshape(P, KD, T).transpose(2, 1, 0).reshape(T, D)
    out = np.empty((1, T, D), np.float32)
    out[0, by_column()] = by_token
    return out
```

```python
from contextlib import ExitStack, contextmanager

import concourse.bass as bass
from concourse import mybir
import numpy as np

F32 = mybir.dt.float32
F32R = mybir.dt.float32r
I32 = mybir.dt.int32
ALU = mybir.AluOpType
ACT = mybir.ActivationFunctionType
AX_X = mybir.AxisListType.X

P = 128
T = 512
D = 1024
KD = D // P
MEM = 256
EPS = 1e-6
LAYERS = 2
HEAD = 64
PAIRS = 4
XPAIRS = 2
QT = T // P
M_HEADS = 4
GROUPS = 4
EXPERTS = 16
FF_MOE = 512
FT_MOE = FF_MOE // P
D_FF = 2816
HALF_FT = D_FF // P // 2
PANEL = KD * P
WIDE = HALF_FT * P
GRID_W = 64
NA_ROWS, NA_COLS = 8, 16
ATT_SCALE = HEAD ** -0.5
M_SCALE = P ** -0.5
NEG = -1e30

CAUSAL = [[(j, j * P, P) for j in range(i + 1)] for i in range(QT)]
CROSS = [[(j, j * P, P) for j in range(MEM // P)]] * QT
NA_EDGES = [0, *range(P // 2, T, P), T]
NEAR_BLOCKS = [(j, at, end - at) for j, (at, end) in enumerate(zip(NA_EDGES, NA_EDGES[1:]))]
NEAR = [NEAR_BLOCKS[i:i + 2] for i in range(QT)]
NEAR_TABLES = [sum(n for _, _, n in NEAR[i]) for i in (0, 1, QT - 1)]
NEAR_AT = [0] + [NEAR_TABLES[0]] * (QT - 2) + [NEAR_TABLES[0] + NEAR_TABLES[1]]
BIAS_COLS = sum(NEAR_TABLES)

PI_LOW = 3.1415925
TWO_PI_PARTS = (6.28125, 0.0019340515136718750, float(2 * np.pi - 6.28125 - 0.0019340515136718750))

N_PANELS1 = 2 * XPAIRS + 2 + 6 * PAIRS + KD + XPAIRS + 2 + 1
PAIR = 2
E_PANELS = 3 * FT_MOE * PAIR
E_SLOTS = 6
MIX2 = 4 * PAIRS + 3 * KD + KD

SEMS = (
    "consts_in x_in mem_in pos_in raw_in0 raw_in1 heads_in bias_in0 bias_in1 dft_in stored "
    "split_hi split_lo gemm_done gemm_taken scores_full scores_taken turned_full turned_taken "
    "out_full out_taken den_full den_taken operand_ready sumsq_ready squares_ready normed high_ready moved std_ready vec_in "
    "dve_step logits_ready exp_done probs_ready turn_ready qk_ready conv_done conv_ready "
    "sin_ready sin_done gate_ready gate_done rows_ready m_args_ready m_exp_ready "
    "act_out route_args route_done out_ready "
    "xn_ready turned_copied low_ready mask_ready rounds_ready "
    "weights_in0 weights_in1 weights_in2 weights_in3 weights_in4 weights_in5 "
    "panel_done select_step select_ready select_turned slots_turned gathered gathered_taken0 gathered_taken1 "
    "shares_ready shares_taken gate_act hidden_ready half_done result_high "
    "result_ready scattered added experts_done"
).split()


RINGS = ("split_hi", "split_lo", "gemm_done", "gemm_taken", "scores_full", "scores_taken", "turned_full", "turned_taken")


def span(blocks):
    return blocks[0][1], sum(n for _, _, n in blocks)


class Counts:

    def __init__(self, eng, who, trips):
        self.eng, self.who, self.trips = eng, who, trips
        self.n = {name: 0 for name in SEMS}
        self.open = []

    def at(self, sem):
        return self.n[sem.name]

    def add(self, sem, by=1):
        self.n[sem.name] += by
        return by

    def skip(self, sem, by=1):
        self.n[sem.name] += by

    def now(self, sem, off=0):
        value = self.n[sem.name] + off
        assert value > 0, (self.who, sem.name)
        for label, reg in self.open:
            per_trip = self.trips.get((self.who, label, sem.name), 0)
            if per_trip:
                value = reg * per_trip + value
        return value

    def next(self, sem, by=1):
        self.n[sem.name] += by
        return self.now(sem)

    @contextmanager
    def loop(self, label, trips):
        before = dict(self.n)
        with self.eng.Fori(0, trips) as reg:
            self.open.append((label, reg))
            yield reg
            self.open.pop()
        for name, start in before.items():
            per_trip = self.n[name] - start if self.n[name] is not None else 0
            assert per_trip % 2 == 0 or name not in RINGS, (self.who, label, name, per_trip)
            self.trips[self.who, label, name] = per_trip
            if start is None:
                continue
            if isinstance(trips, int):
                self.n[name] = start + trips * per_trip
            elif per_trip:
                self.n[name] = None


def build(nc, a, trips):
    ctx = ExitStack()
    with ctx:
        def sb(name, cols, dt=F32):
            return ctx.enter_context(nc.sbuf_tensor(name, [P, cols], dt))

        def f32(ap):
            return ap.bitcast(F32)

        X = sb("X", KD * T)
        XH = sb("XH", KD * T, F32R)
        XL = sb("XL", KD * T, F32R)
        RAW = [sb(f"RAW{i}", WIDE) for i in range(2)]
        with ExitStack() as products:
            def rounded(name, cols):
                return products.enter_context(nc.sbuf_tensor(name, [P, cols], F32R))

            AH = rounded("AH", 2 * KD * T)
            AL = rounded("AL", 2 * KD * T)
            WH = [rounded(f"WH{i}", WIDE) for i in range(2)]
            WL = [rounded(f"WL{i}", WIDE) for i in range(2)]
        with ExitStack() as experts:
            def plain(name, cols, dt=F32):
                return experts.enter_context(nc.sbuf_tensor(name, [P, cols], dt))[:, :]

            with ExitStack() as before:
                XN = before.enter_context(nc.sbuf_tensor("XN", [P, KD * T], F32))[:, :]
            YH, YL = (plain(n, PAIR * D, F32R) for n in ("YH", "YL"))
            XTH, XTL = (plain(n, QT * D, F32R) for n in ("XTH", "XTL"))
            with ExitStack() as before:
                XT = before.enter_context(nc.sbuf_tensor("XT", [P, QT * D], F32))[:, :]
            E_PANEL = [None] * 2 + [plain(f"E_PANEL{i}", PANEL) for i in range(2, E_SLOTS)]
            SEL = plain("SEL", QT * PAIR * P, F32R)
            SLOTS_T = [plain(f"SLOTS_T{i}", T, F32R) for i in range(PAIR)]
            HID, GACT = ([plain(f"{n}{i}", T) for i in range(PAIR)] for n in ("HID", "GACT"))
            IOTA, BEFORE = plain("IOTA", P), plain("BEFORE", P)
            RANK, SHARE = (plain(n, QT * (EXPERTS + PAIR)) for n in ("RANK", "SHARE"))
            SLOT_SHARE = plain("SLOT_SHARE", PAIR)
            for i in range(2):
                E_PANEL[i] = RAW[i][:, 0:PANEL]
        with ExitStack() as gates:
            GATE_A, GATE_B = ([gates.enter_context(nc.sbuf_tensor(f"{n}{i}", [P, KD * T], F32))[:, :] for i in range(2)][1]
                              for n in ("GATE_A", "GATE_B"))
        ctx.enter_context(nc.sbuf_tensor("KEPT", [P, 4 * KD * T + 4 * WIDE], F32))
        BIG = sb("BIG", 2 * QT * T)
        LN_COLS = P * QT * (QT + 1) // 2
        LN = BIG[:, 0:LN_COLS]
        COS = BIG[:, LN_COLS:LN_COLS + T]
        SIN = BIG[:, LN_COLS + T:LN_COLS + 2 * T]
        GATE = BIG[:, LN_COLS + 2 * T:LN_COLS + 3 * T]
        ENM = BIG[:, LN_COLS + 3 * T:LN_COLS + 4 * T]
        KX = BIG[:, LN_COLS + 4 * T:LN_COLS + 5 * T]
        ROT = BIG[:, LN_COLS + 5 * T:LN_COLS + 5 * T + P]
        TRI = BIG[:, LN_COLS + 5 * T + P:LN_COLS + 5 * T + 2 * P]
        CT = BIG[:, 0:QT * T]
        NST = BIG[:, QT * T:2 * QT * T]
        IDENT = sb("IDENT", P)
        CS = sb("CS", 2 * P)
        ONES = sb("ONES", P)
        VEC = sb("VEC", a["vec"].shape[1])
        SMALL = sb("SMALL", 48)
        QB = sb("QB", T)
        KB = sb("KB", T)
        VB = sb("VB", len(NEAR_BLOCKS) * P)
        VT = sb("VT", T)
        PROB = [sb(f"PROB{i}", T) for i in range(2)]
        PT = sb("PT", QT * T)
        XG = PT[:, :]
        AR = sb("AR", 6 * T)
        C, MV, MQ, MK, SG, VX = (AR[:, i * T:(i + 1) * T] for i in range(6))
        ROUNDS = SMALL[0:1, 12:13].bitcast(I32)
        PADU = sb("PADU", T + 4)
        U = PADU[:, 4:4 + T]
        BIAS = [AR[:, i * BIAS_COLS:(i + 1) * BIAS_COLS] for i in range(2)]
        AB = AR[:, 2 * BIAS_COLS:2 * BIAS_COLS + 2 * T]
        MASK = AR[:, 2 * BIAS_COLS + 2 * T:3 * BIAS_COLS + 2 * T]
        UT = U
        WQK = sb("WQK", 2 * P)
        TA = sb("TA", T)
        TB = sb("TB", T)
        DIAG = [TB[:, i * P:(i + 1) * P] for i in range(2)]
        RS = sb("RS", T)
        SQ = sb("SQ", T)

        def bank(name):
            return ctx.enter_context(nc.psum_tensor(name, [P, T], F32))

        GEMM = [bank(f"GEMM{i}") for i in range(2)]
        SCORE = [bank(f"SCORE{i}") for i in range(2)]
        TURN = [bank(f"TURN{i}") for i in range(2)]
        OUT = bank("OUT")
        DEN = bank("DEN")
        (consts_in, x_in, mem_in, pos_in, raw_in0, raw_in1, heads_in, bias_in0,
         bias_in1, dft_in, stored, split_hi, split_lo, gemm_done, gemm_taken, scores_full,
         scores_taken, turned_full, turned_taken, out_full, out_taken, den_full, den_taken, operand_ready,
         sumsq_ready, squares_ready, normed, high_ready, moved, std_ready, vec_in, dve_step,
         logits_ready, exp_done, probs_ready, turn_ready, qk_ready, conv_done, conv_ready, sin_ready,
         sin_done, gate_ready, gate_done, rows_ready, m_args_ready, m_exp_ready, act_out, route_args,
         route_done, out_ready, xn_ready, turned_copied, low_ready, mask_ready, rounds_ready, weights_in0,
         weights_in1, weights_in2, weights_in3, weights_in4, weights_in5, panel_done, select_step, select_ready,
         select_turned, slots_turned, gathered, gathered_taken0, gathered_taken1, shares_ready, shares_taken, gate_act,
         hidden_ready, half_done, result_high, result_ready, scattered, added, experts_done) = (
            ctx.enter_context(nc.semaphore(name)) for name in SEMS)
        gathered_taken = (gathered_taken0, gathered_taken1)
        weights_in = (weights_in0, weights_in1, weights_in2, weights_in3, weights_in4, weights_in5)
        raw_in, bias_in = (raw_in0, raw_in1), (bias_in0, bias_in1)
        block = ctx.enter_context(nc.Block())

        col = a["cols"]

        def vec(name, i=0, n=1):
            return VEC[:, col[name] + i:col[name] + i + n]

        def tile(big, d, n=T):
            return big[:, d * n:(d + 1) * n] if isinstance(d, int) else big[:, bass.ds(d * n, n)]

        LN_AT = [P * i * (i + 1) // 2 for i in range(QT)]

        @block.sync
        def _(sp):
            c = Counts(sp, "sp", trips)

            def load(src, width=PANEL):
                slot = c.at(split_lo) % 2
                if c.at(split_lo) > 1:
                    sp.wait_ge(split_lo, c.now(split_lo, -1))
                c.skip(split_lo)
                sp.dma_start(RAW[slot][:, 0:width], src).then_inc(raw_in[slot], c.add(raw_in[slot], 16))

            def panel(table, i, width=PANEL):
                return table[i] if isinstance(i, int) else table[bass.ds(i, 1)].rearrange("o p n -> (o p) n")

            sp.dma_start(VEC[:, :], a["vec"]).then_inc(vec_in, c.add(vec_in, 16))
            sp.dma_start(PT[:, 0:KD * MEM], a["memT"]).then_inc(mem_in, c.add(mem_in, 16))
            load(a["panels1"][0])
            load(a["panels1"][1])
            sp.dma_start(X[:, :], a["xT"]).then_inc(x_in, c.add(x_in, 16))
            for name, dst in (("ident", IDENT), ("rot", ROT), ("tri", TRI), ("cs", CS), ("ln", LN)):
                sp.dma_start(dst[:, :], a[name]).then_inc(consts_in, c.add(consts_in, 16))
            sp.dma_start(TB[:, :].bitcast(I32), a["positions"].partition_broadcast(P)).then_inc(pos_in, c.add(pos_in, 16))
            base = 2 * XPAIRS + 2
            for i in range(2, base):
                load(a["panels1"][i])
            with c.loop("mix1", PAIRS) as i:
                for j in range(6):
                    load(panel(a["panels1"], i * 6 + (base + j)))
                    if j == 4:
                        sp.wait_ge(conv_done, c.next(conv_done))
                        sp.dma_start(WQK[:, :], panel(a["w_qk_m"], i)).then_inc(heads_in, c.add(heads_in, 16))
            base += 6 * PAIRS
            with c.loop("rest1", (N_PANELS1 - base) // 2) as i:
                load(panel(a["panels1"], i * 2 + base))
                load(panel(a["panels1"], i * 2 + (base + 1)))
            load(a["panels1"][N_PANELS1 - 1])
            sp.wait_ge(rounds_ready, c.next(rounds_ready))
            rounds = sp.value_load(ROUNDS, min_val=1, max_val=QT)
            sp.wait_ge(low_ready, c.next(low_ready, KD))
            c.skip(panel_done, E_SLOTS)
            with c.loop("rounds", rounds):
                with c.loop("experts", EXPERTS // PAIR) as e:
                    for p in range(E_PANELS):
                        sp.wait_ge(panel_done, c.now(panel_done, 1 - E_SLOTS))
                        c.skip(panel_done)
                        at = weights_in[p % E_SLOTS]
                        sp.dma_start(E_PANEL[p % E_SLOTS], panel(a["experts"], e * E_PANELS + p)).then_inc(at, c.add(at, 16))
            sp.wait_ge(experts_done, c.next(experts_done))
            sp.wait_ge(route_args, c.next(route_args))
            sp.dma_start(CT, a["ct"]).then_inc(dft_in, c.add(dft_in, 16))
            sp.dma_start(NST, a["nst"]).then_inc(dft_in, c.add(dft_in, 16))
            sp.dma_start(MASK, a["near"]).then_inc(dft_in, c.add(dft_in, 16))

            def ffn(label, l, which):
                for half in range(2):
                    at = l * 88 + (which * 44 + half * 22)
                    with c.loop(f"up{label}{half}", HALF_FT) as f:
                        load(panel(a["up2"], f * 2 + at))
                        load(panel(a["up2"], f * 2 + (at + 1)))
                    at = l * 32 + (which * 16 + half * 8)
                    with c.loop(f"down{label}{half}", KD // 2) as d:
                        load(panel(a["down2"], d * 2 + at), WIDE)
                        load(panel(a["down2"], d * 2 + (at + 1)), WIDE)

            c.skip(probs_ready, 2 * QT * (PAIRS + XPAIRS))
            with c.loop("layers", LAYERS) as l:
                ffn("a", l, 0)
                with c.loop("na", PAIRS) as i:
                    for j in range(8):
                        load(panel(a["mix2"], i * 8 + (l * MIX2 + j)))
                        if j in (1, 2):
                            sp.wait_ge(probs_ready, c.now(probs_ready))
                            sp.dma_start(
                                BIAS[j - 1], panel(a["bias"], i * 2 + (l * 8 + (j - 1)))).then_inc(bias_in[j - 1], c.add(bias_in[j - 1], 16))
                    c.skip(probs_ready, 2 * QT)
                with c.loop("out", KD) as d:
                    for j in range(2):
                        load(panel(a["mix2"], d * 2 + (l * MIX2 + 8 * PAIRS + j)))
                ffn("b", l, 1)
            sp.wait_ge(out_ready, c.next(out_ready, KD))
            sp.dma_start(a["outT"], X[:, :]).then_inc(stored, c.add(stored, 16))
            sp.wait_ge(stored, c.now(stored))

        @block.gpsimd
        def _(pool):
            c = Counts(pool, "pool", trips)

            def subtract_lo(width=PANEL):
                slot = c.at(split_lo) % 2
                pool.wait_ge(split_hi, c.next(split_hi))
                pool.tensor_tensor(WL[slot][:, 0:width], RAW[slot][:, 0:width],
                                                      f32(WH[slot][:, 0:width]), ALU.subtract).then_inc(split_lo, c.add(split_lo))

            with c.loop("first", N_PANELS1 // 2):
                subtract_lo()
                subtract_lo()
            subtract_lo()
            for d in range(KD):
                pool.wait_ge(turned_copied, c.next(turned_copied))
                low, high, whole = (ap.rearrange("p (t f) -> p t f", t=QT)[:, :, d * P:(d + 1) * P] for ap in (XTL, f32(XTH), XT))
                pool.tensor_tensor(low, whole, high, ALU.subtract).then_inc(low_ready, c.add(low_ready))

            for k in range(KD // 2):
                pool.wait_ge(normed, c.next(normed))
                pool.tensor_copy(tile(X, k), tile(XN, k)).then_inc(moved, c.add(moved))

            def ffn(label):
                for half in range(2):
                    with c.loop(f"up{label}{half}", HALF_FT):
                        subtract_lo()
                        subtract_lo()
                    with c.loop(f"down{label}{half}", KD // 2):
                        subtract_lo(WIDE)
                        subtract_lo(WIDE)

            with c.loop("layers", LAYERS):
                ffn("a")
                with c.loop("mix2", MIX2 // 2):
                    subtract_lo()
                    subtract_lo()
                ffn("b")

        @block.tensor
        def _(pe):
            c = Counts(pe, "pe", trips)
            c.skip(added, 2)
            c.skip(out_taken)
            c.skip(den_taken)

            def next_panel():
                slot = c.at(split_lo) % 2
                pe.wait_ge(split_lo, c.next(split_lo))
                return WH[slot], WL[slot]

            def gemm_bank(n=T):
                ps = GEMM[c.at(gemm_taken) % 2][:, 0:n]
                if c.at(gemm_taken) > 1:
                    pe.wait_ge(gemm_taken, c.now(gemm_taken, -1))
                c.skip(gemm_taken)
                return ps

            def products(ps, w, blocks, srcs, begin=True, end=True):
                wh, wl = w
                for j, (b, (hi, lo)) in enumerate(zip(blocks, srcs)):
                    whb, wlb = wh[:, b * P:(b + 1) * P], wl[:, b * P:(b + 1) * P]
                    pe.matmul(ps, whb, hi, start=(begin and j == 0), stop=False)
                    pe.matmul(ps, whb, lo, start=False, stop=False)
                    mm = pe.matmul(ps, wlb, hi, start=False, stop=(end and j == len(blocks) - 1))
                return mm

            def gemm(w, blocks, srcs, n=T):
                products(gemm_bank(n), w, blocks, srcs).then_inc(gemm_done, c.add(gemm_done))

            def gemm_as_ready(w, blocks, srcs, ready):
                ps = gemm_bank()
                blocks = list(blocks)
                early = len(blocks) - len(ready)
                if early:
                    products(ps, w, blocks[:early], srcs[:early], end=False)
                for j, count in enumerate(ready, early):
                    pe.wait_ge(operand_ready, count)
                    mm = products(ps, w, blocks[j:j + 1], srcs[j:j + 1], begin=(j == 0), end=(j == len(blocks) - 1))
                mm.then_inc(gemm_done, c.add(gemm_done))

            def score_bank():
                at = c.at(scores_taken) % 2
                if c.at(scores_taken) > 1:
                    pe.wait_ge(scores_taken, c.now(scores_taken, -1))
                c.skip(scores_taken)
                return SCORE[at]

            def turn_bank():
                at = c.at(turned_taken) % 2
                if c.at(turned_taken) > 1:
                    pe.wait_ge(turned_taken, c.now(turned_taken, -1))
                c.skip(turned_taken)
                return TURN[at]

            x_tiles = [(tile(XH, k), tile(XL, k)) for k in range(KD)]
            a_tiles = [(tile(AH, k), tile(AL, k)) for k in range(2 * KD)]
            mem_tiles = [(tile(AH, k, MEM), tile(AL, k, MEM)) for k in range(KD)]
            eight = range(KD)

            def den_bank():
                pe.wait_ge(den_taken, c.now(den_taken))
                c.skip(den_taken)
                return DEN

            def sum_squares(n=T):
                pe.wait_ge(sumsq_ready, c.next(sumsq_ready, KD))
                ps = den_bank()
                pe.matmul(ps[:, 0:n], ONES[:, :], SQ[:, 0:n], start=True, stop=True).then_inc(den_full, c.add(den_full))

            def turn(src, blocks, rows=P):
                ps = turn_bank()
                for at, j in enumerate(blocks):
                    mm = pe.transpose(ps[:, at * rows:(at + 1) * rows], src[0:rows, j * P:(j + 1) * P],
                                      IDENT[0:rows, 0:rows])
                mm.then_inc(turned_full, c.add(turned_full))

            jobs = [(h, i) for h in range(2) for i in range(QT)]

            def attention(tiles, v, between=None, k_src=KB):
                for u in range(len(jobs) + 3):
                    if u < len(jobs):
                        h, i = jobs[u]
                        part = slice(h * HEAD, (h + 1) * HEAD)
                        first, n = span(tiles[i])
                        pe.matmul(score_bank()[:, 0:n], QB[part, i * P:(i + 1) * P], k_src[part, first:first + n],
                                  start=True, stop=True).then_inc(scores_full, c.add(scores_full))
                    if between and u in between:
                        between[u]()
                    if 2 <= u < len(jobs) + 2:
                        h, i = jobs[u - 2]
                        pe.wait_ge(probs_ready, c.next(probs_ready))
                        ps = turn_bank()
                        first, n = span(tiles[i])
                        for at, (_, key, size) in enumerate(tiles[i]):
                            mm = pe.matmul(ps[0:size, at * P:(at + 1) * P], PROB[u % 2][:, key - first:key - first + size],
                                           DIAG[u % 2], start=True, stop=True)
                        mm.then_inc(turned_full, c.add(turned_full))
                    if u >= 3:
                        pe.wait_ge(turned_taken, c.now(turned_taken, -1 if u < len(jobs) + 2 else 0))
                        values(*jobs[u - 3], tiles, v)
                c.skip(out_taken)

            def values(h, i, tiles, v):
                if h == 0 and i == 0:
                    pe.wait_ge(out_taken, c.now(out_taken))
                out = OUT[h * HEAD:(h + 1) * HEAD, i * P:(i + 1) * P]
                order = sorted(enumerate(tiles[i]), key=lambda block: -block[1][2])
                for n, (at, (place, _, size)) in enumerate(order):
                    mm = pe.matmul(out, v[0:size, place * P + h * HEAD:place * P + (h + 1) * HEAD],
                                   PT[0:size, i * T + at * P:i * T + (at + 1) * P], start=(n == 0), stop=(n == len(order) - 1))
                mm.then_inc(out_full, c.add(out_full))

            def ffn(label):
                for half in range(2):
                    if half == 0:
                        gemm_as_ready(next_panel(), eight, x_tiles, [c.next(operand_ready) for _ in eight])
                        sum_squares()
                        gemm(next_panel(), eight, x_tiles)
                    with c.loop(f"up{label}{half}", HALF_FT - 1 if half == 0 else HALF_FT):
                        gemm(next_panel(), eight, x_tiles)
                        gemm(next_panel(), eight, x_tiles)
                    c.skip(operand_ready, HALF_FT)
                    with c.loop(f"down{label}{half}", KD // 2):
                        pe.wait_ge(operand_ready, c.now(operand_ready, -1))
                        gemm_as_ready(next_panel(), range(HALF_FT), a_tiles, [c.now(operand_ready)])
                        gemm(next_panel(), range(HALF_FT), a_tiles)

            def experts(e):
                pe.wait_ge(select_ready, c.next(select_ready))
                pe.wait_ge(added, c.now(added))
                for j, bank in enumerate((OUT, DEN)):
                    for t in range(QT):
                        mm = pe.transpose(bank[:, t * P:(t + 1) * P], f32(tile(SEL, t * PAIR + j, P)), IDENT[:, :])
                    mm.then_inc(select_turned, c.add(select_turned))
                for j in range(PAIR):
                    for t in range(QT):
                        mm = pe.matmul(GEMM[0][:, j:j + 1], f32(tile(SEL, t * PAIR + j, P)),
                                       SHARE[:, bass.ds(e * PAIR + (t * (EXPERTS + PAIR) + j), 1)], start=(t == 0), stop=(t == QT - 1))
                mm.then_inc(shares_ready, c.add(shares_ready))
                for q, bank in enumerate((*SCORE, *TURN)):
                    for k in range(2):
                        d = 2 * q + k
                        for t in range(QT):
                            for half in (XTH, XTL):
                                mm = pe.matmul(bank[:, k * PAIR * P:(k + 1) * PAIR * P], half[:, t * D + d * P:t * D + (d + 1) * P],
                                               tile(SEL, t, PAIR * P), start=(t == 0 and half is XTH), stop=(t == QT - 1 and half is XTL))
                    mm.then_inc(gathered, c.add(gathered))
                for j, (gates, *ups) in enumerate(((TURN[0], TURN[1], SCORE[0]), (SCORE[1], *GEMM))):
                    for p in range(2 * FT_MOE):
                        up, f = divmod(p, FT_MOE)
                        ps = gates[:, f * P:(f + 1) * P] if not up else ups[f // 2][:, f % 2 * P:(f % 2 + 1) * P]
                        at = (j * 2 * FT_MOE + p) % E_SLOTS
                        pe.wait_ge(weights_in[at], c.next(weights_in[at], 16))
                        if j == 0 and p == 0:
                            for q in range(4):
                                pe.wait_ge(gathered_taken[q % 2], c.next(gathered_taken[q % 2]))
                        for k in range(KD):
                            mm = pe.matmul(ps, tile(E_PANEL[at], k, P), tile(XG, k * PAIR + j, P), start=(k == 0), stop=(k == KD - 1))
                        mm.then_inc(panel_done, c.add(panel_done))
                pe.wait_ge(slots_turned, c.next(slots_turned, PAIR))
                for j in range(PAIR):
                    for half, ps in enumerate((OUT, DEN)):
                        if j == 1:
                            pe.wait_ge(result_ready, c.next(result_ready))
                        for f in range(FT_MOE):
                            at = ((PAIR * 2 + j) * FT_MOE + f) % E_SLOTS
                            if half == 0:
                                if f % 2 == 0:
                                    pe.wait_ge(hidden_ready, c.next(hidden_ready))
                                pe.wait_ge(weights_in[at], c.next(weights_in[at], 16))
                            mm = pe.matmul(ps[:, :], tile(HID[j], f, P), tile(E_PANEL[at], half), start=(f == 0), stop=(f == FT_MOE - 1))
                            if half == 1:
                                mm.then_inc(panel_done, c.add(panel_done))
                            elif f == FT_MOE - 1:
                                mm.then_inc(half_done, c.add(half_done))
                for d in range(KD):
                    if d % (KD // 2) == 0:
                        pe.wait_ge(result_ready, c.next(result_ready))
                    pe.wait_ge(added, c.now(added, -1))
                    c.skip(added)
                    for j in range(PAIR):
                        for half in (YH, YL):
                            mm = pe.matmul(GEMM[d % 2][:, :], half[:, j * D + d * P:j * D + (d + 1) * P], SLOTS_T[j],
                                           start=(j == 0 and half is YH), stop=(j == 1 and half is YL))
                    mm.then_inc(scattered, c.add(scattered))

            sum_squares(MEM)
            pe.wait_ge(operand_ready, c.next(operand_ready, KD))
            for pair in range(XPAIRS):
                gemm(next_panel(), eight, mem_tiles, MEM)
                gemm(next_panel(), eight, mem_tiles, MEM)
                if pair == 0:
                    pe.wait_ge(consts_in, c.next(consts_in, 5 * 16))
                pe.wait_ge(gemm_taken, c.now(gemm_taken))
                turn(VT, range(MEM // P))
            sum_squares()
            pe.wait_ge(operand_ready, c.next(operand_ready, KD))
            gemm(next_panel(), eight, x_tiles)
            gemm(next_panel(), eight, x_tiles)
            gemm(next_panel(), eight, x_tiles)
            gemm(next_panel(), eight, x_tiles)
            pe.wait_ge(turn_ready, c.next(turn_ready))
            turn(VB, range(QT), M_HEADS)
            begun = []

            def mixer(last):
                pe.wait_ge(gemm_taken, c.now(gemm_taken))
                turn(VT, range(QT))
                gemm(next_panel(), eight, x_tiles)
                gemm(next_panel(), eight, x_tiles)
                gemm(next_panel(), eight, x_tiles)
                pe.wait_ge(gemm_taken, c.now(gemm_taken, -1))
                pe.matmul(score_bank()[:, :], ROT[:, :], QB[:, :], start=True, stop=True).then_inc(scores_full, c.add(scores_full))
                pe.matmul(score_bank()[:, :], ROT[:, :], KB[:, :], start=True, stop=True).then_inc(scores_full, c.add(scores_full))
                pe.wait_ge(gemm_taken, c.now(gemm_taken))
                turn(VT, range(QT))
                pe.wait_ge(conv_ready, c.next(conv_ready))
                pe.wait_ge(heads_in, c.next(heads_in, 16))
                for j in range(2):
                    pe.matmul(score_bank()[:, :], WQK[:, j * P:(j + 1) * P], C,
                                                    start=True, stop=True).then_inc(scores_full, c.add(scores_full))
                pe.wait_ge(qk_ready, c.next(qk_ready))
                attention(CAUSAL, VB, {2: lambda: gemm(next_panel(), eight, x_tiles)})
                if not last:
                    gemm(next_panel(), eight, x_tiles)
                for at in (0, 32):
                    pe.wait_ge(rows_ready, c.next(rows_ready))
                    pe.matmul(score_bank()[:, :], ONES[at:at + M_HEADS, :],
                                                    TB[at:at + M_HEADS, :], start=True, stop=True).then_inc(scores_full, c.add(scores_full))
                pe.wait_ge(scores_taken, c.now(scores_taken))
                for j in range(QT):
                    pe.matmul(score_bank()[:, j * P:T], MK[:, j * P:(j + 1) * P],
                                                    MQ[:, j * P:T], start=True, stop=True).then_inc(scores_full, c.add(scores_full))
                pe.wait_ge(out_taken, c.now(out_taken))
                c.skip(out_taken)
                den_bank()
                for j in range(QT):
                    pe.wait_ge(scores_taken, c.now(scores_taken, j + 1 - QT))
                    w = PT[:, j * T + j * P:(j + 1) * T]
                    num = pe.matmul(OUT[:, j * P:T], MV[:, j * P:(j + 1) * P], w, start=(j == 0), stop=(j == QT - 1))
                    den = pe.matmul(DEN[:, j * P:T], ONES[:, :], w, start=(j == 0), stop=(j == QT - 1))
                num.then_inc(out_full, c.add(out_full))
                den.then_inc(den_full, c.add(den_full))
                if not last:
                    gemm(next_panel(), eight, x_tiles)
                else:
                    pe.wait_ge(operand_ready, c.now(operand_ready))
                    for _ in range(2):
                        w, ps = next_panel(), gemm_bank()
                        products(ps, w, eight[:-1], a_tiles[:KD - 1], end=False)
                        begun.append((w, ps))
                pe.wait_ge(sumsq_ready, c.next(sumsq_ready))
                pe.matmul(den_bank()[:, :], ONES[:, :], TB[:, :], start=True, stop=True).then_inc(den_full, c.add(den_full))
                c.skip(operand_ready)
            with c.loop("mix1", PAIRS - 1):
                mixer(last=False)
            mixer(last=True)
            pe.wait_ge(operand_ready, c.now(operand_ready))
            for w, ps in begun:
                products(ps, w, eight[-1:], a_tiles[KD - 1:KD], begin=False).then_inc(gemm_done, c.add(gemm_done))
            pe.wait_ge(out_taken, c.now(out_taken))
            with c.loop("wout", KD // 2 - 1):
                gemm(next_panel(), eight, a_tiles)
                gemm(next_panel(), eight, a_tiles)
            for pair in range(XPAIRS):
                if pair == 0:
                    gemm_as_ready(next_panel(), eight, x_tiles, [c.next(operand_ready) for _ in eight])
                    sum_squares()
                else:
                    gemm(next_panel(), eight, x_tiles)
                pe.wait_ge(gemm_taken, c.now(gemm_taken))
                attention(CROSS, VX[:, pair * MEM:(pair + 1) * MEM],
                          k_src=KX[:, pair * MEM:(pair + 1) * MEM])
            pe.wait_ge(out_taken, c.now(out_taken))
            for half in range(2):
                w = next_panel()
                for d in range(KD // 2):
                    gemm(w, (2 * d, 2 * d + 1), a_tiles)
            gemm_as_ready(next_panel(), eight, x_tiles, [c.next(operand_ready) for _ in eight])
            sum_squares()
            pe.wait_ge(turn_ready, c.next(turn_ready))
            turn(TA, range(QT), GROUPS + EXPERTS)
            for d in range(KD):
                pe.wait_ge(xn_ready, c.next(xn_ready))
                turn(tile(XN, d), range(QT))
            pe.wait_ge(mask_ready, c.next(mask_ready))
            ps = score_bank()
            mask = [TB[:, 192 + t * EXPERTS:192 + (t + 1) * EXPERTS] for t in range(QT)]
            for t in range(QT):
                rank = ps[:, t * EXPERTS:(t + 1) * EXPERTS]
                for s in range(t):
                    pe.matmul(rank, ONES[:, :], mask[s], start=(s == 0), stop=False)
                mm = pe.matmul(rank, BEFORE, mask[t], start=(t == 0), stop=True)
                if t == 0:
                    mm.then_inc(panel_done, c.add(panel_done, E_SLOTS))
            for t in range(QT):
                pe.matmul(ps[:, QT * EXPERTS:(QT + 1) * EXPERTS], ONES[:, :], mask[t], start=(t == 0), stop=(t == QT - 1))
            pe.matmul(ps[:, P:2 * P], ONES[:, :], BEFORE, start=True, stop=True).then_inc(scores_full, c.add(scores_full))
            pe.wait_ge(low_ready, c.next(low_ready, KD))
            pe.wait_ge(rounds_ready, c.next(rounds_ready))
            rounds = pe.value_load(ROUNDS, min_val=1, max_val=QT)
            with c.loop("rounds", rounds):
                with c.loop("experts", EXPERTS // PAIR) as e:
                    experts(e)
            sum_squares()
            pe.wait_ge(dft_in, c.next(dft_in, 3 * 16))
            with c.loop("layers", LAYERS):
                ffn("a")
                pe.wait_ge(operand_ready, c.next(operand_ready, KD))
                sum_squares()
                with c.loop("na", PAIRS):
                    gemm(next_panel(), eight, x_tiles)
                    gemm(next_panel(), eight, x_tiles)
                    gemm(next_panel(), eight, x_tiles)
                    gemm(next_panel(), eight, x_tiles)
                    pe.wait_ge(gemm_taken, c.now(gemm_taken, -1))
                    for part in (NEAR_BLOCKS[1::-1], NEAR_BLOCKS[2:]):
                        ps = turn_bank()
                        for place, key, size in part:
                            at = (place - min(part)[0]) * P
                            mm = pe.transpose(ps[0:size, at:at + P], VT[:, key:key + size], IDENT[:, :])
                        mm.then_inc(turned_full, c.add(turned_full))
                    pe.wait_ge(gemm_taken, c.now(gemm_taken))
                    for b in range(2):
                        ps = score_bank()
                        for t in range(2):
                            mm = pe.matmul(ps[:, t * 2 * P:(t + 1) * 2 * P],
                                           UT[:, (2 * b + t) * P:(2 * b + t + 1) * P], CS[:, :],
                                           start=True, stop=True)
                        mm.then_inc(scores_full, c.add(scores_full))

                    def dft():
                        pe.wait_ge(scores_taken, c.now(scores_taken, -3))
                        den_bank()
                        for t in range(QT):
                            pe.matmul(DEN[:, :], AB[:, t * 2 * P:t * 2 * P + P], tile(CT, t),
                                      start=(t == 0), stop=False)
                            mm = pe.matmul(DEN[:, :], AB[:, t * 2 * P + P:(t + 1) * 2 * P], tile(NST, t),
                                           start=False, stop=(t == QT - 1))
                        mm.then_inc(den_full, c.add(den_full))

                    def gate():
                        gemm(next_panel(), eight, x_tiles)

                    attention(NEAR, VB, {1: gate, 2: dft, 4: gate, 6: gate, 8: gate})
                    c.skip(operand_ready)
                branches = c.now(operand_ready)
                with c.loop("comb", KD // 2):
                    pe.wait_ge(out_taken, c.now(out_taken))
                    pe.wait_ge(operand_ready, branches)
                    for d in range(2):
                        w = next_panel()
                        gemm(w, range(0, PAIRS), a_tiles[0:PAIRS])
                        gemm(w, range(PAIRS, 2 * PAIRS), a_tiles[PAIRS:KD])
                    c.skip(operand_ready, 2)
                with c.loop("wo", KD // 2):
                    pe.wait_ge(operand_ready, c.now(operand_ready))
                    gemm(next_panel(), eight, a_tiles[KD:])
                    gemm(next_panel(), eight, a_tiles[KD:])
                ffn("b")
            c.skip(operand_ready, KD)
            sum_squares()

        @block.scalar
        def _(act):
            c = Counts(act, "act", trips)
            c.skip(out_full)

            results = [1]

            def round_hi(width=PANEL, units=1):
                slot = c.at(split_hi) % 2
                act.wait_ge(raw_in[slot], c.next(raw_in[slot], 16))
                if c.at(gemm_done) > results[0]:
                    act.wait_ge(gemm_done, c.now(gemm_done, -results[0]))
                c.skip(gemm_done, units)
                results[0] = units
                act.copy(WH[slot][:, 0:width], RAW[slot][:, 0:width]).then_inc(split_hi, c.add(split_hi))

            def root(n=T):
                act.wait_ge(den_full, c.next(den_full))
                act.activation(RS[:, 0:n], DEN[:, 0:n], ACT.Sqrt, bias=SMALL[:, 14:15], scale=1.0 / D).then_inc(
                    std_ready, c.add(std_ready))

            def turned(dst, src_cols, rows=P):
                at = c.at(turned_full) % 2
                act.wait_ge(turned_full, c.next(turned_full))
                act.copy(dst, TURN[at][0:rows, src_cols]).then_inc(turned_taken, c.add(turned_taken))

            jobs = [(h, i) for h in range(2) for i in range(QT)]

            def attention(tiles, between=None):
                for u in range(len(jobs) + 2):
                    if u >= 2:
                        h, i = jobs[u - 2]
                        n = len(tiles[i]) * P
                        act.wait_ge(out_full, c.now(out_full))
                        if u >= len(jobs) // 2 + 1:
                            c.skip(out_full)
                        turned(PT[:, i * T:i * T + n], slice(0, n))
                    if u < len(jobs):
                        h, i = jobs[u]
                        act.wait_ge(logits_ready, c.next(logits_ready))
                        p = PROB[u % 2][:, 0:span(tiles[i])[1]]
                        act.activation(p, p, ACT.Exp, bias=SMALL[:, u % 2:u % 2 + 1],
                                       accum_out=SMALL[:, 2 + u % 2:3 + u % 2]).then_inc(exp_done, c.add(exp_done))
                    if between and u in between:
                        between[u]()
                c.skip(out_full, len(jobs) // 2 - 1)

            def table(func):
                act.activation(SMALL[:, 13:14], SMALL[:, 13:14], func)

            def silu_unit(off=-1):
                act.wait_ge(gemm_taken, c.now(gemm_done, off))
                act.activation(TB[:, :], TA[:, :], ACT.Silu).then_inc(act_out, c.add(act_out))

            def sigmoid_unit(dst, src, off, **bias):
                act.wait_ge(gemm_taken, c.now(gemm_done, off))
                act.activation(dst, src, ACT.Sigmoid, **bias).then_inc(act_out, c.add(act_out))

            def ffn(label):
                for half in range(2):
                    if half == 0:
                        round_hi()
                        round_hi()
                        root()
                        table(ACT.Silu)
                        with c.loop(f"up{label}{half}", HALF_FT - 1):
                            round_hi()
                            silu_unit(-2)
                            round_hi()
                        silu_unit()
                    else:
                        with c.loop(f"up{label}{half}", HALF_FT):
                            round_hi()
                            round_hi()
                            silu_unit()
                    with c.loop(f"down{label}{half}", KD // 2):
                        round_hi(WIDE)
                        round_hi(WIDE)

            act.wait_ge(mem_in, c.next(mem_in, 16))
            act.activation(GATE_A[:, 0:KD * MEM], PT[:, 0:KD * MEM], ACT.Square).then_inc(squares_ready, c.add(squares_ready))
            round_hi()
            round_hi()
            act.wait_ge(x_in, c.next(x_in, 16))
            act.activation(GATE_B, X[:, :], ACT.Square).then_inc(squares_ready, c.add(squares_ready))
            root(MEM)
            for pair in range(XPAIRS):
                if pair:
                    round_hi()
                    round_hi()
                turned(VX[:, pair * MEM:(pair + 1) * MEM], slice(0, MEM))
            round_hi()
            round_hi()
            root()
            round_hi()
            round_hi()
            act.wait_ge(sin_ready, c.next(sin_ready))
            act.activation(SIN, SIN, ACT.Sin).then_inc(sin_done, c.add(sin_done))
            act.wait_ge(sin_ready, c.next(sin_ready))
            act.activation(COS, COS, ACT.Sin).then_inc(sin_done, c.add(sin_done))
            act.wait_ge(gate_ready, c.next(gate_ready))
            act.activation(TB[0:M_HEADS, :], TB[0:M_HEADS, :], ACT.Exp).then_inc(gate_done, c.add(gate_done))
            act.wait_ge(gate_ready, c.next(gate_ready))
            act.activation(TB[0:M_HEADS, :], TB[0:M_HEADS, :], ACT.Ln).then_inc(gate_done, c.add(gate_done))
            act.wait_ge(gate_ready, c.next(gate_ready))
            act.activation(GATE[32:32 + M_HEADS, :], GATE[32:32 + M_HEADS, :], ACT.Exp, scale=-1.0).then_inc(gate_done, c.add(gate_done))
            round_hi()
            turned(SMALL[:, 16:16 + QT * M_HEADS], slice(0, QT * M_HEADS))
            round_hi()
            def mixer(m, last):
                turned(MV, slice(0, T))
                round_hi()
                act.wait_ge(conv_done, c.next(conv_done))
                act.activation(SG, C, ACT.Sigmoid).then_inc(act_out, c.add(act_out))
                round_hi()
                turned(VB[:, 0:T], slice(0, T))
                attention(CAUSAL, {3: round_hi, 5: round_hi, 6: lambda: sigmoid_unit(SG, TA[:, :], -2)})
                act.wait_ge(out_full, c.now(out_full))
                for j in range(QT):
                    bias = SMALL[:, bass.ds(m + (16 + j * M_HEADS), 1)]
                    if j == 0:
                        act.wait_ge(m_args_ready, c.next(m_args_ready))
                    ins = act.activation(PT[:, j * T + j * P:j * T + (j + 1) * P], VT[:, j * P:(j + 1) * P], ACT.Exp, bias=bias)
                    if j < QT - 1:
                        ins = act.activation(PT[:, j * T + (j + 1) * P:(j + 1) * T], U[:, (j + 1) * P:T], ACT.Exp, bias=bias)
                    ins.then_inc(m_exp_ready, c.add(m_exp_ready))
                c.skip(out_full)
                if not last:
                    round_hi()
                    round_hi()
                c.skip(den_full)
                act.wait_ge(den_full, c.next(den_full))
                act.activation(TB[:, :], DEN[:, :], ACT.Sqrt, bias=SMALL[:, 14:15], scale=1.0 / P).then_inc(std_ready, c.add(std_ready))
            with c.loop("mix1", PAIRS - 1) as m:
                mixer(m, last=False)
            mixer(PAIRS - 1, last=True)
            with c.loop("wout", KD // 2 - 1):
                round_hi()
                round_hi()
            round_hi()
            root()
            for pair in range(XPAIRS):
                if pair == 0:
                    round_hi()
                attention(CROSS)
            for half in range(2):
                round_hi(units=KD // 2)
            round_hi()
            root()
            turned(QB[:, 0:QT * (GROUPS + EXPERTS)], slice(0, QT * (GROUPS + EXPERTS)))
            c.skip(panel_done, E_SLOTS)
            for d in range(KD):
                at = c.at(turned_full) % 2
                act.wait_ge(turned_full, c.next(turned_full))
                bank = TURN[at][:, :].rearrange("p (t f) -> p t f", t=QT)
                whole, high = (ap.rearrange("p (t f) -> p t f", t=QT)[:, :, d * P:(d + 1) * P] for ap in (XT, XTH))
                act.copy(whole, bank).then_inc(turned_taken, c.add(turned_taken))
                act.wait_ge(turned_taken, c.now(turned_taken))
                act.copy(high, whole).then_inc(turned_copied, c.add(turned_copied))
            for k in range(2):
                act.wait_ge(route_args, c.next(route_args))
                ap = SMALL[:, 0:QT] if k else TA[:, 0:QT * GROUPS]
                act.activation(ap, ap, ACT.Exp).then_inc(route_done, c.add(route_done))
            act.wait_ge(rounds_ready, c.next(rounds_ready))
            rounds = act.value_load(ROUNDS, min_val=1, max_val=QT)
            table(ACT.Silu)
            with c.loop("rounds", rounds):
                with c.loop("experts", EXPERTS // PAIR):
                    for j, bank in enumerate((OUT, DEN)):
                        act.wait_ge(select_turned, c.next(select_turned))
                        act.copy(SLOTS_T[j], bank[:, :]).then_inc(slots_turned, c.add(slots_turned))
                    for q, bank in ((0, SCORE[0]), (2, TURN[0])):
                        act.wait_ge(gathered, c.next(gathered))
                        act.copy(tile(XG, q), bank[:, :]).then_inc(gathered_taken0, c.add(gathered_taken0))
                        c.skip(gathered)
                    for j, bank in enumerate((TURN[0], SCORE[1])):
                        act.wait_ge(panel_done, c.next(panel_done, FT_MOE))
                        act.activation(GACT[j], bank[:, :], ACT.Silu).then_inc(gate_act, c.add(gate_act))
                        c.skip(panel_done, FT_MOE)
                    act.wait_ge(shares_taken, c.next(shares_taken))
                    for j in range(PAIR):
                        share = SLOT_SHARE[:, j:j + 1]
                        act.wait_ge(half_done, c.next(half_done))
                        act.activation(tile(YH, 2 * j), OUT[:, :], ACT.Copy, scale=share).then_inc(result_high, c.add(result_high))
                        act.wait_ge(panel_done, c.next(panel_done, FT_MOE))
                        act.activation(tile(YH, 2 * j + 1), DEN[:, :], ACT.Copy, scale=share).then_inc(result_high, c.add(result_high))
            table(ACT.Sqrt)
            act.wait_ge(experts_done, c.next(experts_done))
            act.activation(XN, X[:, :], ACT.Square).then_inc(squares_ready, c.add(squares_ready))
            root()
            for k in range(KD):
                act.wait_ge(normed, c.next(normed))
                act.activation(tile(XH, k), tile(XN, k), ACT.Copy, scale=vec("gains2", k)).then_inc(high_ready, c.add(high_ready))
                act.activation(tile(GATE_A, k), tile(XN, k), ACT.Square).then_inc(squares_ready, c.add(squares_ready))
            with c.loop("layers", LAYERS) as l:
                ffn("a")
                round_hi()
                round_hi()
                root()
                table(ACT.Exp)
                with c.loop("na", PAIRS):
                    round_hi()
                    round_hi()
                    turned(VB[:, 0:2 * P], slice(0, 2 * P))
                    turned(VB[:, 2 * P:], slice(0, 3 * P))
                    round_hi()
                    round_hi()
                    c.skip(den_full)
                    attention(NEAR, {2: round_hi, 5: round_hi, 7: round_hi, 8: round_hi})
                act.wait_ge(gemm_taken, c.now(gemm_done, -2))
                c.skip(gemm_done, 2)
                results[0] = 2
                table(ACT.Sigmoid)
                with c.loop("comb", KD // 2) as d:
                    def gate_bias(s, j):
                        return VEC[:, bass.ds(l * 16 + (d * 2) + (col["gate_b"] + 8 * s + j), 1)]

                    for j in range(2):
                        for g, gates in enumerate((GATE_A, GATE_B)):
                            gate = tile(gates, d * 2 + j)
                            act.activation(gate, gate, ACT.Sigmoid, bias=gate_bias(g, j)).then_inc(act_out, c.add(act_out))
                        round_hi(units=2)
                c.skip(gemm_done, -2)
                results[0] = 1
                with c.loop("wo", KD // 2 - 1):
                    round_hi()
                    round_hi()
                ffn("b")
            root()

        @block.vector
        def _(v):
            c = Counts(v, "dve", trips)

            def step(ins):
                ins.then_inc(dve_step, c.add(dve_step))

            def chain(ins):
                ins.then_inc(dve_step, c.add(dve_step))
                v.wait_ge(dve_step, c.now(dve_step))

            def prep(x, gain, hi, lo, n=T):
                step(v.tensor_tensor(TA[:, 0:n], x, x, ALU.mult))
                chain(v.tensor_scalar(hi, x, gain, None, ALU.mult))
                v.scalar_tensor_tensor(lo, x, gain, f32(hi), ALU.mult, ALU.subtract).then_inc(operand_ready, c.add(operand_ready))
                v.tensor_tensor(SQ[:, 0:n], SQ[:, 0:n], TA[:, 0:n], ALU.add).then_inc(sumsq_ready, c.add(sumsq_ready))
                v.wait_ge(sumsq_ready, c.now(sumsq_ready))

            def clear_squares():
                step(v.memset(SQ[:, :], 0.0))

            def scores_in():
                at = c.at(scores_full) % 2
                v.wait_ge(scores_full, c.next(scores_full))
                return SCORE[at]

            def den_in():
                v.wait_ge(den_full, c.next(den_full))
                return DEN

            def rstd(n=T):
                c.skip(den_full)
                v.wait_ge(std_ready, c.next(std_ready))
                v.reciprocal(RS[:, 0:n], RS[:, 0:n]).then_inc(den_taken, c.add(den_taken))

            def fold(squares, n=T):
                chain(v.tensor_tensor(squares[:, 0:4 * n], squares[:, 0:4 * n], squares[:, 4 * n:8 * n], ALU.add))
                chain(v.tensor_tensor(squares[:, 0:2 * n], squares[:, 0:2 * n], squares[:, 2 * n:4 * n], ALU.add))
                v.tensor_tensor(SQ[:, 0:n], squares[:, 0:n], squares[:, n:2 * n], ALU.add).then_inc(sumsq_ready, c.add(sumsq_ready, KD))

            def high(x, gain, hi, n=T):
                for k in range(KD):
                    step(v.tensor_scalar(tile(hi, k, n), tile(x, k, n), vec(gain, k), None, ALU.mult))

            def low(x, gain, hi, lo, n=T):
                v.wait_ge(dve_step, c.now(dve_step))
                for k in range(KD):
                    v.scalar_tensor_tensor(tile(lo, k, n), tile(x, k, n), vec(gain, k), f32(tile(hi, k, n)),
                                           ALU.mult, ALU.subtract).then_inc(operand_ready, c.add(operand_ready))

            def gemm_in(n=T):
                at = c.at(gemm_done) % 2
                v.wait_ge(gemm_done, c.next(gemm_done))
                return GEMM[at][:, 0:n]

            def take(dst, scale=1.0, by=None, n=T):
                ps = gemm_in(n)
                by = RS[:, 0:n] if by is None else by
                v.scalar_tensor_tensor(dst, ps, scale, by, ALU.mult, ALU.mult).then_inc(gemm_taken, c.add(gemm_taken))

            def add_to(x, scale=1.0):
                ps = gemm_in()
                v.scalar_tensor_tensor(x, ps, scale, x, ALU.mult, ALU.add).then_inc(gemm_taken, c.add(gemm_taken))
                v.wait_ge(gemm_taken, c.now(gemm_taken))

            def halves(hi, lo, src):
                chain(v.tensor_copy(hi, src))
                v.tensor_tensor(lo, src, f32(hi), ALU.subtract).then_inc(operand_ready, c.add(operand_ready))

            jobs = [(h, i) for h in range(2) for i in range(QT)]

            def attention(tiles, bias, hi, lo, between=None):
                for u in range(len(jobs) + 1):
                    if u < len(jobs):
                        h, i = jobs[u]
                        n = span(tiles[i])[1]
                        prob = PROB[u % 2][:, 0:n]
                        if u >= 2:
                            v.wait_ge(turned_full, c.next(turned_full))
                        ps = scores_in()[:, 0:n]
                        if bias is None:
                            v.tensor_copy(prob, ps).then_inc(scores_taken, c.add(scores_taken))
                        else:
                            v.tensor_tensor(prob, ps, bias(h, i), ALU.add).then_inc(scores_taken, c.add(scores_taken))
                        v.wait_ge(scores_taken, c.now(scores_taken))
                        v.tensor_reduce(SMALL[:, u % 2:u % 2 + 1], prob, AX_X, ALU.max, negate=True).then_inc(
                            logits_ready, c.add(logits_ready))
                    if u >= 1:
                        s = (u - 1) % 2
                        v.wait_ge(exp_done, c.next(exp_done))
                        chain(v.reciprocal(SMALL[:, 4 + s:5 + s], SMALL[:, 2 + s:3 + s]))
                        v.tensor_scalar(DIAG[s], IDENT[:, :], SMALL[:, 4 + s:5 + s], None, ALU.mult).then_inc(
                            probs_ready, c.add(probs_ready))
                    if between and u in between:
                        between[u]()
                v.wait_ge(turned_full, c.next(turned_full, 2))
                v.wait_ge(out_full, c.next(out_full, len(jobs)))
                chain(v.tensor_copy(hi, OUT[:, :]))
                v.tensor_tensor(lo, OUT[:, :], f32(hi), ALU.subtract).then_inc(out_taken, c.add(out_taken))

            def ffn(label, gain):
                rstd()
                for half in range(2):
                    with c.loop(f"up{label}{half}", HALF_FT) as f:
                        v.wait_ge(den_taken, c.now(den_taken))
                        v.wait_ge(gemm_taken, c.now(gemm_taken))
                        hidden_unit(tile(AH, f), tile(AL, f), RS[:, :])
                    if half == 0:
                        with c.loop(f"down{label}{half}", KD // 2) as d:
                            add_to(tile(X, d * 2), 0.5)
                            add_to(tile(X, d * 2 + 1), 0.5)
                    else:
                        clear_squares()
                        with c.loop(f"down{label}{half}", KD // 2) as d:
                            v.wait_ge(dve_step, c.now(dve_step))
                            for j in range(2):
                                e = d * 2 + j
                                add_to(tile(X, e), 0.5)
                                prep(tile(X, e), gain(e), tile(XH, e), tile(XL, e))

            def hidden_unit(hi, lo, by):
                take(TA[:, :])
                take(PROB[0][:, :], by=by)
                v.wait_ge(act_out, c.next(act_out))
                v.wait_ge(gemm_taken, c.now(gemm_taken))
                chain(v.tensor_tensor(PROB[0][:, :], PROB[0][:, :], TB[:, :], ALU.mult))
                halves(hi, lo, PROB[0][:, :])
                v.wait_ge(operand_ready, c.now(operand_ready))

            v.memset(ONES[:, :], 1.0).then_inc(out_taken, c.add(out_taken))
            v.memset(PADU[:, 0:4], 0.0).then_inc(den_taken, c.add(den_taken))
            v.memset(SMALL[:, 0:14], 0.0).then_inc(out_full, c.add(out_full))
            chain(v.memset(SMALL[:, 14:15], EPS))
            v.wait_ge(vec_in, c.next(vec_in, 16))
            v.wait_ge(mem_in, c.next(mem_in, 16))
            high(PT, "g_mem", AH, MEM)
            v.wait_ge(squares_ready, c.next(squares_ready))
            fold(GATE_A, MEM)
            low(PT, "g_mem", AH, AL, MEM)
            v.wait_ge(x_in, c.next(x_in, 16))
            high(X, "g_mix", XH)
            rstd(MEM)
            v.wait_ge(den_taken, c.now(den_taken))
            for pair in range(XPAIRS):
                take(KX[:, pair * MEM:(pair + 1) * MEM], n=MEM)
                if pair:
                    v.wait_ge(turned_full, c.next(turned_full))
                take(VT[:, 0:MEM], n=MEM)
                if pair == 0:
                    low(X, "g_mix", XH, XL)
            v.wait_ge(squares_ready, c.next(squares_ready))
            fold(GATE_B)
            rstd()
            v.wait_ge(pos_in, c.next(pos_in, 16))
            v.wait_ge(consts_in, c.next(consts_in, 5 * 16))
            chain(v.tensor_copy(VB[:, 0:T], TB[:, :].bitcast(I32)))
            chain(v.tensor_scalar(VB[:, 0:T], VB[:, 0:T], vec("invf"), None, ALU.mult))
            chain(v.tensor_scalar(TB[:, :], VB[:, 0:T], float(np.float32(1 / (2 * np.pi))), None, ALU.mult))
            chain(v.tensor_scalar(TB[:, :], TB[:, :], 12582912.0, None, ALU.add))
            chain(v.tensor_scalar(TB[:, :], TB[:, :], -12582912.0, None, ALU.add))
            for part in TWO_PI_PARTS:
                chain(v.scalar_tensor_tensor(VB[:, 0:T], TB[:, :], -part, VB[:, 0:T], ALU.mult, ALU.add))
            v.tensor_scalar(SIN, VB[:, 0:T], PI_LOW, -PI_LOW, ALU.min, ALU.max).then_inc(sin_ready, c.add(sin_ready))
            chain(v.tensor_scalar(VB[:, 0:T], VB[:, 0:T], float(np.pi / 2), None, ALU.add))
            chain(v.tensor_scalar(TB[:, :], VB[:, 0:T], float(np.pi), float(-2 * np.pi), ALU.is_gt, ALU.mult))
            chain(v.tensor_tensor(VB[:, 0:T], VB[:, 0:T], TB[:, :], ALU.add))
            v.tensor_scalar(COS, VB[:, 0:T], PI_LOW, -PI_LOW, ALU.min, ALU.max).then_inc(sin_ready, c.add(sin_ready))
            v.wait_ge(sin_ready, c.now(sin_ready))
            H4 = slice(0, M_HEADS)
            ig, fg, mn, one = VB[H4, 0:T], PROB[0][H4, :], PROB[1][H4, :], KB[H4, :]
            for dst, b in ((ig, "b_i"), (fg, "b_f")):
                ps = gemm_in()
                v.tensor_tensor(dst, ps[H4, :], RS[H4, :], ALU.mult).then_inc(gemm_taken, c.add(gemm_taken))
                v.wait_ge(gemm_taken, c.now(gemm_taken))
                chain(v.tensor_scalar(dst, dst, vec(b)[H4, :], None, ALU.add))
            step(v.memset(one, 0.0))
            chain(v.tensor_scalar(mn, fg, 0.0, None, ALU.min))
            v.scalar_tensor_tensor(TB[H4, :], mn, 2.0, fg, ALU.mult, ALU.subtract).then_inc(gate_ready, c.add(gate_ready))
            take(PADU[:, 4:4 + T])
            v.wait_ge(gate_done, c.next(gate_done))
            v.tensor_scalar(TB[H4, :], TB[H4, :], 1.0, None, ALU.add).then_inc(gate_ready, c.add(gate_ready))
            v.wait_ge(turned_full, c.next(turned_full))
            take(VT[:, :])
            v.wait_ge(gate_done, c.next(gate_done))
            chain(v.tensor_tensor(fg, mn, TB[H4, :], ALU.subtract))
            chain(v.tensor_tensor_scan(mn, fg, one, 0.0, ALU.add, ALU.add))
            v.tensor_tensor(ig, ig, mn, ALU.subtract).then_inc(turn_ready, c.add(turn_ready))
            v.wait_ge(turn_ready, c.now(turn_ready))
            chain(v.tensor_tensor_scan(fg, ig, ig, 0.0, ALU.max, ALU.max))
            chain(v.tensor_scalar(GATE[H4, :], fg, -1.0, None, ALU.mult))
            chain(v.tensor_tensor(mn, mn, fg, ALU.add))
            v.tensor_copy(GATE[32:32 + M_HEADS, :], mn).then_inc(gate_ready, c.add(gate_ready))
            v.wait_ge(gate_done, c.next(gate_done))
            v.wait_ge(turned_full, c.next(turned_full))
            v.wait_ge(sin_done, c.next(sin_done, 2))
            def mixer(m, last):
                def mv(name, j):
                    return VEC[:, bass.ds(m * 8 + (col["mvec"] + j), 1)]

                take(QB[:, :], ATT_SCALE)
                v.wait_ge(gemm_taken, c.now(gemm_taken))
                chain(v.tensor_scalar(C, PADU[:, 1:1 + T], mv("w", 0), mv("b", 4), ALU.mult, ALU.add))
                for j in range(1, 3):
                    chain(v.scalar_tensor_tensor(C, PADU[:, 1 + j:1 + j + T], mv("w", j), C, ALU.mult, ALU.add))
                v.scalar_tensor_tensor(C, PADU[:, 4:4 + T], mv("w", 3), C, ALU.mult, ALU.add).then_inc(conv_done, c.add(conv_done))
                take(KB[:, :])
                v.wait_ge(act_out, c.next(act_out))
                v.tensor_tensor(C, C, SG, ALU.mult).then_inc(conv_ready, c.add(conv_ready))
                v.wait_ge(turned_full, c.next(turned_full))
                take(VT[:, :])
                v.wait_ge(gemm_taken, c.now(gemm_taken))
                for j, buf in enumerate((QB, KB)):
                    ps = scores_in()
                    v.tensor_tensor(TA[:, :], ps[:, :], SIN, ALU.mult).then_inc(scores_taken, c.add(scores_taken))
                    chain(v.tensor_tensor(buf[:, :], buf[:, :], COS, ALU.mult))
                    if j == 0:
                        chain(v.tensor_tensor(buf[:, :], buf[:, :], TA[:, :], ALU.add))
                    else:
                        v.tensor_tensor(buf[:, :], buf[:, :], TA[:, :], ALU.add).then_inc(qk_ready, c.add(qk_ready))
                for dst, scale in ((MQ, 1.0), (MK, M_SCALE)):
                    ps = scores_in()
                    v.tensor_scalar(dst, ps[:, :], scale, None, ALU.mult).then_inc(scores_taken, c.add(scores_taken))
                v.wait_ge(scores_taken, c.now(scores_taken))
                v.wait_ge(turned_full, c.next(turned_full))

                attention(CAUSAL, lambda h, i: LN[:, LN_AT[i]:LN_AT[i] + (i + 1) * P],
                          tile(AH, m), tile(AL, m), {4: lambda: take(TA[:, :])})
                v.wait_ge(act_out, c.next(act_out))
                for dst, at in ((U, 0), (ENM, 32)):
                    rows = slice(at, at + M_HEADS)
                    v.tensor_scalar(TB[rows, :], GATE[rows, :], IDENT[rows, bass.ds(m + at, 1)], None, ALU.mult).then_inc(rows_ready, c.add(rows_ready))
                    ps = scores_in()
                    v.tensor_copy(dst, ps[:, :]).then_inc(scores_taken, c.add(scores_taken))
                v.wait_ge(scores_taken, c.now(scores_taken))
                v.tensor_tensor(
                    VT[:, :].rearrange("p (j t) -> p j t", j=QT), U.rearrange("p (j t) -> p j t", j=QT),
                    TRI[:, :].unsqueeze(1).to_broadcast([P, QT, P]), ALU.add).then_inc(m_args_ready, c.add(m_args_ready))
                for j in range(QT):
                    ps = scores_in()
                    v.wait_ge(m_exp_ready, c.next(m_exp_ready))
                    w = PT[:, j * T + j * P:(j + 1) * T]
                    v.tensor_tensor(w, ps[:, j * P:T], w, ALU.mult).then_inc(scores_taken, c.add(scores_taken))
                if not last:
                    take(PADU[:, 4:4 + T])
                v.wait_ge(out_full, c.next(out_full))
                v.wait_ge(den_full, c.next(den_full))
                chain(v.tensor_scalar(TA[:, :], DEN[:, :], -1.0, None, ALU.mult))
                v.tensor_tensor(TA[:, :], DEN[:, :], TA[:, :], ALU.max).then_inc(den_taken, c.add(den_taken))
                v.wait_ge(den_taken, c.now(den_taken))
                chain(v.tensor_tensor(TA[:, :], TA[:, :], ENM, ALU.max))
                chain(v.reciprocal(TA[:, :], TA[:, :]))
                v.tensor_tensor(TA[:, :], OUT[:, :], TA[:, :], ALU.mult).then_inc(out_taken, c.add(out_taken))
                v.wait_ge(out_taken, c.now(out_taken))
                v.tensor_tensor(TB[:, :], TA[:, :], TA[:, :], ALU.mult).then_inc(sumsq_ready, c.add(sumsq_ready))
                if not last:
                    take(VT[:, :])
                c.skip(den_full)
                v.wait_ge(std_ready, c.next(std_ready))
                v.reciprocal(TB[:, :], TB[:, :]).then_inc(den_taken, c.add(den_taken))
                v.wait_ge(den_taken, c.now(den_taken))
                chain(v.scalar_tensor_tensor(TA[:, :], TA[:, :], mv("g", 5), TB[:, :], ALU.mult, ALU.mult))
                chain(v.scalar_tensor_tensor(TA[:, :], C, mv("skip", 6), TA[:, :], ALU.mult, ALU.add))
                chain(v.tensor_tensor(TA[:, :], TA[:, :], SG, ALU.mult))
                halves(tile(AH, m + PAIRS), tile(AL, m + PAIRS), TA[:, :])
                v.wait_ge(operand_ready, c.now(operand_ready))
            with c.loop("mix1", PAIRS - 1) as m:
                mixer(m, last=False)
            mixer(PAIRS - 1, last=True)
            clear_squares()
            with c.loop("wout", KD // 2) as d:
                v.wait_ge(dve_step, c.now(dve_step))
                for j in range(2):
                    e = d * 2 + j
                    add_to(tile(X, e))
                    prep(tile(X, e), VEC[:, bass.ds(e + col["g_cross"], 1)], tile(XH, e), tile(XL, e))
            rstd()
            v.wait_ge(den_taken, c.now(den_taken))
            for pair in range(XPAIRS):
                take(QB[:, :], ATT_SCALE)
                attention(CROSS, None, tile(AH, pair), tile(AL, pair))
            clear_squares()
            v.wait_ge(dve_step, c.now(dve_step))
            for d in range(KD):
                add_to(tile(X, d))
                prep(tile(X, d), vec("g_ffn", d), tile(XH, d), tile(XL, d))
            rstd()
            v.wait_ge(den_taken, c.now(den_taken))
            NR = GROUPS + EXPERTS
            ps = gemm_in()
            v.tensor_tensor(TB[0:NR, :], ps[0:NR, :], RS[0:NR, :], ALU.mult).then_inc(gemm_taken, c.add(gemm_taken))
            v.wait_ge(gemm_taken, c.now(gemm_taken))
            v.tensor_scalar(TA[0:NR, :], TB[0:NR, :], vec("b_route")[0:NR, :], None, ALU.add).then_inc(turn_ready, c.add(turn_ready))
            for k in range(KD):
                v.scalar_tensor_tensor(tile(XN, k), tile(X, k), vec("g_ffn", k), RS[:, :], ALU.mult, ALU.mult).then_inc(
                    xn_ready, c.add(xn_ready))
            chain(v.tensor_scalar(BEFORE, TRI[:, :], 0.0, None, ALU.is_ge))
            chain(v.tensor_tensor(BEFORE, BEFORE, IDENT[:, :], ALU.subtract))
            v.wait_ge(turned_full, c.next(turned_full))
            v.wait_ge(turned_taken, c.now(turned_full))
            c.skip(turned_full, KD)

            def b3(ap, k):
                return ap.unsqueeze(2).to_broadcast([P, QT, k])

            LG = QB[:, 0:QT * NR].rearrange("p (t e) -> p t e", t=QT)
            lg, le = LG[:, :, 0:GROUPS], LG[:, :, GROUPS:NR]
            g4 = TA[:, 0:QT * GROUPS].rearrange("p (t e) -> p t e", t=QT)

            def e16(i):
                return TB[:, i * 64:(i + 1) * 64].rearrange("p (t e) -> p t e", t=QT)

            gmax, gsum, gw, first, v1, v2, w1, w2 = (SMALL[:, 4 * i:4 * i + 4] for i in range(4, 12))
            d2 = SMALL[:, 0:4]
            pen = TA[:, 32:48].rearrange("p (t e) -> p t e", t=QT)
            desc = vec("desc", 0, EXPERTS)

            def desc_b(k):
                return desc[:, EXPERTS - k:EXPERTS].unsqueeze(1).to_broadcast([P, QT, k])

            def first_of(hot, eq, k):
                chain(v.tensor_tensor(eq, eq, desc_b(k), ALU.mult))
                chain(v.tensor_reduce(first, eq, AX_X, ALU.max))
                chain(v.tensor_tensor(hot, eq, b3(first, k), ALU.is_equal))

            chain(v.tensor_reduce(gmax, lg, AX_X, ALU.max))
            v.tensor_tensor(g4, lg, b3(gmax, GROUPS), ALU.subtract).then_inc(route_args, c.add(route_args))
            chain(v.tensor_tensor(pen, lg, b3(gmax, GROUPS), ALU.is_equal))
            first_of(pen, pen, GROUPS)
            chain(v.tensor_scalar(pen, pen, -1.0, -NEG, ALU.add, ALU.mult))
            chain(v.tensor_tensor(
                TB[:, 0:64].rearrange("p (t g e) -> p t g e", t=QT, g=GROUPS),
                le.rearrange("p t (g e) -> p t g e", g=GROUPS),
                pen.unsqueeze(3).to_broadcast([P, QT, GROUPS, EXPERTS // GROUPS]), ALU.add))
            for k, (best, hot) in enumerate(((v1, e16(1)), (v2, e16(2)))):
                chain(v.tensor_reduce(best, e16(0), AX_X, ALU.max))
                chain(v.tensor_tensor(hot, e16(0), b3(best, EXPERTS), ALU.is_equal))
                first_of(hot, hot, EXPERTS)
                if k == 0:
                    chain(v.scalar_tensor_tensor(e16(0), hot, 2 * NEG, e16(0), ALU.mult, ALU.add))
            v.tensor_tensor(d2, v2, v1, ALU.subtract).then_inc(route_args, c.add(route_args))
            v.tensor_tensor(e16(3), e16(1), e16(2), ALU.add).then_inc(mask_ready, c.add(mask_ready))
            v.wait_ge(route_done, c.next(route_done, 2))
            chain(v.tensor_reduce(gsum, g4, AX_X, ALU.add))
            chain(v.reciprocal(gw, gsum))
            chain(v.tensor_scalar(w1, d2, 1.0, None, ALU.add))
            chain(v.reciprocal(w1, w1))
            chain(v.tensor_tensor(w1, w1, gw, ALU.mult))
            chain(v.tensor_tensor(w2, w1, d2, ALU.mult))
            chain(v.tensor_tensor(e16(1), e16(1), b3(w1, EXPERTS), ALU.mult))
            chain(v.tensor_tensor(e16(2), e16(2), b3(w2, EXPERTS), ALU.mult))
            rank3, share3 = (ap.rearrange("p (t e) -> p t e", t=QT) for ap in (RANK, SHARE))
            chain(v.tensor_tensor(share3[:, :, 0:EXPERTS], e16(1), e16(2), ALU.add))
            ps = scores_in()
            chain(v.tensor_reduce(gmax[:, 0:1], ps[:, QT * EXPERTS:(QT + 1) * EXPERTS], AX_X, ALU.max))
            step(v.tensor_copy(IOTA, ps[:, P:2 * P]))
            v.scalar_tensor_tensor(rank3[:, :, 0:EXPERTS], ps[:, 0:QT * EXPERTS].rearrange("p (t e) -> p t e", t=QT), 1.0,
                                   e16(3), ALU.add, ALU.mult).then_inc(scores_taken, c.add(scores_taken))
            v.wait_ge(scores_taken, c.now(scores_taken))
            chain(v.tensor_scalar(rank3[:, :, 0:EXPERTS], rank3[:, :, 0:EXPERTS], -1.0, None, ALU.add))
            step(v.tensor_scalar(rank3[:, :, EXPERTS:], rank3[:, :, 0:PAIR], float(-P), None, ALU.add))
            chain(v.tensor_scalar(first[:, 0:1], gmax[:, 0:1], float(P), 1.0, ALU.is_gt, ALU.add))
            for k in range(2, QT):
                chain(v.scalar_tensor_tensor(first[:, 0:1], gmax[:, 0:1], float(k * P), first[:, 0:1], ALU.is_gt, ALU.add))
            v.tensor_copy(ROUNDS, first[0:1, 0:1]).then_inc(rounds_ready, c.add(rounds_ready))
            v.wait_ge(rounds_ready, c.now(rounds_ready))
            rounds = v.value_load(ROUNDS, min_val=1, max_val=QT)

            def select(e):
                for t in range(QT):
                    for j in range(PAIR):
                        at = e * PAIR + (t * (EXPERTS + PAIR) + j)
                        rank = RANK[:, at:at + 1] if isinstance(at, int) else RANK[:, bass.ds(at, 1)]
                        ins = v.tensor_scalar(tile(SEL, t * PAIR + j, P), IOTA, rank, None, ALU.is_equal)
                        if (t, j) != (QT - 1, PAIR - 1):
                            ins.then_inc(select_step, c.add(select_step))
                ins.then_inc(select_ready, c.add(select_ready))

            v.memset(SMALL[:, 15:16], 0.0).then_inc(added, c.add(added, 2))
            select(0)
            c.skip(panel_done, E_SLOTS)
            with c.loop("rounds", rounds):
                with c.loop("experts", EXPERTS // PAIR) as e:
                    v.wait_ge(shares_ready, c.next(shares_ready))
                    v.tensor_copy(SLOT_SHARE, GEMM[0][:, 0:PAIR]).then_inc(shares_taken, c.add(shares_taken))
                    for q, bank in ((1, SCORE[1]), (3, TURN[1])):
                        v.wait_ge(gathered, c.next(gathered, 2))
                        v.tensor_copy(tile(XG, q), bank[:, :]).then_inc(gathered_taken1, c.add(gathered_taken1))
                    select(e + 1)
                    for j, ups in enumerate(((TURN[1], SCORE[0]), GEMM)):
                        c.skip(panel_done, FT_MOE)
                        v.wait_ge(gate_act, c.next(gate_act))
                        for f, ps in enumerate(ups):
                            v.wait_ge(panel_done, c.next(panel_done, 2))
                            v.tensor_tensor(tile(HID[j], f, 2 * P), ps[:, 0:2 * P], tile(GACT[j], f, 2 * P), ALU.mult).then_inc(
                                hidden_ready, c.add(hidden_ready))
                    c.skip(panel_done, PAIR * FT_MOE)
                    for j in range(PAIR):
                        for half, ps in enumerate((OUT, DEN)):
                            v.wait_ge(result_high, c.next(result_high))
                            v.scalar_tensor_tensor(tile(YL, 2 * j + half), ps[:, :], SLOT_SHARE[:, j:j + 1], f32(tile(YH, 2 * j + half)),
                                                   ALU.mult, ALU.subtract).then_inc(result_ready, c.add(result_ready))
                    for d in range(KD):
                        v.wait_ge(scattered, c.next(scattered))
                        v.tensor_tensor(tile(X, d), GEMM[d % 2][:, :], tile(X, d), ALU.add).then_inc(added, c.add(added))
                v.tensor_scalar(RANK, RANK, float(-P), None, ALU.add).then_inc(select_step, c.add(select_step))
                v.wait_ge(select_step, c.now(select_step))
            v.memset(SQ[:, :], 0.0).then_inc(experts_done, c.add(experts_done))
            v.wait_ge(squares_ready, c.next(squares_ready))
            fold(XN)
            rstd()
            v.wait_ge(den_taken, c.now(den_taken))

            def low_of(k):
                v.wait_ge(normed, c.now(normed))
                v.wait_ge(high_ready, c.next(high_ready))
                v.scalar_tensor_tensor(tile(XL, k), tile(XN, k), vec("gains2", k), f32(tile(XH, k)),
                                       ALU.mult, ALU.subtract).then_inc(operand_ready, c.add(operand_ready))

            for k in range(KD):
                def by_row(ap):
                    return ap.rearrange("p (r c) -> p r c", r=NA_ROWS)

                v.scalar_tensor_tensor(tile(XN, k).rearrange("p (c r) -> p r c", r=NA_ROWS), by_row(tile(X, k)),
                                       vec("g_final", k), by_row(RS[:, :]), ALU.mult, ALU.mult).then_inc(normed, c.add(normed))
                if k:
                    low_of(k - 1)
            low_of(KD - 1)
            v.wait_ge(squares_ready, c.next(squares_ready, KD))
            fold(GATE_A)
            for k in range(KD // 2, KD):
                step(v.tensor_copy(tile(X, k), tile(XN, k)))
            v.wait_ge(dve_step, c.now(dve_step))
            v.wait_ge(moved, c.next(moved, KD // 2))
            with c.loop("layers", LAYERS) as l:
                def gain(s):
                    return lambda e: VEC[:, bass.ds(l * 24 + e + (col["gains2"] + 8 * s), 1)]

                ffn("a", gain(1))
                rstd()
                with c.loop("na", PAIRS) as i:
                    v.wait_ge(den_taken, c.now(den_taken))
                    take(QB[:, :], ATT_SCALE)
                    take(KB[:, :])
                    take(VT[:, :])
                    take(UT)
                    for b in range(2):
                        ps = scores_in()
                        v.tensor_copy(AB[:, b * T:(b + 1) * T], ps[:, :]).then_inc(scores_taken, c.add(scores_taken))
                    for h in range(2):
                        v.wait_ge(bias_in[h], c.next(bias_in[h], 16))
                        chain(v.tensor_tensor(BIAS[h], BIAS[h], MASK, ALU.add))
                    v.wait_ge(turned_full, c.next(turned_full, 2))

                    def fourier_out():
                        v.tensor_copy(TA[:, :], den_in()[:, :]).then_inc(den_taken, c.add(den_taken))
                        v.wait_ge(den_taken, c.now(den_taken))
                        halves(tile(AH, i + PAIRS), tile(AL, i + PAIRS), TA[:, :])
                        v.wait_ge(operand_ready, c.now(operand_ready))

                    def bias_of(h, t):
                        return BIAS[h][:, NEAR_AT[t]:NEAR_AT[t] + span(NEAR[t])[1]]

                    attention(NEAR, bias_of, tile(AH, i), tile(AL, i),
                              {2: lambda: take(tile(GATE_A, i * 2)), 3: fourier_out, 5: lambda: take(tile(GATE_B, i * 2)),
                               7: lambda: take(tile(GATE_A, i * 2 + 1)), 8: lambda: take(tile(GATE_B, i * 2 + 1))})
                with c.loop("comb", KD // 2) as d:
                    for j in range(2):
                        e = d * 2 + j
                        for s, gates in enumerate((GATE_A, GATE_B)):
                            ps = gemm_in()
                            v.wait_ge(act_out, c.next(act_out))
                            v.tensor_tensor(PROB[s][:, :], ps, tile(gates, e), ALU.mult).then_inc(gemm_taken, c.add(gemm_taken))
                        v.wait_ge(gemm_taken, c.now(gemm_taken))
                        chain(v.tensor_tensor(PROB[0][:, :], PROB[0][:, :], PROB[1][:, :], ALU.add))
                        halves(tile(AH, e + KD), tile(AL, e + KD), PROB[0][:, :])
                        v.wait_ge(operand_ready, c.now(operand_ready))
                clear_squares()
                with c.loop("wo", KD // 2) as d:
                    v.wait_ge(dve_step, c.now(dve_step))
                    for j in range(2):
                        e = d * 2 + j
                        add_to(tile(X, e))
                        prep(tile(X, e), gain(2)(e), tile(XH, e), tile(XL, e))
                ffn("b", gain(3))
            rstd()
            with c.loop("last", KD) as k:
                v.wait_ge(den_taken, c.now(den_taken))
                v.scalar_tensor_tensor(tile(X, k), tile(X, k), VEC[:, bass.ds(k + col["last_gain"], 1)],
                                                           RS[:, :], ALU.mult, ALU.mult).then_inc(out_ready, c.add(out_ready))


def panels(w):
    k, n = w.shape
    return w.reshape(k // P, P, n // P, P).transpose(2, 1, 0, 3).reshape(n // P, P, k)


def columns(g):
    return g.reshape(-1, P).T


def feature_major(x):
    t, d = x.shape
    return np.ascontiguousarray(x.T.reshape(d // P, P, t).transpose(1, 0, 2).reshape(P, d // P * t))


def by_column():
    return np.arange(T).reshape(NA_ROWS, GRID_W).T.reshape(-1)


def near_tables():
    for i in (0, 1, QT - 1):
        key, n = span(NEAR[i])
        q, k = i * P + np.arange(P)[:, None], key + np.arange(n)[None]
        start = np.clip(q // NA_ROWS - NA_COLS // 2, 0, GRID_W - NA_COLS)
        yield k % NA_ROWS - q % NA_ROWS, k // NA_ROWS - q // NA_ROWS, k // NA_ROWS + 0 * q, start


def constants():
    f = np.float32
    q, k = np.arange(T)[:, None], np.arange(T)[None]
    far = q - k
    times = ((far >= 0) & (far <= 128)).astype(int) + ((far >= 0) & (far % 4 == 0)) + ((far >= 0) & (far % 16 == 0))
    ln = np.where(times > 0, np.log(np.maximum(times, 1)), NEG).astype(f)
    ln = np.concatenate([ln[i * P:(i + 1) * P, :(i + 1) * P] for i in range(QT)], axis=1)
    rot = np.zeros((P, P), f)
    invf = np.zeros((P, 1), f)
    half = HEAD // 8
    inv = (f(500000.0) ** (-np.arange(0, 2 * half, 2, dtype=f) / f(2 * half))).astype(f)
    for h in range(2):
        for j in range(half):
            lo, hi = h * HEAD + j, h * HEAD + half + j
            rot[hi, lo], rot[lo, hi] = -1, 1
            invf[lo] = invf[hi] = inv[j]
    s, t = np.arange(P)[:, None], np.arange(P)[None]
    tri = np.where(t >= s, 0, NEG).astype(f)
    near = []
    for _, _, dist, start in near_tables():
        near.append(np.where((dist >= start) & (dist < start + NA_COLS), 0, NEG).astype(f))
    near = np.concatenate(near, axis=1)
    ang = 2 * np.pi * (s * t % P) / P
    cs = np.concatenate([np.cos(ang), np.sin(ang)], axis=1).astype(f)
    at = by_column()
    ang = 2 * np.pi * (at[:, None] * at[None] % T) / T
    norm = (T * P) ** -0.5
    ct, nst = ((m * norm).astype(f).reshape(QT, P, T).transpose(1, 0, 2).reshape(P, QT * T) for m in (np.cos(ang), -np.sin(ang)))
    return {"ident": np.eye(P, dtype=f), "rot": rot, "tri": tri, "near": near, "cs": cs, "ln": ln,
            "ct": np.ascontiguousarray(ct), "nst": np.ascontiguousarray(nst)}, invf


def lay_out(x):
    f = np.float32
    arrays, invf = constants()
    vecs, cols, at = [], {}, 0

    def put(name, part):
        nonlocal at
        whole = np.zeros((P, part.shape[1]), f)
        whole[:part.shape[0]] = part
        vecs.append(whole)
        cols[name] = at
        at += part.shape[1]

    for name in ("g_mix", "g_mem", "g_cross", "g_ffn"):
        put(name, columns(x[name][0]))
    put("g_final", columns(x["g_final"]))
    put("gains2", np.concatenate([columns(x[n][l]) for l in range(LAYERS) for n in ("ffn1_norm_2", "mix_norm_2", "ffn2_norm_2")]
                                 + [columns(x["final_norm_2"])], axis=1))
    cols["last_gain"] = cols["gains2"] + 24 * LAYERS
    put("gate_b", np.concatenate([columns(x["mix_gate_bias_2"][l, s]) for l in range(LAYERS) for s in range(2)], axis=1))
    heads = [columns(x["conv_w"][0, j]) for j in range(4)] + [columns(x[n][0]) for n in ("conv_b", "g_mhn", "skip_m", "skip_m")]
    put("mvec", np.stack(heads, axis=2).reshape(P, M_HEADS * 8))
    put("b_i", x["b_i"][0][:, None])
    put("b_f", x["b_f"][0][:, None])
    put("b_route", np.concatenate([x["b_router_g"][0], x["b_router_e"][0]])[:, None])
    put("invf", invf)
    put("desc", np.tile(np.arange(EXPERTS, 0, -1, dtype=f), (P, 1)))
    arrays["vec"] = np.concatenate(vecs, axis=1)

    arrays["xT"] = feature_major(x["x"][0])
    arrays["memT"] = feature_major(x["mem"][0])
    arrays["positions"] = np.ascontiguousarray(x["positions"])

    def padded(*ws):
        w = np.concatenate(ws, axis=1)
        return np.pad(w, ((0, 0), (0, P - w.shape[1])))

    kv = panels(x["w_kv_x"][0])
    w_in = panels(x["w_in"][0][:, :6 * PAIRS * P])
    gates = x["w_in"][0][:, 6 * PAIRS * P:]
    order = [w_in[part * PAIRS + i] for i in range(PAIRS) for part in (3, 4, 0, 1, 2, 5)]
    experts = []
    for e in range(0, EXPERTS, PAIR):
        for j in range(PAIR):
            experts += list(panels(x["w1"][0, e + j])) + list(panels(x["w3"][0, e + j]))
        for j in range(PAIR):
            experts += list(x["w2"][0, e + j].reshape(FT_MOE, P, D))
    wo = panels(x["w_o_x"][0]).reshape(2, KD // 2, P, 2 * P).transpose(0, 2, 1, 3).reshape(2, P, KD * P)
    first = [kv[0], kv[2], kv[1], kv[3], panels(padded(gates[:, :M_HEADS]))[0], panels(padded(gates[:, M_HEADS:]))[0]]
    first += order + list(panels(x["w_out"][0])) + list(panels(x["w_q_x"][0])) + list(wo)
    first += [panels(padded(x["w_router_g"][0], x["w_router_e"][0]))[0]]
    arrays["experts"] = np.stack(experts)
    arrays["panels1"] = np.stack(first)
    arrays["w_qk_m"] = np.concatenate([x["w_q_m"][0], x["w_k_m"][0]], axis=2)

    up, down, mix, bias = [], [], [], []
    for l in range(LAYERS):
        for which in ("ffn1", "ffn2"):
            wi = panels(x[f"{which}_w_in_2"][l]).reshape(2, 2 * HALF_FT, P, PANEL).transpose(1, 0, 2, 3)
            up.append(wi.reshape(4 * HALF_FT, P, PANEL))
            wo = panels(x[f"{which}_w_out_2"][l]).reshape(KD, P, 2, WIDE).transpose(2, 0, 1, 3)
            down.append(wo.reshape(2 * KD, P, WIDE))
        wi = panels(x["mix_w_in_2"][l])
        for i in range(PAIRS):
            mix += [wi[part * PAIRS + i] for part in range(4)]
            mix += [wi[16 + g * KD + d] for d in (2 * i, 2 * i + 1) for g in range(2)]
        both = np.concatenate([panels(x["na_w_out_2"][l]), panels(x["f_w_out_2"][l])], axis=2)
        mix += list(both)
        mix += list(panels(x["mix_w_o_2"][l]))
        rpb = x["na_rpb_2"][l]
        wide = np.pad(rpb, ((0, 0), (0, 0), (GRID_W, GRID_W)))
        for h in range(rpb.shape[0]):
            bias.append(np.concatenate([wide[h, rows + NA_ROWS - 1, cols + NA_COLS - 1 + GRID_W]
                                        for rows, cols, _, _ in near_tables()], axis=1))
    arrays["up2"], arrays["down2"] = np.concatenate(up), np.concatenate(down)
    arrays["mix2"], arrays["bias"] = np.stack(mix), np.stack(bias)
    return arrays, cols


def kernel(**inputs):
    import concourse.bacc as bacc
    from concourse.bass_utils import run_bass_kernel_spmd

    arrays, cols = lay_out({k: np.asarray(v) for k, v in inputs.items()})

    def program(trips):
        nc = bacc.Bacc("TRN2", target_bir_lowering=False, num_devices=1)
        a = {n: nc.dram_tensor(n, v.shape, mybir.dt.from_np(v.dtype), kind="ExternalInput").ap() for n, v in arrays.items()}
        a["cols"] = cols
        a["outT"] = nc.dram_tensor("outT", (P, KD * T), F32, kind="ExternalOutput").ap()
        build(nc, a, trips)
        return nc

    trips = {}
    program(trips)
    nc = program(trips)
    r = run_bass_kernel_spmd(nc, [arrays], core_ids=[0])
    by_token = np.asarray(r.results[0]["outT"]).reshape(P, KD, T).transpose(2, 1, 0).reshape(T, D)
    out = np.empty((1, T, D), np.float32)
    out[0, by_column()] = by_token
    return out
```
